# Optimizing a Trainium2 kernel written in Bass

```python
import math
import jax, jax.numpy as jnp
from jax import lax
import numpy as np

D_MODEL = 1024
BATCH = 1
SEQ = 1024
DEPTH = 1

CTX_LEN = 256
GRID_W = 64
NORM_EPS = 1e-6
ROPE_BASE = 10000.0
Q_BLOCK = 128

GDN_HEADS = 4
GDN_DK = 128
GDN_DV = 128
GDN_CHUNK = 64
CONV_W = 5
GDN_WIDTH = GDN_HEADS * GDN_DV
GDN_QK = GDN_HEADS * GDN_DK
GDN_CONV_CH = 2 * GDN_QK + GDN_WIDTH
GDN_COLS = GDN_CONV_CH + GDN_WIDTH + 4 * GDN_HEADS

MLA_HEADS = 4
MLA_Q_RANK = 256
MLA_KV_RANK = 128
MLA_NOPE = 64
MLA_ROPE = 32
MLA_V = 64
MLA_WIDTH = MLA_HEADS * MLA_V
MLA_COLS = MLA_Q_RANK + MLA_KV_RANK + MLA_ROPE + MLA_WIDTH
MLA_SCALE = (MLA_NOPE + MLA_ROPE) ** -0.5

DIFF_HEADS = 4
DIFF_QK = 32
DIFF_V = 64
DIFF_WIDTH = DIFF_HEADS * DIFF_V
DIFF_QK_COLS = DIFF_HEADS * 2 * DIFF_QK
DIFF_COLS = 2 * DIFF_QK_COLS + 2 * DIFF_WIDTH
DIFF_SCALE = DIFF_QK ** -0.5

MIX_WIDTH = GDN_WIDTH + MLA_WIDTH + DIFF_WIDTH
IN_COLS = GDN_COLS + MLA_COLS + DIFF_COLS

kernel_name = 'hybrid_parallel_groups_dit_block'

def rms_norm(x, g):
    xf = x.astype(jnp.float32)
    y = xf * lax.rsqrt(jnp.mean(xf * xf, axis=-1, keepdims=True) + NORM_EPS)
    return (y * g.astype(jnp.float32)).astype(x.dtype)

def l2_normalize(x):
    return x * lax.rsqrt(jnp.sum(x * x, axis=-1, keepdims=True) + NORM_EPS)

def axial_rope_tables(n_rows, dim):
    row = jnp.repeat(jnp.arange(n_rows), GRID_W).astype(jnp.float32)
    col = jnp.tile(jnp.arange(GRID_W), n_rows).astype(jnp.float32)
    d_axis = dim // 2
    inv = 1.0 / (ROPE_BASE ** (jnp.arange(0, d_axis, 2, dtype=jnp.float32) / d_axis))
    ang = jnp.concatenate([row[:, None] * inv, col[:, None] * inv], axis=-1)
    return jnp.cos(ang), jnp.sin(ang)

def apply_rope(x, cos, sin):
    shape = (cos.shape[0],) + (1,) * (x.ndim - 3) + (cos.shape[1],)
    cs, sn = cos.reshape(shape), sin.reshape(shape)
    x1, x2 = jnp.split(x.astype(jnp.float32), 2, axis=-1)
    return jnp.concatenate([x1 * cs - x2 * sn, x1 * sn + x2 * cs], axis=-1).astype(x.dtype)

def sweep_query_blocks(attend, q):
    B, S = q.shape[:2]
    nb = S // Q_BLOCK
    qb = jnp.moveaxis(q.reshape((B, nb, Q_BLOCK) + q.shape[2:]), 1, 0)
    ob = lax.map(attend, qb)
    return jnp.moveaxis(ob, 0, 1).reshape((B, S) + ob.shape[3:])

def softmax_attention(q, k, v, scale):
    s = jnp.einsum('bqhd,bkhd->bhqk', q, k).astype(jnp.float32) * scale
    p = jax.nn.softmax(s, axis=-1).astype(v.dtype)
    return jnp.einsum('bhqk,bkhd->bqhd', p, v)

def differential_attention(q, k, v, lam):
    s = jnp.einsum('bqhmd,bkhmd->bhmqk', q, k).astype(jnp.float32) * DIFF_SCALE
    p = jax.nn.softmax(s, axis=-1)
    w = p[:, :, 0] - lam * p[:, :, 1]
    return jnp.einsum('bhqk,bkhd->bqhd', w.astype(v.dtype), v)

def centred_depthwise_conv(x, w):
    C = x.shape[-1]
    return lax.conv_general_dilated(
        x, w[:, None, :].astype(x.dtype), window_strides=(1,),
        padding=[(CONV_W // 2, CONV_W // 2)],
        dimension_numbers=('NWC', 'WIO', 'NWC'), feature_group_count=C)

def gated_delta_chunked(q, k, v, g, beta, s0):
    B, T, H, K = q.shape
    N = T // GDN_CHUNK

    def chunks(a):
        a = a.reshape((B, N, GDN_CHUNK, H) + a.shape[3:])
        return jnp.moveaxis(a, (1, 3), (0, 2))

    qc, kc, vc, gc, bc = (chunks(a) for a in (q * (K ** -0.5), k, v, g, beta))
    gam = jnp.cumsum(gc, axis=-1)
    idx = jnp.arange(GDN_CHUNK)
    incl = idx[:, None] >= idx[None, :]
    strict = idx[:, None] > idx[None, :]
    diff = gam[..., :, None] - gam[..., None, :]
    dec = jnp.where(incl, jnp.exp(jnp.where(incl, diff, 0.0)), 0.0)
    kb = kc * bc[..., None]
    a_mat = jnp.where(strict, jnp.einsum('nbhik,nbhjk->nbhij', kb, kc) * dec, 0.0)
    eye = jnp.eye(GDN_CHUNK, dtype=a_mat.dtype)
    t_mat = lax.linalg.triangular_solve(eye + a_mat, jnp.broadcast_to(eye, a_mat.shape),
                                        left_side=True, lower=True)
    eg = jnp.exp(gam)[..., None]
    u = t_mat @ (vc * bc[..., None])
    w = t_mat @ (kb * eg)
    qk = jnp.where(incl, jnp.einsum('nbhik,nbhjk->nbhij', qc, kc) * dec, 0.0)
    q_dec = qc * eg
    k_dec = kc * jnp.exp(gam[..., -1:] - gam)[..., None]
    g_last = jnp.exp(gam[..., -1])

    def step(s, xs):
        u_i, w_i, qk_i, qd_i, kd_i, gl_i = xs
        v_new = u_i - w_i @ s
        o = qd_i @ s + qk_i @ v_new
        s = s * gl_i[..., None, None] + jnp.swapaxes(kd_i, -1, -2) @ v_new
        return s, o

    s_fin, o = lax.scan(step, s0, (u, w, qk, q_dec, k_dec, g_last))
    o = jnp.moveaxis(o, (0, 2), (1, 3)).reshape(B, T, H, v.shape[-1])
    return o, s_fin

def gdn_prepare(p, conv_w, a_log, dt_bias):
    B, T = p.shape[:2]
    qkv, z, b_logit, a_logit = jnp.split(
        p, [GDN_CONV_CH, GDN_CONV_CH + GDN_WIDTH, GDN_CONV_CH + GDN_WIDTH + 2 * GDN_HEADS], axis=-1)
    qkv = jax.nn.silu(centred_depthwise_conv(qkv, conv_w)).astype(jnp.float32)
    q, k, v = jnp.split(qkv, [GDN_QK, 2 * GDN_QK], axis=-1)
    q = l2_normalize(q.reshape(B, T, GDN_HEADS, GDN_DK))
    k = l2_normalize(k.reshape(B, T, GDN_HEADS, GDN_DK))
    v = v.reshape(B, T, GDN_HEADS, GDN_DV)
    beta = jax.nn.sigmoid(b_logit.astype(jnp.float32)).reshape(B, T, 2, GDN_HEADS)
    g = -jnp.exp(a_log.astype(jnp.float32)) * jax.nn.softplus(
        a_logit.astype(jnp.float32).reshape(B, T, 2, GDN_HEADS) + dt_bias.astype(jnp.float32))
    return q, k, v, beta, g, z

def bidirectional_gated_delta(lat, ctx):
    q, k, v, beta, g = lat
    qc, kc, vc, betac, gc = ctx
    s0 = jnp.zeros((q.shape[0], GDN_HEADS, GDN_DK, GDN_DV), jnp.float32)
    flip = lambda a: jnp.flip(a, axis=1)
    oc_f, sc_f = gated_delta_chunked(qc, kc, vc, gc[:, :, 0], betac[:, :, 0], s0)
    ol_f, _ = gated_delta_chunked(q, k, v, g[:, :, 0], beta[:, :, 0], sc_f)
    oc_b, sc_b = gated_delta_chunked(flip(qc), flip(kc), flip(vc), flip(gc[:, :, 1]), flip(betac[:, :, 1]), s0)
    ol_b, _ = gated_delta_chunked(flip(q), flip(k), flip(v), flip(g[:, :, 1]), flip(beta[:, :, 1]), sc_b)
    return ol_f + flip(ol_b), oc_f + flip(oc_b)

def gdn_finish(o, z, out_gain, dtype):
    B, T = o.shape[:2]
    y = rms_norm(o, out_gain) * jax.nn.silu(z.astype(jnp.float32).reshape(B, T, GDN_HEADS, GDN_DV))
    return y.reshape(B, T, GDN_WIDTH).astype(dtype)

def mla_project(p, q_gain, w_uq, kv_gain, w_ukv, rope):
    B, T = p.shape[:2]
    c_q, c_kv, k_r, z = jnp.split(
        p, [MLA_Q_RANK, MLA_Q_RANK + MLA_KV_RANK, MLA_Q_RANK + MLA_KV_RANK + MLA_ROPE], axis=-1)
    q = (rms_norm(c_q, q_gain) @ w_uq).reshape(B, T, MLA_HEADS, MLA_NOPE + MLA_ROPE)
    kv = (rms_norm(c_kv, kv_gain) @ w_ukv).reshape(B, T, MLA_HEADS, MLA_NOPE + MLA_V)
    q_n, q_r = jnp.split(q, [MLA_NOPE], axis=-1)
    k_n, v = jnp.split(kv, [MLA_NOPE], axis=-1)
    k_r = k_r[:, :, None, :]
    if rope is not None:
        q_r = apply_rope(q_r, *rope)
        k_r = apply_rope(k_r, *rope)
    q = jnp.concatenate([q_n, q_r], axis=-1)
    k = jnp.concatenate([k_n, jnp.broadcast_to(k_r, (B, T, MLA_HEADS, MLA_ROPE)).astype(k_n.dtype)], axis=-1)
    return q, k, v, z

def diff_project(p, rope):
    B, T = p.shape[:2]
    q, k, v, z = jnp.split(p, [DIFF_QK_COLS, 2 * DIFF_QK_COLS, 2 * DIFF_QK_COLS + DIFF_WIDTH], axis=-1)
    q = q.reshape(B, T, DIFF_HEADS, 2, DIFF_QK)
    k = k.reshape(B, T, DIFF_HEADS, 2, DIFF_QK)
    if rope is not None:
        q = apply_rope(q, *rope)
        k = apply_rope(k, *rope)
    return q, k, v.reshape(B, T, DIFF_HEADS, DIFF_V), z

def diff_finish(o, z, sub_gain, lam_init, dtype):
    B, T = o.shape[:2]
    y = rms_norm(o, sub_gain) * (1.0 - lam_init) * jax.nn.silu(z.reshape(B, T, DIFF_HEADS, DIFF_V))
    return y.reshape(B, T, DIFF_WIDTH).astype(dtype)

def hybrid_layer(x, xc, c, c_ctx, ada_w, ada_b, pre_gain, post_gain, w_in, gdn_conv, gdn_a_log,
                 gdn_dt_bias, gdn_out_gain, mla_q_gain, mla_w_uq, mla_kv_gain, mla_w_ukv,
                 diff_lambda, diff_sub_gain, w_out, lam_init, rope_mla, rope_diff, need_ctx):
    B, S, _ = x.shape
    shift, scale, gate = jnp.split(jax.nn.silu(c) @ ada_w + ada_b, 3, axis=-1)
    shift_c, scale_c, gate_c = jnp.split(jax.nn.silu(c_ctx) @ ada_w + ada_b, 3, axis=-1)
    h = rms_norm(x, pre_gain) * (1.0 + scale[:, None, :]) + shift[:, None, :]
    hc = rms_norm(xc, pre_gain) * (1.0 + scale_c) + shift_c
    cuts = [GDN_COLS, GDN_COLS + MLA_COLS]
    p_a, p_b, p_c = jnp.split(h @ w_in, cuts, axis=-1)
    pc_a, pc_b, pc_c = jnp.split(hc @ w_in, cuts, axis=-1)

    qa, ka, va, ba, ga, za = gdn_prepare(p_a, gdn_conv, gdn_a_log, gdn_dt_bias)
    qca, kca, vca, bca, gca, zca = gdn_prepare(pc_a, gdn_conv, gdn_a_log, gdn_dt_bias)
    oa, oca = bidirectional_gated_delta((qa, ka, va, ba, ga), (qca, kca, vca, bca, gca))
    out_a = gdn_finish(oa, za, gdn_out_gain, x.dtype)

    qb, kb, vb, zb = mla_project(p_b, mla_q_gain, mla_w_uq, mla_kv_gain, mla_w_ukv, rope_mla)
    qcb, kcb, vcb, zcb = mla_project(pc_b, mla_q_gain, mla_w_uq, mla_kv_gain, mla_w_ukv, None)
    kb_all = jnp.concatenate([kb, kcb], axis=1)
    vb_all = jnp.concatenate([vb, vcb], axis=1)
    ob = sweep_query_blocks(lambda qq: softmax_attention(qq, kb_all, vb_all, MLA_SCALE), qb)
    out_b = (ob * jax.nn.silu(zb).reshape(B, S, MLA_HEADS, MLA_V)).reshape(B, S, MLA_WIDTH).astype(x.dtype)

    lq1, lk1, lq2, lk2 = diff_lambda.astype(jnp.float32)
    lam = jnp.exp(jnp.sum(lq1 * lk1)) - jnp.exp(jnp.sum(lq2 * lk2)) + lam_init
    qd, kd, vd, zd = diff_project(p_c, rope_diff)
    qcd, kcd, vcd, zcd = diff_project(pc_c, None)
    kd_all = jnp.concatenate([kd, kcd], axis=1)
    vd_all = jnp.concatenate([vd, vcd], axis=1)
    od = sweep_query_blocks(lambda qq: differential_attention(qq, kd_all, vd_all, lam), qd)
    out_c = diff_finish(od, zd, diff_sub_gain, lam_init, x.dtype)

    y = jnp.concatenate([out_a, out_b, out_c], axis=-1) @ w_out
    x = x + gate[:, None, :] * rms_norm(y, post_gain)

    if need_ctx:
        Bc, Tc = xc.shape[:2]
        oc_a = gdn_finish(oca, zca, gdn_out_gain, xc.dtype)
        oc_b = softmax_attention(qcb, kcb, vcb, MLA_SCALE)
        oc_b = (oc_b * jax.nn.silu(zcb).reshape(Bc, Tc, MLA_HEADS, MLA_V)).reshape(Bc, Tc, MLA_WIDTH).astype(xc.dtype)
        oc_c = diff_finish(differential_attention(qcd, kcd, vcd, lam), zcd, diff_sub_gain, lam_init, xc.dtype)
        yc = jnp.concatenate([oc_a, oc_b, oc_c], axis=-1) @ w_out
        xc = xc + gate_c * rms_norm(yc, post_gain)
    else:
        xc = None
    return x, xc

def setup_inputs(seed: int = 0) -> dict:
    key = jax.random.key(seed)
    ks = jax.random.split(key, 20)
    L = DEPTH

    def nrm(k, shape, s):
        return jax.random.normal(k, shape, jnp.float32) * s

    dt = jnp.exp(jax.random.uniform(ks[11], (L, 2, GDN_HEADS), jnp.float32,
                                    minval=math.log(1e-3), maxval=math.log(1e-1)))
    return {
        'x': nrm(ks[0], (BATCH, SEQ, D_MODEL), 1.0),
        'c': nrm(ks[1], (BATCH, D_MODEL), 1.0),
        'ctx': nrm(ks[2], (BATCH, CTX_LEN, D_MODEL), 1.0),
        'c_ctx': nrm(ks[3], (D_MODEL,), 1.0),
        'ada_w': nrm(ks[4], (L, D_MODEL, 3 * D_MODEL), 0.5 * D_MODEL ** -0.5),
        'ada_b': nrm(ks[5], (L, 3 * D_MODEL), 0.01),
        'pre_gain': 1.0 + nrm(ks[6], (L, D_MODEL), 0.02),
        'post_gain': 1.0 + nrm(ks[7], (L, D_MODEL), 0.02),
        'w_in': nrm(ks[8], (L, D_MODEL, IN_COLS), D_MODEL ** -0.5),
        'gdn_conv': nrm(ks[9], (L, CONV_W, GDN_CONV_CH), CONV_W ** -0.5),
        'gdn_a_log': jnp.log(jax.random.uniform(ks[10], (L, 2, GDN_HEADS), jnp.float32, minval=1.0, maxval=16.0)),
        'gdn_dt_bias': dt + jnp.log(-jnp.expm1(-dt)),
        'gdn_out_gain': 1.0 + nrm(ks[12], (L, GDN_DV), 0.02),
        'mla_q_gain': 1.0 + nrm(ks[13], (L, MLA_Q_RANK), 0.02),
        'mla_w_uq': nrm(ks[14], (L, MLA_Q_RANK, MLA_HEADS * (MLA_NOPE + MLA_ROPE)), MLA_Q_RANK ** -0.5),
        'mla_kv_gain': 1.0 + nrm(ks[15], (L, MLA_KV_RANK), 0.02),
        'mla_w_ukv': nrm(ks[16], (L, MLA_KV_RANK, MLA_HEADS * (MLA_NOPE + MLA_V)), MLA_KV_RANK ** -0.5),
        'diff_lambda': nrm(ks[17], (L, 4, DIFF_QK), 0.1),
        'diff_sub_gain': 1.0 + nrm(ks[18], (L, DIFF_V), 0.02),
        'w_out': nrm(ks[19], (L, MIX_WIDTH, D_MODEL), MIX_WIDTH ** -0.5),
    }

def reference(x, c, ctx, c_ctx, ada_w, ada_b, pre_gain, post_gain, w_in, gdn_conv, gdn_a_log,
              gdn_dt_bias, gdn_out_gain, mla_q_gain, mla_w_uq, mla_kv_gain, mla_w_ukv,
              diff_lambda, diff_sub_gain, w_out):
    ROWS = x.shape[1] // GRID_W
    rope_mla = axial_rope_tables(ROWS, MLA_ROPE)
    rope_diff = axial_rope_tables(ROWS, DIFF_QK)
    xc = ctx
    for l in range(DEPTH):
        lam_init = 0.8 - 0.6 * math.exp(-0.3 * l)
        x, xc = hybrid_layer(
            x, xc, c, c_ctx, ada_w[l], ada_b[l], pre_gain[l], post_gain[l], w_in[l], gdn_conv[l],
            gdn_a_log[l], gdn_dt_bias[l], gdn_out_gain[l], mla_q_gain[l], mla_w_uq[l], mla_kv_gain[l],
            mla_w_ukv[l], diff_lambda[l], diff_sub_gain[l], w_out[l], lam_init, rope_mla, rope_diff,
            l < DEPTH - 1)
    return x


_drawn_inputs = setup_inputs


def setup_inputs(seed=0):
    import zlib

    import numpy as np

    out = dict(_drawn_inputs(seed))
    spreads = {}
    factors = {'ada_b': 4.635,
     'pre_gain': 6.936,
     'post_gain': 8.0,
     'gdn_out_gain': 8.0,
     'mla_q_gain': 8.0,
     'mla_w_uq': 3.785,
     'mla_kv_gain': 8.0,
     'diff_lambda': 8.0,
     'diff_sub_gain': 8.0}
    for name, (base, spread) in spreads.items():
        noise = np.random.default_rng([zlib.crc32(name.encode()), seed]).standard_normal(out[name].shape)
        drawn = base * np.exp(spread * noise) if base else spread * noise
        out[name] = __import__('jax').numpy.asarray(drawn.astype(out[name].dtype))
    for name, factor in factors.items():
        out[name] = (out[name] * factor).astype(out[name].dtype)
    return out
```

```python
import math
from contextlib import ExitStack

import numpy as np

import concourse.bass as bass
from concourse import mybir

F32 = mybir.dt.float32
ALU = mybir.AluOpType
ACT = mybir.ActivationFunctionType
AX = mybir.AxisListType

P = 128
D = 1024
KD = D // P
LAT, CTX = 1024, 256
TOK = LAT + CTX
NT = TOK // P
NLAT = LAT // P
SEG = 512
H = 4
DK = 128
QK_COLS = H * DK
CONV_W = 5
EPS = 1e-6
GRID_W = 64
ROPE_BASE = 10000.0
MLA_NOPE, MLA_ROPE, MLA_V = 64, 32, 64
MLA_QK = MLA_NOPE + MLA_ROPE
MLA_SCALE = MLA_QK ** -0.5
Q_RANK, KV_RANK = 256, 128
DIFF_QK, DIFF_V = 32, 64
DIFF_SCALE = DIFF_QK ** -0.5
LAM_INIT = 0.8 - 0.6 * math.exp(0.0)
NEG = -1e30

GDN_TILES = ["misc"] + ["q"] * H + ["k"] * H + ["v"] * H
REST_TILES = ["za"] * 4 + ["cq"] * 2 + ["ckv"] + ["zb"] * 2 + ["dq"] * 2 + ["dk"] * 2 + ["dv"] * 2 + ["dz"] * 2
TILES = GDN_TILES + REST_TILES
LAT_ONLY = {"q", "za", "cq", "zb", "dq", "dz"}
W_RING = 3
KR0 = 64
LEVELS = [1 << i for i in range(7)]

COLS = {}
_at = 0
for _n, _c in (("c", 16), ("ada_b", 24), ("pre", 8), ("post", 8), ("conv", 60), ("og", 1), ("qg", 2),
               ("kvg", 1), ("sg", 1), ("alog", 8), ("dt", 8), ("lam", 128)):
    COLS[_n] = (_at, _c)
    _at += _c
NCOLS = _at
CONSTS = ["ident", "triu", "tril", "ones", "swap", "neg_f", "neg_b"] + [f"sib{b}" for b in LEVELS] + \
    [f"alt{b}" for b in LEVELS[1:]]


def segments(n):
    return [(s, min(SEG, n - s)) for s in range(0, n, SEG)]


def hybrid_block(nc, x, ctx_in, cols_d, const_d, rope_d, ada_w, w_in, w_uq, w_ukv, w_out, out):
    es = ExitStack()
    with es:
        def sb(name, shape):
            return es.enter_context(nc.sbuf_tensor(name, shape, F32))

        def sem(name):
            return es.enter_context(nc.semaphore(name))

        def need(eng, s, n):
            if n > 0:
                eng.wait_ge(s, n)

        ps = es.enter_context(nc.psum_tensor("ps", [P, 8, SEG], F32))
        hT_spill = nc.dram_tensor("hT_spill", [P, KD * TOK], F32, kind="Internal").ap()
        kr_spill = nc.dram_tensor("kr_spill", [MLA_ROPE, TOK], F32, kind="Internal").ap()

        cols = sb("cols", [P, NCOLS])
        const = sb("const", [P, len(CONSTS), P])
        GP = sb("GP", [P, D])
        ARENA_KB = 184
        arena = sb("arena", [P, ARENA_KB * 256])

        def view(kb, *shape):
            n = int(np.prod(shape))
            lo = int(kb * 256)
            assert lo + n <= ARENA_KB * 256
            v = arena[:, lo:lo + n]
            if len(shape) == 2:
                v = v.rearrange("p (a b) -> p a b", b=shape[1])
            if len(shape) == 3:
                v = v.rearrange("p (a b c) -> p a b c", b=shape[1], c=shape[2])
            return v

        def col(name, i=0, n=1):
            return cols[:, COLS[name][0] + i:COLS[name][0] + i + n]

        def cst(name):
            return const[:, CONSTS.index(name), :]

        def heads(ap):
            return ap.unsqueeze(1).broadcast_to([P, H, P])

        def per_head(ap):
            return ap.unsqueeze(2).broadcast_to([P, H, P])

        ident, ones = cst("ident"), cst("ones")
        small = sb("small", [P, 16 + 16 + 48 + 16 + 8 + 2 * NT + 4])
        _o = [0]

        def take(n):
            _o[0] += n
            return small[:, _o[0] - n:_o[0]]
        cs = take(16)
        cs_e = take(16)
        mod = take(48)
        mA = take(16)
        gp_col = take(8)
        ssq = take(NT)
        rstd = take(NT)
        eps_col = take(1)
        one_col = take(1)
        eps_q = take(1)

        hT = view(0, KD, TOK)
        ada = [view(40 + 32 * i, KD, D) for i in range(3)]
        xin = view(136, 4, D)
        junk = view(152, D)
        gp_diag = view(156, KD, P)
        w_ring = view(172, W_RING, KD, P)

        kT = view(40, H, TOK)
        qT = view(60, H, LAT)
        k_tok = view(76, NT, H * P)
        v_tok = view(96, NT, H * P)
        W0 = 116 * 256
        RAW_W, CV_W = LAT + CTX + 8, LAT + CTX + 4
        CTX_RAW, CTX_CV = LAT + 6, LAT + 4

        def words(off, n):
            return arena[:, W0 + off:W0 + off + n]
        raw = [words(i * RAW_W, RAW_W) for i in range(2)]
        cv = [words(2 * RAW_W + i * CV_W, CV_W) for i in range(2)]
        ebuf = words(2 * RAW_W + 2 * CV_W, CV_W)
        sqb = [words(2 * RAW_W + 3 * CV_W + i * TOK, TOK) for i in range(2)]
        yv = [words(2 * RAW_W + 3 * CV_W + (2 + i) * TOK, TOK) for i in range(2)]
        misc = view(162, TOK)

        gates = sb("gates", [P, 16 * NT + 13 * 8 * NT])
        lg = gates[:, 0:16 * NT].rearrange("p (c n) -> p c n", n=16)

        def gate(i):
            lo = 16 * NT + i * 8 * NT
            return gates[:, lo:lo + 8 * NT].rearrange("p (c n) -> p c n", n=8)
        xa, na, en, sp, g_, beta, gam, tot, dtk, EG, EKD, GL, bek = [gate(i) for i in range(13)]
        ea = sb("ea", [P, 8])

        Q_all = view(0, NT, H * P)
        QK = view(116, 2 * NLAT, H * P)
        wk = [20, 30]

        def inv_buf(s):
            b = wk[s]
            c = 164 + 4 * s
            return {"gbc": view(b, 8, P), "M": view(b, H, P), "N": view(b + 2, H, P), "E": view(b + 4, 8, P),
                    "At": view(b + 8, H, P), "P": view(c, H, P), "X": view(c + 2, H, P), "tmp": view(c + 2, H, P)}
        iv = [inv_buf(0), inv_buf(1)]
        S = view(20, 2, H * P)
        Sg = view(24, 2, H * P)
        R = view(28, 2, H * P)
        Vn = view(32, 2, H * P)
        Vs = view(36, 2, H * P)
        t2 = view(164, 2, H * P)
        Um = view(168, 2, H * P)
        o_acc = view(148, NLAT, H * P)
        o_sq = view(0, NLAT * H, P)
        o_stat = sb("o_stat", [P, 2 * NLAT * H])

        mixT = view(40, 8, LAT)
        cq = view(72, 2, LAT)
        ckv = view(80, TOK)
        krT = view(85, TOK)
        dq = view(90, 2, LAT)
        dk = view(98, 2, TOK)
        dv_tok = view(108, NT, H * DIFF_V)
        zexp = view(118, 2, LAT)
        zbuf = view(126, 2, LAT)
        dvT = view(134, TOK)
        rbuf = view(139, LAT)
        uq_sb = view(143, 2, H * MLA_QK)
        ukv_sb = view(146, H * P)
        rope = view(164, 2, LAT)
        QTm = view(0, H, LAT)
        KTm = view(16, H, TOK)
        V_tok = view(148, NT, H * MLA_V)
        cq_sq = view(118, 2, LAT)
        kv_sq = view(126, TOK)
        cq_rn = view(131, LAT)
        kv_rn = view(135, TOK)

        prob = view(118, 4, TOK)
        wT = view(138, 2, TOK)
        o_tok = view(158, 2, 2 * H * 64)
        d_sq = view(162, H, 64)
        NSET = NLAT * 3 * H
        stat = sb("stat", [P, 2 * NSET + 4 * NLAT * 2 * H + 2 * NLAT * H + 16])
        nmax = stat[:, 0:NSET]
        lsum = stat[:, NSET:2 * NSET]
        _s = 2 * NSET
        rinv = stat[:, _s:_s + NLAT * 8]
        rinv1 = stat[:, _s + NLAT * 8:_s + NLAT * 16]
        coef = stat[:, _s + NLAT * 16:_s + NLAT * 24]
        dss = stat[:, _s + NLAT * 24:_s + NLAT * 28]
        drs = stat[:, _s + NLAT * 28:_s + NLAT * 32]
        lamt = stat[:, _s + NLAT * 32:_s + NLAT * 32 + 8]
        lam_p = sb("lam_p", [P, 64])

        wo_sb = [view(164 + 4 * k, D) if k < 5 else view(72 + 4 * (k - 5), D) for k in range(KD)]
        y_buf = view(118, 2, D)
        x_buf = view(126, 2, D)
        y_junk = view(134, D)
        yst = sb("yst", [P, 2 * NLAT])

        names = """cols_in const_in rope_in uq_in x_in0 x_in1 x_in2 x_in3 ada_in0 ada_in1 ada_in2 w_in0 w_in1 w_in2
        setup c_exp c_one c_rec c_silu ada_mm ada_gate mod_add mod_A gp_done ssq_done rs_done xn_done xT_mm hT_dve hT_act
        diag_done gp_mm GP_done in_mm evac_done conv_step exp_done add1 rec silu_done sq_done aux_mm aux_read rn_done
        fin_done pad_done misc_out spill spill_kr gt_d gt_a gt_mm
        gbc_done pre_mm ex_done e_done pool_w at_done qk_done pool_q tr_mm p_done mn_done x_mm xs_done pq_mm upd
        s_init um_done sg_done ks_mm qs_mm r_done tr4_mm vv_done ds_mm qkv_mm s_upd t2_done o1_done oa_done
        osq_done ostat_d ostat_a o_ready hT_back kr_back in2_mm z_exp z_add z_rec z_done c_evac aux2_mm aux2_read
        raw_cos rope_t rope_done lam_d lam_a
        n_sq n_mm n_ln n_exp n_done mq_mm mq_ev mq_swap mq_t mq_c mq_done mk_mm mk_ev mk_rope mv_mm mv_ev kr_mm kr_t kr_c kr_done
        sc_mm mx_done p_exp l_inv w_done wt_mm wt_ev_a wt_ev_d pv_mm pv_ev d_sqd d_red d_ln d_exp d_norm ot_mm mix_b
        wo_in y_mm y_sq y_ln y_exp y_scaled x2_in0 x2_in1 y_out0 y_out1 y_added""".split()
        sm = {n: sem(n) for n in names}
        x_in = [sm[f"x_in{i}"] for i in range(4)]
        ada_in = [sm[f"ada_in{i}"] for i in range(3)]
        w_in_s = [sm[f"w_in{i}"] for i in range(W_RING)]
        x2_in = [sm["x2_in0"], sm["x2_in1"]]
        y_out = [sm["y_out0"], sm["y_out1"]]

        xv = x.rearrange("(t p) d -> t p d", p=P)
        cv_d = ctx_in.rearrange("(t p) d -> t p d", p=P)
        out_v = out.rearrange("(t p) d -> t p d", p=P)

        NG = len(GDN_TILES)
        GROUPS = [(0, 4), (4, 4), (8, 2)]

        def ntok(kind):
            return LAT if kind in LAT_ONLY else TOK

        def aux_jobs():
            jobs = []
            for i in range(NG + 3):
                if 0 <= i - 2 < NG and GDN_TILES[i - 2] in "qk":
                    for s, w in segments(ntok(GDN_TILES[i - 2])):
                        jobs.append(("ones", i - 2, s, w, i))
                t = i - 3
                if 0 <= t < NG and GDN_TILES[t] == "misc":
                    jobs.append(("logits", t, 0, TOK, i))
                if 0 <= t < NG and GDN_TILES[t] in "kv":
                    for s, w in segments(TOK):
                        jobs.append(("turn", t, s, w, i))
            return jobs
        AUX = aux_jobs()

        def aux_at(i, what):
            return [(j, a) for j, a in enumerate(AUX) if a[4] == i and a[0] in what]

        def head_of(t):
            return (t - 1) % H

        def y_of(t):
            kind = GDN_TILES[t]
            return {"q": lambda: qT[:, head_of(t), :], "k": lambda: kT[:, head_of(t), :],
                    "v": lambda: yv[t % 2]}[kind]()

        QKI = [t for t in range(NG) if GDN_TILES[t] in "qk"]
        AUX2 = []
        for j in range(len(REST_TILES) + 1):
            if j >= 1:
                kind = REST_TILES[j - 1]
                if kind in ("za", "dq", "dk"):
                    for s, w in segments(LAT):
                        AUX2.append((kind, j - 1, s, w, j))
                if kind == "dv":
                    for s, w in segments(TOK):
                        AUX2.append((kind, j - 1, s, w, j))
        first_of = {k: REST_TILES.index(k) for k in set(REST_TILES)}
        ROPED = [j for j, k in enumerate(REST_TILES) if k in ("dq", "dk")]
        ZT = [j for j, k in enumerate(REST_TILES) if k[0] == "z" or k == "dz"]
        CT = [j for j, k in enumerate(REST_TILES) if j not in ZT]

        order = [[8, 9] + list(range(8)), [9, 8] + list(range(7, -1, -1))]
        LATSTEP = [[m for m in range(20) if order[m % 2][m // 2] < NLAT]][0]

        UNITS = [(qb, u) for qb in range(NLAT) for u in range(2 * H)]

        def sets_of(n):
            qb, u = UNITS[n]
            base = qb * 3 * H
            return [base + u] if u < H else [base + H + 2 * (u - H), base + H + 2 * (u - H) + 1]
        KSEG = segments(TOK)

        block = es.enter_context(nc.Block())

        @block.sync
        def _(sp):
            sp.dma_start(cols[:, :], cols_d).then_inc(sm["cols_in"], 16)
            sp.dma_start(xin[:, 0, :], xv[0]).then_inc(x_in[0], 16)
            sp.dma_start(ada[0], ada_w[0]).then_inc(ada_in[0], 16)
            sp.dma_start(const[:, :, :], const_d).then_inc(sm["const_in"], 16)
            sp.dma_start(ada[1], ada_w[1]).then_inc(ada_in[1], 16)
            for t in range(1, 4):
                sp.dma_start(xin[:, t, :], xv[t]).then_inc(x_in[t], 16)
            for i in range(W_RING):
                sp.dma_start(w_ring[:, i, :, :], w_in[i]).then_inc(w_in_s[i], 16)
            sp.dma_start(ada[2], ada_w[2]).then_inc(ada_in[2], 16)
            for t in range(4, NT):
                sp.wait_ge(sm["xT_mm"], 8 * (t // 4))
                src = xv[t] if t < NLAT else cv_d[t - NLAT]
                sp.dma_start(xin[:, t % 4, :], src).then_inc(x_in[t % 4], 16)
            for i in range(W_RING, NG):
                sp.wait_ge(sm["in_mm"], i - W_RING + 1)
                sp.dma_start(w_ring[:, i % W_RING, :, :], w_in[i]).then_inc(w_in_s[i % W_RING], 16)
            sp.wait_ge(sm["hT_dve"], 12)
            sp.wait_ge(sm["hT_act"], 12)
            sp.dma_start(hT_spill, arena[:, 0:KD * TOK]).then_inc(sm["spill"], 16)
            sp.wait_ge(sm["evac_done"], 1)
            sp.dma_start(kr_spill, misc[KR0:KR0 + MLA_ROPE, :]).then_inc(sm["spill_kr"], 16)
            for i in range(NG, NG + W_RING):
                sp.wait_ge(sm["in_mm"], min(i - W_RING + 1, NG))
                sp.dma_start(w_ring[:, i % W_RING, :, :], w_in[i]).then_inc(w_in_s[i % W_RING], 16)
            sp.wait_ge(sm["spill"], 16)
            sp.wait_ge(sm["spill_kr"], 16)
            sp.wait_ge(sm["ostat_d"], 1)
            sp.wait_ge(sm["s_upd"], 20)
            sp.wait_ge(sm["o1_done"], 16)
            sp.wait_ge(sm["oa_done"], 16)
            sp.dma_start(arena[:, 0:KD * TOK], hT_spill).then_inc(sm["hT_back"], 16)
            sp.dma_start(rope, rope_d).then_inc(sm["rope_in"], 16)
            sp.dma_start(krT[KR0:KR0 + MLA_ROPE, :], kr_spill).then_inc(sm["kr_back"], 16)
            sp.dma_start(uq_sb, w_uq).then_inc(sm["uq_in"], 16)
            sp.dma_start(ukv_sb, w_ukv).then_inc(sm["uq_in"], 16)
            for i in range(NG + W_RING, len(TILES)):
                sp.wait_ge(sm["in2_mm"], i - W_RING + 1 - NG)
                sp.dma_start(w_ring[:, i % W_RING, :, :], w_in[i]).then_inc(w_in_s[i % W_RING], 16)
            sp.wait_ge(sm["mq_done"], H)
            sp.wait_ge(sm["kr_done"], 1)
            sp.wait_ge(sm["mv_mm"], 5)
            sp.wait_ge(sm["mk_mm"], H)
            for k in range(KD):
                sp.dma_start(wo_sb[k], w_out[k]).then_inc(sm["wo_in"], 16)
            for t in range(NLAT):
                if t == 0:
                    sp.wait_ge(sm["wt_mm"], 3 * len(UNITS))
                if t >= 2:
                    sp.wait_ge(sm["y_added"], t - 1)
                sp.dma_start(x_buf[:, t % 2, :], xv[t]).then_inc(x2_in[t % 2], 16)
                if t >= 1:
                    sp.wait_ge(sm["y_added"], t)
                    sp.dma_start(out_v[t - 1], y_buf[:, (t - 1) % 2, :]).then_inc(y_out[(t - 1) % 2], 16)
            sp.wait_ge(sm["y_added"], NLAT)
            sp.dma_start(out_v[NLAT - 1], y_buf[:, (NLAT - 1) % 2, :]).then_inc(y_out[(NLAT - 1) % 2], 16)
            sp.wait_ge(y_out[0], 16 * (NLAT // 2))
            sp.wait_ge(y_out[1], 16 * (NLAT // 2))

        def wait_turn_copy(pe, q):
            need(pe, sm["wt_ev_a"], (q + 1) // 2)
            need(pe, sm["wt_ev_d"], q // 2)

        def turn_x(pe, gi):
            t0, n = GROUPS[gi]
            for k in range(KD):
                q = gi * KD + k
                if k == 0:
                    pe.wait_ge(sm["const_in"], 16)
                    pe.wait_ge(sm["xn_done"], t0 + n)
                if q >= 6:
                    pe.wait_ge(sm["hT_dve"] if q % 2 == 0 else sm["hT_act"], (q - 6) // 2 + 1)
                for t in range(n):
                    last = nc.tensor.transpose(ps[:, 2 + q % 6, t * P:(t + 1) * P],
                                               xin[:, (t0 + t) % 4, k * P:(k + 1) * P], ident)
                last.then_inc(sm["xT_mm"], 1)

        def project(pe, i, n, free_sem, free_n, done, parity=None):
            parity = i % 2 if parity is None else parity
            pe.wait_ge(w_in_s[i % W_RING], 16 * (i // W_RING + 1))
            if free_sem is not None:
                need(pe, free_sem, free_n)
            for s, w in segments(n):
                for k in range(KD):
                    last = nc.tensor.matmul(ps[:, 3 * parity + s // SEG, 0:w], w_ring[:, i % W_RING, k, :],
                                            hT[:, k, s:s + w], start=(k == 0), stop=(k == KD - 1))
            last.then_inc(done, 1)

        def swap_q(pe, h):
            pe.wait_ge(sm["mq_ev"], h + 1)
            if h == 0:
                pe.wait_ge(sm["kr_t"], 1)
            need(pe, sm["mq_t"], h)
            for s, w in segments(LAT):
                last = nc.tensor.matmul(ps[KR0:KR0 + 32, 6 + s // SEG, 0:w],
                                        cst("swap")[KR0:KR0 + 32, KR0:KR0 + 32],
                                        QTm[KR0:KR0 + 32, h, s:s + w], start=True, stop=True)
            last.then_inc(sm["mq_swap"], 1)

        @block.tensor
        def _(pe):
            mm, tr = nc.tensor.matmul, nc.tensor.transpose

            pe.wait_ge(sm["c_silu"], 1)
            for piece in range(3):
                pe.wait_ge(ada_in[piece], 16)
                bank = 0 if piece < 2 else 1
                for j in range(KD):
                    o = (piece % 2 * KD + j) * 2
                    for k in range(KD):
                        last = mm(ps[:, bank, o:o + 2], ada[piece][:, k, j * P:(j + 1) * P],
                                  cs[:, 2 * k:2 * k + 2], start=(k == 0), stop=(k == KD - 1))
                if piece == 1:
                    last.then_inc(sm["ada_mm"], 1)
                if piece == 2:
                    last.then_inc(sm["ada_gate"], 1)
                if piece == 1:
                    turn_x(pe, 0)
            for gi in (1, 2):
                turn_x(pe, gi)
            pe.wait_ge(sm["diag_done"], 1)
            for i in range(2):
                last = mm(ps[:, i, :], ones, gp_diag[:, 4 * i:4 * i + 4, :], start=True, stop=True)
            last.then_inc(sm["gp_mm"], 1)

            for i in range(NG + 3):
                if i < NG:
                    if i == 0:
                        pe.wait_ge(sm["hT_dve"], 12)
                        pe.wait_ge(sm["hT_act"], 12)
                        pe.wait_ge(sm["GP_done"], 1)
                    project(pe, i, ntok(GDN_TILES[i]), sm["evac_done"], i - 1, sm["in_mm"])
                for j, (_, t, s, w, _) in aux_at(i, ("ones",)):
                    if s == 0:
                        pe.wait_ge(sm["sq_done"], QKI.index(t) + 1)
                    need(pe, sm["aux_read"], j - 1)
                    mm(ps[:, 6 + j % 2, 0:w], ones, sqb[t % 2][:, s:s + w], start=True,
                       stop=True).then_inc(sm["aux_mm"], 1)
                for j, (what, t, s, w, _) in aux_at(i, ("turn", "logits")):
                    need(pe, sm["aux_read"], j - 1)
                    bank = 6 + j % 2
                    if what == "logits":
                        for c in range(NT):
                            last = tr(ps[:, bank, 16 * c:16 * c + 16], misc[0:16, c * P:(c + 1) * P],
                                      ident[0:16, 0:16])
                    else:
                        if s == 0 and GDN_TILES[t] == "k":
                            pe.wait_ge(sm["fin_done"], QKI.index(t) + 1)
                        if s == 0:
                            pe.wait_ge(sm["silu_done"], t)
                        src = y_of(t)
                        for c in range(w // P):
                            last = tr(ps[:, bank, c * P:(c + 1) * P], src[:, s + c * P:s + (c + 1) * P], ident)
                    last.then_inc(sm["aux_mm"], 1)

            pe.wait_ge(sm["gt_d"], 4)
            mm(ps[:, 0, 0:8 * NT].rearrange("p (c n) -> p c n", n=8)[:, :, 0:4], cst("triu"), g_[:, :, 0:4],
               start=True, stop=True)
            mm(ps[:, 0, 0:8 * NT].rearrange("p (c n) -> p c n", n=8)[:, :, 4:8], cst("tril"), g_[:, :, 4:8],
               start=True, stop=True)
            mm(ps[:, 0, 128:128 + 8 * NT].rearrange("p (c n) -> p c n", n=8), ones, g_, start=True,
               stop=True).then_inc(sm["gt_mm"], 1)

            for pair in range(NT // 2):
                for s in range(2):
                    c = 2 * pair + s
                    b = 4 * s
                    pe.wait_ge(sm["gbc_done"], c + 1)
                    if pair == 0:
                        pe.wait_ge(sm["gt_d"], 6)
                        need(pe, sm["aux_read"], len(AUX))
                    need(pe, sm["upd"], 2 * (((pair - 1) * 6 + 5) * 2 + s + 1))
                    cc = slice(c * P, (c + 1) * P)
                    for h in range(H):
                        mm(ps[:, b, h * P:(h + 1) * P], kT[:, h, cc], kT[:, h, cc], start=True, stop=True)
                    if c < NLAT:
                        for h in range(H):
                            mm(ps[:, b + 1, h * P:(h + 1) * P], kT[:, h, cc], qT[:, h, cc], start=True, stop=True)
                    for d in range(2):
                        for h in range(H):
                            last = mm(ps[:, b + 2 + d, h * P:(h + 1) * P], iv[s]["gbc"][:, 4 * d + h, :],
                                      cst("triu") if d == 0 else cst("tril"), start=True, stop=True)
                    last.then_inc(sm["pre_mm"], 1)
                for s in range(2):
                    c = 2 * pair + s
                    pe.wait_ge(sm["pool_q"], 2 * (c + 1))
                    for h in range(H):
                        last = tr(ps[:, 4 * s, h * P:(h + 1) * P], Q_all[:, c, h * P:(h + 1) * P], ident)
                    last.then_inc(sm["tr_mm"], 1)
                for lev in range(6):
                    for s in range(2):
                        c = 2 * pair + s
                        n = (pair * 6 + lev) * 2 + s
                        pe.wait_ge(sm["mn_done"], 2 * n + 2)
                        if lev == 0:
                            pe.wait_ge(sm["qk_done"], 2 * min(c + 1, NLAT))
                        for h in range(H):
                            last = mm(ps[:, 4 * s + 1, h * P:(h + 1) * P], iv[s]["At"][:, h, :], iv[s]["M"][:, h, :],
                                      start=True, stop=True)
                        last.then_inc(sm["x_mm"], 1)
                    for s in range(2):
                        n = (pair * 6 + lev) * 2 + s
                        pe.wait_ge(sm["xs_done"], n + 1)
                        if lev < 5:
                            for h in range(H):
                                mm(ps[:, 4 * s + 2, h * P:(h + 1) * P], iv[s]["N"][:, h, :], iv[s]["X"][:, h, :],
                                   start=True, stop=True)
                        for h in range(H):
                            last = mm(ps[:, 4 * s + 3, h * P:(h + 1) * P], iv[s]["X"][:, h, :], iv[s]["N"][:, h, :],
                                      start=True, stop=True)
                        last.then_inc(sm["pq_mm"], 1)

            pe.wait_ge(sm["upd"], 2 * 60)
            for i in range(NT):
                for d in range(2):
                    m = 2 * i + d
                    c = order[d][i]
                    cc = slice(c * P, (c + 1) * P)
                    if i == 0:
                        pe.wait_ge(sm["s_init"], 2)
                    need(pe, sm["s_upd"], m - 1)
                    lat_before = len([q for q in LATSTEP if q <= m - 2])
                    need(pe, sm["o1_done"], lat_before)
                    for h in range(H):
                        last = mm(ps[:, 4 * d, h * P:(h + 1) * P], kT[:, h, cc], S[:, d, h * P:(h + 1) * P],
                                  start=True, stop=True)
                    last.then_inc(sm["ks_mm"], 1)
                    if c < NLAT:
                        need(pe, sm["t2_done"], lat_before)
                        for h in range(H):
                            last = mm(ps[:, 4 * d + 3, h * P:(h + 1) * P], qT[:, h, cc], S[:, d, h * P:(h + 1) * P],
                                      start=True, stop=True)
                        last.then_inc(sm["qs_mm"], 1)
                for d in range(2):
                    m = 2 * i + d
                    pe.wait_ge(sm["r_done"], 2 * (m + 1))
                    pe.wait_ge(sm["um_done"], m + 1)
                    for h in range(H):
                        last = mm(ps[:, 4 * d + 1, h * P:(h + 1) * P], Um[:, d, h * P:(h + 1) * P],
                                  R[:, d, h * P:(h + 1) * P], start=True, stop=True)
                    last.then_inc(sm["tr4_mm"], 1)
                for d in range(2):
                    m = 2 * i + d
                    c = order[d][i]
                    pe.wait_ge(sm["vv_done"], 2 * (m + 1))
                    for h in range(H):
                        last = mm(ps[:, 4 * d + 2, h * P:(h + 1) * P], k_tok[:, c, h * P:(h + 1) * P],
                                  Vs[:, d, h * P:(h + 1) * P], start=True, stop=True)
                    last.then_inc(sm["ds_mm"], 1)
                    if c < NLAT:
                        for h in range(H):
                            last = mm(ps[:, 4 * d, h * P:(h + 1) * P], QK[:, d * NLAT + c, h * P:(h + 1) * P],
                                      Vn[:, d, h * P:(h + 1) * P], start=True, stop=True)
                        last.then_inc(sm["qkv_mm"], 1)

            NR = len(REST_TILES)
            for j in range(NR + 1):
                if j < NR:
                    if j == 0:
                        pe.wait_ge(sm["hT_back"], 16)
                        pe.wait_ge(sm["o1_done"], 16)
                    if j >= 2:
                        if j - 2 in ZT:
                            pe.wait_ge(sm["z_done"], ZT.index(j - 2) + 1)
                        else:
                            pe.wait_ge(sm["c_evac"], CT.index(j - 2) + 1)
                    project(pe, NG + j, ntok(REST_TILES[j]), None, 0, sm["in2_mm"], parity=j % 2)
                for a, (kind, t, s, w, jj) in enumerate(AUX2):
                    if jj != j:
                        continue
                    need(pe, sm["aux2_read"], a - 1)
                    bank = 6 + a % 2
                    if kind == "za":
                        pe.wait_ge(sm["o_ready"], 1)
                        h = t - first_of["za"]
                        for c in range(w // P):
                            cc = s // P + c
                            last = tr(ps[:, bank, c * P:(c + 1) * P], o_acc[:, cc, h * P:(h + 1) * P], ident)
                    else:
                        pe.wait_ge(sm["c_evac"], CT.index(t) + 1)
                        if kind == "dv":
                            for c in range(w // P):
                                last = tr(ps[:, bank, c * P:(c + 1) * P], dvT[:, s + c * P:s + (c + 1) * P], ident)
                        else:
                            src = (dq if kind == "dq" else dk)[:, t - first_of[kind], :]
                            last = mm(ps[:, bank, 0:w], cst("swap"), src[:, s:s + w], start=True, stop=True)
                    last.then_inc(sm["aux2_mm"], 1)

            pe.wait_ge(sm["n_sq"], 3)
            pe.wait_ge(sm["z_done"], len(ZT))
            pe.wait_ge(sm["c_evac"], len(CT))
            for s, w in segments(LAT):
                for k in range(2):
                    mm(ps[:, s // SEG, 0:w], ones, cq_sq[:, k, s:s + w], start=(k == 0), stop=(k == 1))
            for s, w in segments(TOK):
                last = mm(ps[:, 2 + s // SEG, 0:w], ones, kv_sq[:, s:s + w], start=True, stop=True)
            last.then_inc(sm["n_mm"], 1)
            pe.wait_ge(sm["kr_back"], 16)
            for s, w in segments(LAT):
                last = mm(ps[KR0:KR0 + 32, 6 + s // SEG, 0:w], cst("swap")[KR0:KR0 + 32, KR0:KR0 + 32],
                          krT[KR0:KR0 + 32, s:s + w], start=True, stop=True)
                if s == 0:
                    need(pe, sm["aux2_read"], len(AUX2))
            last.then_inc(sm["kr_mm"], 1)
            pe.wait_ge(sm["n_done"], 3)
            pe.wait_ge(sm["uq_in"], 32)
            for h in range(H):
                b = 2 * (h % 2)
                need(pe, sm["mq_ev"], h - 1)
                for s, w in segments(LAT):
                    for k in range(2):
                        last = mm(ps[0:MLA_QK, b + s // SEG, 0:w], uq_sb[:, k, h * MLA_QK:(h + 1) * MLA_QK],
                                  cq[:, k, s:s + w], start=(k == 0), stop=(k == 1))
                last.then_inc(sm["mq_mm"], 1)
                if h >= 1:
                    swap_q(pe, h - 1)
            for v in range(NT // 2):
                if v < 2:
                    pe.wait_ge(sm["mq_ev"], H)
                else:
                    pe.wait_ge(sm["mv_ev"], v - 1)
                for e in range(2):
                    c = 2 * v + e
                    last = mm(ps[:, v % 2, 256 * e:256 * e + 256], ckv[:, c * P:(c + 1) * P],
                              ukv_sb.rearrange("p (h a) -> p h a", h=H)[:, :, MLA_NOPE:], start=True, stop=True)
                last.then_inc(sm["mv_mm"], 1)
            swap_q(pe, H - 1)
            for h in range(H):
                if h == 0:
                    pe.wait_ge(sm["mv_ev"], NT // 2)
                    pe.wait_ge(sm["n_ln"], 2)
                need(pe, sm["mk_ev"], h - 1)
                b = 3 * (h % 2)
                for s, w in segments(TOK):
                    last = mm(ps[0:MLA_NOPE, b + s // SEG, 0:w], ukv_sb[:, h * P:h * P + MLA_NOPE],
                              ckv[:, s:s + w], start=True, stop=True)
                last.then_inc(sm["mk_mm"], 1)

            def scores(n):
                qb, u = UNITS[n]
                qc = slice(qb * P, (qb + 1) * P)
                for e, st in enumerate(sets_of(n)):
                    if st >= 2:
                        pe.wait_ge(sm["p_exp"], st - 1)
                    if st < 2:
                        pe.wait_ge(sm["mk_ev"], H)
                        pe.wait_ge(sm["mk_rope"], H)
                        pe.wait_ge(sm["mq_done"], H)
                        pe.wait_ge(sm["rope_done"], 2 * len(ROPED))
                    b = 3 * (st % 2)
                    for s, w in KSEG:
                        if u < H:
                            last = mm(ps[:, b + s // SEG, 0:w], QTm[0:MLA_QK, u, qc], KTm[0:MLA_QK, u, s:s + w],
                                      start=True, stop=True)
                        else:
                            g = 2 * (u - H) + e
                            r = 32 * (g % 4)
                            last = mm(ps[:, b + s // SEG, 0:w], dq[r:r + 32, g // 4, qc], dk[r:r + 32, g // 4, s:s + w],
                                      start=True, stop=True)
                    last.then_inc(sm["sc_mm"], 1)

            def turn_probs(n):
                qb, u = UNITS[n]
                slot = sets_of(n)[0] % 4
                if u < H:
                    pe.wait_ge(sm["p_exp"], sets_of(n)[0] + 1)
                else:
                    pe.wait_ge(sm["w_done"], qb * H + u - H + 1)
                for gi, (s, w) in enumerate(KSEG):
                    q = 3 * n + gi
                    if q > 0:
                        wait_turn_copy(pe, q)
                    elif q == 0:
                        pe.wait_ge(sm["kr_t"], 1)
                    if gi == 0 and u == 0 and qb > 0:
                        pe.wait_ge(sm["mix_b"], 2 * qb)
                    for c in range(w // P):
                        last = tr(ps[:, 6, c * P:(c + 1) * P], prob[:, slot, s + c * P:s + (c + 1) * P], ident)
                    last.then_inc(sm["wt_mm"], 1)

            def pv(n):
                qb, u = UNITS[n]
                wait_turn_copy(pe, 3 * n + 3)
                need(pe, sm["pv_ev"], n)
                V = V_tok if u < H else dv_tok
                h = u % H
                for c in range(NT):
                    last = mm(ps[:, 7, u * 64:u * 64 + 64], wT[:, n % 2, c * P:(c + 1) * P],
                              V[:, c, h * 64:h * 64 + 64], start=(c == 0), stop=(c == NT - 1))
                last.then_inc(sm["pv_mm"], 1)

            def turn_out(qb):
                pe.wait_ge(sm["d_norm"], qb + 1)
                wait_turn_copy(pe, 3 * 8 * (qb + 1))
                for i in range(4):
                    last = tr(ps[:, 6, i * P:(i + 1) * P], o_tok[:, qb % 2, i * P:(i + 1) * P], ident)
                last.then_inc(sm["ot_mm"], 1)

            scores(0)
            for n in range(len(UNITS)):
                if n + 1 < len(UNITS):
                    scores(n + 1)
                turn_probs(n)
                pv(n)
                if n % 8 == 7:
                    turn_out(n // 8)

            for t in range(NLAT):
                if t == 0:
                    pe.wait_ge(sm["wo_in"], 16 * KD)
                    pe.wait_ge(sm["mix_b"], 2 * NLAT)
                    pe.wait_ge(sm["p_exp"], NSET)
                b = 2 * (t % 2)
                need(pe, sm["y_scaled"], t - 1)
                for i in range(2):
                    for k in range(KD):
                        last = mm(ps[:, b + i, :], mixT[:, k, t * P:(t + 1) * P], wo_sb[k][:, i * SEG:(i + 1) * SEG],
                                  start=(k == 0), stop=(k == KD - 1))
                last.then_inc(sm["y_mm"], 1)

        @block.scalar
        def _(act):
            A = nc.scalar.activation
            act.wait_ge(sm["cols_in"], 16)
            A(cs_e, col("c", 0, 16), ACT.Exp, scale=-1.0).then_inc(sm["c_exp"], 1)
            act.wait_ge(sm["setup"], 1)

            def x_stat(t):
                act.wait_ge(x_in[t % 4], 16 * (t // 4 + 1))
                need(act, sm["ssq_done"], t)
                A(junk, xin[:, t % 4, :], ACT.Square, accum_out=ssq[:, t:t + 1]).then_inc(sm["ssq_done"], 1)
                act.wait_ge(sm["ssq_done"], t + 1)
                A(rstd[:, t:t + 1], ssq[:, t:t + 1], ACT.Ln, scale=1.0 / D, bias=eps_col).then_inc(sm["rs_done"], 1)
                act.wait_ge(sm["rs_done"], 2 * t + 1)
                A(rstd[:, t:t + 1], rstd[:, t:t + 1], ACT.Exp, scale=-0.5).then_inc(sm["rs_done"], 1)

            for gi, (t0, n) in enumerate(GROUPS):
                for t in range(t0, t0 + n):
                    x_stat(t)
                for k in range(1, KD, 2):
                    q = gi * KD + k
                    act.wait_ge(sm["xT_mm"], q + 1)
                    act.wait_ge(sm["mod_A"], 2)
                    m = 0 if t0 < NLAT else 1
                    A(hT[:, k, t0 * P:(t0 + n) * P], ps[:, 2 + q % 6, 0:n * P], ACT.Identity,
                      scale=mA[:, 2 * k + m:2 * k + m + 1], bias=mod[:, 2 * k + m:2 * k + m + 1]
                      ).then_inc(sm["hT_act"], 1)
            act.wait_ge(sm["gp_mm"], 1)
            A(GP[:, :], ps[:, 0:2, :], ACT.Copy).then_inc(sm["GP_done"], 1)

            for i in range(NG + 3):
                if i < NG:
                    act.wait_ge(sm["in_mm"], i + 1)
                    b = 3 * (i % 2)
                    if i == 0:
                        A(misc[:, 0:LAT], ps[:, b:b + 2, :], ACT.Copy)
                        A(misc[:, LAT:TOK], ps[:, b + 2, 0:CTX], ACT.Copy).then_inc(sm["evac_done"], 1)
                    else:
                        if i < 3:
                            act.wait_ge(sm["pad_done"], 6)
                        need(act, sm["conv_step"], 5 * (i - 2))
                        op = A(raw[i % 2][:, 2:2 + LAT], ps[:, b:b + 2, :], ACT.Copy)
                        if GDN_TILES[i] != "q":
                            op = A(raw[i % 2][:, CTX_RAW:CTX_RAW + CTX], ps[:, b + 2, 0:CTX], ACT.Copy)
                        op.then_inc(sm["evac_done"], 1)
                t = i - 1
                if 1 <= t < NG:
                    n = LAT if GDN_TILES[t] == "q" else CV_W
                    act.wait_ge(sm["conv_step"], 5 * t)
                    need(act, sm["silu_done"], t - 1)
                    A(ebuf[:, 0:n], cv[t % 2][:, 0:n], ACT.Exp, scale=-1.0).then_inc(sm["exp_done"], 1)
                jobs = aux_at(i, ("ones",))
                for j, (_, t, s, w, _) in jobs:
                    act.wait_ge(sm["aux_mm"], j + 1)
                    big = float(DK) if GDN_TILES[t] == "q" else 1.0
                    A(sqb[t % 2][:, s:s + w], ps[:, 6 + j % 2, 0:w], ACT.Ln, scale=big,
                      bias=eps_q if GDN_TILES[t] == "q" else eps_col).then_inc(sm["aux_read"], 1)
                if jobs:
                    j, (_, t, _, _, _) = jobs[-1]
                    n = ntok(GDN_TILES[t])
                    act.wait_ge(sm["aux_read"], j + 1)
                    A(sqb[t % 2][:, 0:n], sqb[t % 2][:, 0:n], ACT.Exp, scale=-0.5).then_inc(sm["rn_done"], 1)
                for j, (what, t, s, w, _) in aux_at(i, ("turn", "logits")):
                    act.wait_ge(sm["aux_mm"], j + 1)
                    bank = 6 + j % 2
                    if what == "logits":
                        A(gates[:, 0:16 * NT], ps[:, bank, 0:16 * NT], ACT.Copy).then_inc(sm["aux_read"], 1)
                        continue
                    h = head_of(t)
                    dst = k_tok if GDN_TILES[t] == "k" else v_tok
                    A(dst[:, s // P:(s + w) // P, h * P:(h + 1) * P],
                      ps[:, bank, 0:w].rearrange("p (c n) -> p c n", n=P), ACT.Copy).then_inc(sm["aux_read"], 1)

            act.wait_ge(sm["gt_d"], 2)
            A(en, na, ACT.Exp, scale=-1.0).then_inc(sm["gt_a"], 1)
            act.wait_ge(sm["gt_a"], 1)
            A(en, en, ACT.Ln, bias=one_col).then_inc(sm["gt_a"], 1)
            A(beta, lg[:, :, 0:8], ACT.Exp, scale=-1.0).then_inc(sm["gt_a"], 1)
            A(ea[:, :], col("alog", 0, 8), ACT.Exp).then_inc(sm["gt_a"], 1)
            act.wait_ge(sm["gt_d"], 7)
            A(EG, gam, ACT.Exp).then_inc(sm["gt_a"], 1)
            A(EKD, dtk, ACT.Exp).then_inc(sm["gt_a"], 1)
            A(GL, tot, ACT.Exp).then_inc(sm["gt_a"], 1)

            for pair in range(NT // 2):
                for s in range(2):
                    c = 2 * pair + s
                    act.wait_ge(sm["ex_done"], 8 * (c + 1))
                    A(iv[s]["E"], iv[s]["E"], ACT.Exp).then_inc(sm["e_done"], 1)
                for s in range(2):
                    c = 2 * pair + s
                    act.wait_ge(sm["tr_mm"], c + 1)
                    A(iv[s]["P"], ps[:, 4 * s, :], ACT.Copy).then_inc(sm["p_done"], 1)

            for m in LATSTEP:
                i, d = m // 2, m % 2
                c = order[d][i]
                act.wait_ge(sm["qs_mm"], LATSTEP.index(m) + 1)
                need(act, sm["oa_done"], len([q for q in LATSTEP if q <= m - 2]))
                for h in range(H):
                    op = A(t2[:, d, h * P:(h + 1) * P], ps[:, 4 * d + 3, h * P:(h + 1) * P], ACT.Copy,
                           scale=EG[:, c, 4 * d + h:4 * d + h + 1])
                op.then_inc(sm["t2_done"], 1)
            o_ss, o_rs = o_stat[:, 0:NLAT * H], o_stat[:, NLAT * H:]
            act.wait_ge(sm["ostat_d"], 1)
            A(o_rs, o_ss, ACT.Ln, scale=1.0 / P, bias=eps_col).then_inc(sm["ostat_a"], 1)
            act.wait_ge(sm["ostat_a"], 1)
            A(o_rs, o_rs, ACT.Exp, scale=-0.5).then_inc(sm["ostat_a"], 1)

            for j, kind in enumerate(REST_TILES):
                act.wait_ge(sm["in2_mm"], j + 1)
                b = 3 * (j % 2)
                i = j - first_of[kind]
                if j in ZT:
                    z = ZT.index(j)
                    need(act, sm["z_done"], z - 1)
                    A(zexp[:, z % 2, :], ps[:, b:b + 2, :], ACT.Exp, scale=-1.0).then_inc(sm["z_exp"], 1)
                    continue
                if kind == "dv":
                    need(act, sm["aux2_mm"], len([a for a in AUX2 if a[4] <= j]) if i else 0)
                dst = {"cq": lambda: cq[:, i, :], "ckv": lambda: ckv, "dq": lambda: dq[:, i, :],
                       "dk": lambda: dk[:, i, :], "dv": lambda: dvT}[kind]()
                op = A(dst[:, 0:LAT], ps[:, b:b + 2, :], ACT.Copy, scale=DIFF_SCALE if kind == "dq" else 1.0)
                if kind not in LAT_ONLY:
                    op = A(dst[:, LAT:TOK], ps[:, b + 2, 0:CTX], ACT.Copy)
                op.then_inc(sm["c_evac"], 1)

            act.wait_ge(sm["lam_d"], 4)
            A(lamt[:, 0:2], lamt[:, 0:2], ACT.Exp).then_inc(sm["lam_a"], 1)

            act.wait_ge(sm["n_mm"], 1)
            A(cq_rn, ps[:, 0:2, :], ACT.Ln, scale=1.0 / Q_RANK, bias=eps_col).then_inc(sm["n_ln"], 1)
            A(kv_rn[:, 0:LAT], ps[:, 2:4, :], ACT.Ln, scale=1.0 / KV_RANK, bias=eps_col)
            A(kv_rn[:, LAT:TOK], ps[:, 4, 0:CTX], ACT.Ln, scale=1.0 / KV_RANK,
              bias=eps_col).then_inc(sm["n_ln"], 1)
            act.wait_ge(sm["n_ln"], 2)
            A(cq_rn, cq_rn, ACT.Exp, scale=-0.5).then_inc(sm["n_exp"], 1)
            A(kv_rn, kv_rn, ACT.Exp, scale=-0.5).then_inc(sm["n_exp"], 1)
            for h in range(H):
                act.wait_ge(sm["mq_mm"], h + 1)
                b = 2 * (h % 2)
                A(QTm[0:MLA_QK, h, :], ps[0:MLA_QK, b:b + 2, :], ACT.Copy, scale=MLA_SCALE).then_inc(sm["mq_ev"], 1)
            for v in range(NT // 2):
                act.wait_ge(sm["mv_mm"], v + 1)
                A(V_tok[:, 2 * v:2 * v + 2, :], ps[:, v % 2, :].rearrange("p (a b) -> p a b", a=2),
                  ACT.Copy).then_inc(sm["mv_ev"], 1)
            for h in range(H):
                act.wait_ge(sm["mk_mm"], h + 1)
                b = 3 * (h % 2)
                A(KTm[0:MLA_NOPE, h, 0:LAT], ps[0:MLA_NOPE, b:b + 2, :], ACT.Copy)
                A(KTm[0:MLA_NOPE, h, LAT:TOK], ps[0:MLA_NOPE, b + 2, 0:CTX], ACT.Copy).then_inc(sm["mk_ev"], 1)
                if h == 0:
                    act.wait_ge(sm["kr_done"], 1)
                A(KTm[KR0:MLA_QK, h, :], krT[KR0:MLA_QK, :], ACT.Copy).then_inc(sm["mk_rope"], 1)

            def exps(n):
                qb, u = UNITS[n]
                for st in sets_of(n):
                    act.wait_ge(sm["mx_done"], st + 1)
                    if st >= 4:
                        prev = [q for q in range(len(UNITS)) if st - 4 in sets_of(q)][0]
                        act.wait_ge(sm["wt_mm"], 3 * (prev + 1))
                    if st < 4:
                        act.wait_ge(sm["n_done"], 3)
                    b = 3 * (st % 2)
                    A(prob[:, st % 4, :], ps[:, b:b + 3, :].rearrange("p a b -> p (a b)")[:, 0:TOK], ACT.Exp,
                      bias=nmax[:, st:st + 1], accum_out=lsum[:, st:st + 1]).then_inc(sm["p_exp"], 1)

            def turned(n, par):
                for gi, (s, w) in enumerate(KSEG):
                    q = 3 * n + gi
                    if q % 2 != par:
                        continue
                    act.wait_ge(sm["wt_mm"], q + 1)
                    need(act, sm["pv_mm"], n - 1)
                    A(wT[:, n % 2, s:s + w], ps[:, 6, 0:w], ACT.Copy).then_inc(sm["wt_ev_a"], 1)

            def d_stat(qb):
                act.wait_ge(sm["d_red"], qb + 1)
                A(drs[:, 4 * qb:4 * qb + 4], dss[:, 4 * qb:4 * qb + 4], ACT.Ln, scale=1.0 / DIFF_V,
                  bias=eps_col).then_inc(sm["d_ln"], 1)
                act.wait_ge(sm["d_ln"], qb + 1)
                A(drs[:, 4 * qb:4 * qb + 4], drs[:, 4 * qb:4 * qb + 4], ACT.Exp, scale=-0.5).then_inc(sm["d_exp"], 1)

            exps(0)
            for n in range(len(UNITS)):
                if n + 1 < len(UNITS):
                    exps(n + 1)
                turned(n, 0)
                if n % 8 == 7:
                    d_stat(n // 8)

            for t in range(NLAT):
                act.wait_ge(sm["y_mm"], t + 1)
                b = 2 * (t % 2)
                need(act, sm["y_sq"], t)
                A(y_junk, ps[:, b:b + 2, :], ACT.Square, accum_out=yst[:, t:t + 1]).then_inc(sm["y_sq"], 1)
                act.wait_ge(sm["y_sq"], t + 1)
                r = yst[:, NLAT + t:NLAT + t + 1]
                A(r, yst[:, t:t + 1], ACT.Ln, scale=1.0 / D, bias=eps_col).then_inc(sm["y_ln"], 1)
                act.wait_ge(sm["y_ln"], t + 1)
                A(r, r, ACT.Exp, scale=-0.5).then_inc(sm["y_exp"], 1)

        @block.vector
        def _(dve):
            V = nc.vector
            V.memset(eps_col, EPS)
            V.memset(one_col, 1.0)
            V.memset(eps_q, EPS * DK).then_inc(sm["setup"], 1)
            dve.wait_ge(sm["c_exp"], 1)
            V.tensor_scalar(cs_e, cs_e, 1.0, None, ALU.add).then_inc(sm["c_one"], 1)
            dve.wait_ge(sm["c_one"], 1)
            V.reciprocal(cs_e, cs_e).then_inc(sm["c_rec"], 1)
            dve.wait_ge(sm["c_rec"], 1)
            V.tensor_tensor(cs, cs_e, col("c", 0, 16), ALU.mult).then_inc(sm["c_silu"], 1)

            def xn(gi):
                t0, n = GROUPS[gi]
                for t in range(t0, t0 + n):
                    dve.wait_ge(sm["rs_done"], 2 * t + 2)
                    V.tensor_scalar(xin[:, t % 4, :], xin[:, t % 4, :], rstd[:, t:t + 1], None,
                                    ALU.mult).then_inc(sm["xn_done"], 1)

            def hT_even(gi):
                t0, n = GROUPS[gi]
                m = 0 if t0 < NLAT else 1
                for k in range(0, KD, 2):
                    q = gi * KD + k
                    dve.wait_ge(sm["xT_mm"], q + 1)
                    V.tensor_scalar(hT[:, k, t0 * P:(t0 + n) * P], ps[:, 2 + q % 6, 0:n * P],
                                    mA[:, 2 * k + m:2 * k + m + 1], mod[:, 2 * k + m:2 * k + m + 1],
                                    ALU.mult, ALU.add).then_inc(sm["hT_dve"], 1)

            xn(0)
            mod3 = mod.rearrange("p (j c) -> p j c", c=2)
            dve.wait_ge(sm["ada_mm"], 1)
            V.tensor_tensor(mod3[:, 0:16, :], ps[:, 0, 0:32].rearrange("p (j c) -> p j c", c=2),
                            col("ada_b", 0, 16).unsqueeze(2).broadcast_to([P, 16, 2]), ALU.add
                            ).then_inc(sm["mod_add"], 1)
            dve.wait_ge(sm["mod_add"], 1)
            mA3 = mA.rearrange("p (j c) -> p j c", c=2)
            V.tensor_scalar(mA, mod[:, 16:32], 1.0, None, ALU.add).then_inc(sm["mod_A"], 1)
            dve.wait_ge(sm["mod_A"], 1)
            V.tensor_tensor(mA3, mA3, col("pre", 0, 8).unsqueeze(2).broadcast_to([P, 8, 2]),
                            ALU.mult).then_inc(sm["mod_A"], 1)
            dve.wait_ge(sm["mod_A"], 2)
            hT_even(0)
            xn(1)
            hT_even(1)
            xn(2)
            hT_even(2)
            dve.wait_ge(sm["ada_gate"], 1)
            V.tensor_tensor(mod3[:, 16:24, :], ps[:, 1, 0:16].rearrange("p (j c) -> p j c", c=2),
                            col("ada_b", 16, 8).unsqueeze(2).broadcast_to([P, 8, 2]), ALU.add
                            ).then_inc(sm["mod_add"], 1)
            dve.wait_ge(sm["mod_add"], 2)
            V.tensor_tensor(gp_col, mod3[:, 16:24, 0], col("post", 0, 8), ALU.mult).then_inc(sm["gp_done"], 1)
            dve.wait_ge(sm["gp_done"], 1)
            V.tensor_tensor(gp_diag, ident.unsqueeze(1).broadcast_to([P, KD, P]),
                            gp_col.unsqueeze(2).broadcast_to([P, KD, P]), ALU.mult).then_inc(sm["diag_done"], 1)

            for i in range(NG + 1):
                if 1 <= i < NG:
                    n = LAT if GDN_TILES[i] == "q" else CV_W
                    dve.wait_ge(sm["evac_done"], i + 1)
                    need(dve, sm["silu_done"], i - 2)
                    src, dst = raw[i % 2], cv[i % 2]
                    for j in range(CONV_W):
                        wj = col("conv", (i - 1) * CONV_W + j)
                        if j == 0:
                            op = V.tensor_scalar(dst[:, 0:n], src[:, 0:n], wj, None, ALU.mult)
                        else:
                            dve.wait_ge(sm["conv_step"], 5 * (i - 1) + j)
                            op = V.scalar_tensor_tensor(out=dst[:, 0:n], in0=src[:, j:j + n], scalar=wj,
                                                        in1=dst[:, 0:n], op0=ALU.mult, op1=ALU.add)
                        op.then_inc(sm["conv_step"], 1)
                t = i - 1
                if 1 <= t < NG:
                    n = LAT if GDN_TILES[t] == "q" else CV_W
                    dve.wait_ge(sm["add1"], t)
                    V.reciprocal(ebuf[:, 0:n], ebuf[:, 0:n]).then_inc(sm["rec"], 1)

            logits_read = [j for j, a in enumerate(AUX) if a[0] == "logits"][0] + 1
            dve.wait_ge(sm["aux_read"], logits_read)
            V.tensor_tensor(xa, lg[:, :, 8:16], col("dt", 0, 8).unsqueeze(1).broadcast_to([P, NT, 8]),
                            ALU.add).then_inc(sm["gt_d"], 1)
            dve.wait_ge(sm["gt_d"], 1)
            V.scalar_tensor_tensor(out=na, in0=xa, scalar=-1.0, in1=xa, op0=ALU.mult,
                                   op1=ALU.max).then_inc(sm["gt_d"], 1)
            dve.wait_ge(sm["gt_a"], 4)
            V.scalar_tensor_tensor(out=sp, in0=xa, scalar=0.0, in1=en, op0=ALU.max,
                                   op1=ALU.add).then_inc(sm["gt_d"], 1)
            dve.wait_ge(sm["gt_d"], 3)
            V.scalar_tensor_tensor(out=g_, in0=sp, scalar=-1.0, in1=ea[:, :].unsqueeze(1).broadcast_to([P, NT, 8]),
                                   op0=ALU.mult, op1=ALU.mult).then_inc(sm["gt_d"], 1)
            dve.wait_ge(sm["gt_mm"], 1)
            V.tensor_copy(gam, ps[:, 0, 0:8 * NT].rearrange("p (c n) -> p c n", n=8)).then_inc(sm["gt_d"], 1)
            V.tensor_copy(tot, ps[:, 0, 128:128 + 8 * NT].rearrange("p (c n) -> p c n", n=8)).then_inc(sm["gt_d"], 1)
            dve.wait_ge(sm["gt_d"], 6)
            V.tensor_tensor(dtk, tot, gam, ALU.subtract).then_inc(sm["gt_d"], 1)
            V.tensor_scalar(beta, beta, 1.0, None, ALU.add).then_inc(sm["gt_d"], 1)
            dve.wait_ge(sm["gt_d"], 8)
            V.reciprocal(beta, beta).then_inc(sm["gt_d"], 1)
            dve.wait_ge(sm["gt_d"], 9)
            dve.wait_ge(sm["gt_a"], 7)
            V.tensor_tensor(bek, beta, EKD, ALU.mult).then_inc(sm["gt_d"], 1)

            for pair in range(NT // 2):
                for s in range(2):
                    c = 2 * pair + s
                    dve.wait_ge(sm["pre_mm"], c + 1)
                    for d in range(2):
                        for h in range(H):
                            V.scalar_tensor_tensor(
                                out=iv[s]["E"][:, 4 * d + h, :], in0=ps[:, 4 * s + 2 + d, h * P:(h + 1) * P],
                                scalar=gam[:, c, 4 * d + h:4 * d + h + 1], in1=cst("neg_f" if d == 0 else "neg_b"),
                                op0=ALU.subtract, op1=ALU.min).then_inc(sm["ex_done"], 1)
                for s in range(2):
                    c = 2 * pair + s
                    dve.wait_ge(sm["pool_w"], 3 * (c + 1))
                    V.tensor_tensor(iv[s]["At"], ps[:, 4 * s, :].rearrange("p (h n) -> p h n", n=P), iv[s]["At"],
                                    ALU.mult).then_inc(sm["at_done"], 1)
                    if c < NLAT:
                        for d in range(2):
                            V.tensor_tensor(QK[:, d * NLAT + c, :].rearrange("p (h n) -> p h n", n=P),
                                            ps[:, 4 * s + 1, :].rearrange("p (h n) -> p h n", n=P),
                                            iv[s]["E"][:, 4 * d:4 * d + 4, :], ALU.mult).then_inc(sm["qk_done"], 1)
                for lev in range(6):
                    for s in range(2):
                        n = (pair * 6 + lev) * 2 + s
                        dve.wait_ge(sm["x_mm"], n + 1)
                        V.tensor_tensor(iv[s]["X"], ps[:, 4 * s + 1, :].rearrange("p (h n) -> p h n", n=P),
                                        heads(cst(f"sib{LEVELS[lev + 1]}")), ALU.mult).then_inc(sm["xs_done"], 1)
                    for s in range(2):
                        c = 2 * pair + s
                        n = (pair * 6 + lev) * 2 + s
                        dve.wait_ge(sm["pq_mm"], n + 1)
                        if lev < 5:
                            V.tensor_tensor(iv[s]["P"], iv[s]["P"],
                                            ps[:, 4 * s + 2, :].rearrange("p (h n) -> p h n", n=P),
                                            ALU.subtract).then_inc(sm["upd"], 1)
                        V.tensor_tensor(Q_all[:, c, :], Q_all[:, c, :], ps[:, 4 * s + 3, :],
                                        ALU.subtract).then_inc(sm["upd"], 1 if lev < 5 else 2)

            def h3(ap):
                return ap.rearrange("p (h n) -> p h n", n=P)
            dve.wait_ge(sm["gt_d"], 10)
            for i in range(NT):
                for d in range(2):
                    m = 2 * i + d
                    c = order[d][i]
                    dve.wait_ge(sm["ks_mm"], m + 1)
                    V.tensor_tensor(h3(R[:, d, :]), h3(ps[:, 4 * d, :]), per_head(EG[:, c, 4 * d:4 * d + 4]),
                                    ALU.mult).then_inc(sm["r_done"], 1)
                    dve.wait_ge(sm["r_done"], 2 * m + 1)
                    V.tensor_tensor(R[:, d, :], v_tok[:, c, :], R[:, d, :], ALU.subtract).then_inc(sm["r_done"], 1)
                for d in range(2):
                    m = 2 * i + d
                    c = order[d][i]
                    dve.wait_ge(sm["tr4_mm"], m + 1)
                    V.tensor_tensor(h3(Vs[:, d, :]), h3(ps[:, 4 * d + 1, :]), per_head(bek[:, c, 4 * d:4 * d + 4]),
                                    ALU.mult).then_inc(sm["vv_done"], 1)
                    need(dve, sm["qkv_mm"], len([q for q in LATSTEP if q <= m - 2]))
                    V.tensor_tensor(h3(Vn[:, d, :]), h3(ps[:, 4 * d + 1, :]), per_head(beta[:, c, 4 * d:4 * d + 4]),
                                    ALU.mult).then_inc(sm["vv_done"], 1)
                for d in range(2):
                    m = 2 * i + d
                    c = order[d][i]
                    dve.wait_ge(sm["ds_mm"], m + 1)
                    dve.wait_ge(sm["sg_done"], m + 1)
                    V.tensor_tensor(S[:, d, :], Sg[:, d, :], ps[:, 4 * d + 2, :], ALU.add).then_inc(sm["s_upd"], 1)
                    if c < NLAT:
                        li = LATSTEP.index(m)
                        dve.wait_ge(sm["qkv_mm"], li + 1)
                        dve.wait_ge(sm["t2_done"], li + 1)
                        V.tensor_tensor(t2[:, d, :], t2[:, d, :], ps[:, 4 * d, :], ALU.add).then_inc(sm["o1_done"], 1)
            dve.wait_ge(sm["osq_done"], 1)
            V.tensor_reduce(o_stat[:, 0:NLAT * H], o_sq, AX.X, ALU.add).then_inc(sm["ostat_d"], 1)
            dve.wait_ge(sm["ostat_a"], 2)
            oa3 = o_acc.rearrange("p c (h n) -> p (c h) n", n=P)
            V.tensor_tensor(oa3, oa3, o_stat[:, NLAT * H:].unsqueeze(2).broadcast_to([P, NLAT * H, P]),
                            ALU.mult).then_inc(sm["o_ready"], 1)

            lam4 = col("lam", 0, 128).rearrange("p (a b n) -> p a b n", a=2, b=2)
            lp = lam_p[:, :].rearrange("p (a n) -> p a n", a=2)
            V.tensor_tensor(lp, lam4[:, :, 0, :], lam4[:, :, 1, :], ALU.mult).then_inc(sm["lam_d"], 1)
            dve.wait_ge(sm["lam_d"], 1)
            V.tensor_reduce(lamt[:, 0:2], lp, AX.X, ALU.add).then_inc(sm["lam_d"], 1)
            V.tensor_scalar(lamt[:, 4:5], col("sg"), 1.0 - LAM_INIT, None, ALU.mult).then_inc(sm["lam_d"], 2)

            def z_dest(j):
                kind = REST_TILES[j]
                i = j - first_of[kind]
                return {"za": lambda: zbuf[:, i % 2, :], "zb": lambda: mixT[:, 4 + i, :],
                        "dz": lambda: mixT[:, 6 + i, :]}[kind]()

            for j in range(len(REST_TILES) + 1):
                if j < len(REST_TILES) and j in ZT:
                    z = ZT.index(j)
                    b = 3 * (j % 2)
                    dve.wait_ge(sm["z_add"], z + 1)
                    V.reciprocal(zexp[:, z % 2, :], zexp[:, z % 2, :]).then_inc(sm["z_rec"], 1)
                    dve.wait_ge(sm["z_rec"], z + 1)
                    V.tensor_tensor(z_dest(j).rearrange("p (a b) -> p a b", a=2), ps[:, b:b + 2, :],
                                    zexp[:, z % 2, :].rearrange("p (a b) -> p a b", a=2),
                                    ALU.mult).then_inc(sm["z_done"], 1)
                for a, (kind, t, s, w, jj) in enumerate(AUX2):
                    if jj != j:
                        continue
                    dve.wait_ge(sm["aux2_mm"], a + 1)
                    bank = 6 + a % 2
                    if kind == "za":
                        h = t - first_of["za"]
                        dve.wait_ge(sm["z_done"], ZT.index(t) + 1)
                        V.scalar_tensor_tensor(out=mixT[:, h, s:s + w], in0=ps[:, bank, 0:w], scalar=col("og"),
                                               in1=zbuf[:, h % 2, s:s + w], op0=ALU.mult,
                                               op1=ALU.mult).then_inc(sm["aux2_read"], 1)
                    elif kind == "dv":
                        i = t - first_of["dv"]
                        V.tensor_copy(dv_tok[:, s // P:(s + w) // P, i * P:(i + 1) * P],
                                      ps[:, bank, 0:w].rearrange("p (c n) -> p c n", n=P)
                                      ).then_inc(sm["aux2_read"], 1)
                    else:
                        dve.wait_ge(sm["rope_in"], 16)
                        r = ROPED.index(t)
                        if s == 0:
                            need(dve, sm["rope_done"], 2 * r)
                        V.tensor_tensor(rbuf[:, s:s + w], ps[:, bank, 0:w], rope[:, 1, s:s + w],
                                        ALU.mult).then_inc(sm["aux2_read"], 1)

            dve.wait_ge(sm["n_exp"], 2)
            for k in range(2):
                V.scalar_tensor_tensor(out=cq[:, k, :], in0=cq[:, k, :], scalar=col("qg", k), in1=cq_rn,
                                       op0=ALU.mult, op1=ALU.mult).then_inc(sm["n_done"], 1)
            V.scalar_tensor_tensor(out=ckv, in0=ckv, scalar=col("kvg"), in1=kv_rn,
                                   op0=ALU.mult, op1=ALU.mult).then_inc(sm["n_done"], 1)
            rows = slice(KR0, KR0 + MLA_ROPE)
            dve.wait_ge(sm["n_done"], 3)
            dve.wait_ge(sm["kr_mm"], 1)
            dve.wait_ge(sm["rope_done"], 2 * len(ROPED))
            V.tensor_tensor(rbuf[rows, :].rearrange("p (a b) -> p a b", a=2), ps[rows, 6:8, :],
                            rope[rows, 1, :].rearrange("p (a b) -> p a b", a=2), ALU.mult).then_inc(sm["kr_t"], 1)
            V.tensor_tensor(krT[rows, 0:LAT], krT[rows, 0:LAT], rope[rows, 0, :], ALU.mult).then_inc(sm["kr_c"], 1)
            dve.wait_ge(sm["kr_t"], 1)
            dve.wait_ge(sm["kr_c"], 1)
            V.tensor_tensor(krT[rows, 0:LAT], krT[rows, 0:LAT], rbuf[rows, :], ALU.add).then_inc(sm["kr_done"], 1)
            for h in range(H):
                dve.wait_ge(sm["mq_swap"], h + 1)
                dve.wait_ge(sm["mq_done"], h) if h else dve.wait_ge(sm["kr_done"], 1)
                V.tensor_tensor(rbuf[rows, :].rearrange("p (a b) -> p a b", a=2), ps[rows, 6:8, :],
                                rope[rows, 1, :].rearrange("p (a b) -> p a b", a=2), ALU.mult).then_inc(sm["mq_t"], 1)
                V.tensor_tensor(QTm[rows, h, :], QTm[rows, h, :], rope[rows, 0, :], ALU.mult).then_inc(sm["mq_c"], 1)
                dve.wait_ge(sm["mq_t"], h + 1)
                dve.wait_ge(sm["mq_c"], h + 1)
                V.tensor_tensor(QTm[rows, h, :], QTm[rows, h, :], rbuf[rows, :], ALU.add).then_inc(sm["mq_done"], 1)

            dve.wait_ge(sm["lam_a"], 1)
            V.tensor_tensor(lamt[:, 5:6], lamt[:, 1:2], lamt[:, 0:1], ALU.subtract).then_inc(sm["lam_d"], 1)
            dve.wait_ge(sm["lam_d"], 5)
            V.tensor_scalar(lamt[:, 6:7], lamt[:, 5:6], -LAM_INIT, None, ALU.add).then_inc(sm["lam_d"], 1)
            dve.wait_ge(sm["lam_d"], 6)

            def row_max(n):
                for st in sets_of(n):
                    dve.wait_ge(sm["sc_mm"], st + 1)
                    b = 3 * (st % 2)
                    V.tensor_reduce(nmax[:, st:st + 1], ps[:, b:b + 3, :].rearrange("p a b -> p (a b)")[:, 0:TOK],
                                    AX.X, ALU.max, negate=True).then_inc(sm["mx_done"], 1)

            linv = [0]

            def counted(op):
                linv[0] += 1
                op.then_inc(sm["l_inv"], 1)
                return linv[0]

            def combine(n):
                qb, u = UNITS[n]
                st = sets_of(n)
                dve.wait_ge(sm["p_exp"], st[-1] + 1)
                v = counted(V.reciprocal(rinv[:, n:n + 1], lsum[:, st[0]:st[0] + 1]))
                if u < H:
                    return
                v = counted(V.reciprocal(rinv1[:, n:n + 1], lsum[:, st[1]:st[1] + 1]))
                dve.wait_ge(sm["l_inv"], v)
                v = counted(V.scalar_tensor_tensor(out=coef[:, n:n + 1], in0=lsum[:, st[0]:st[0] + 1],
                                                   scalar=lamt[:, 6:7], in1=rinv1[:, n:n + 1],
                                                   op0=ALU.mult, op1=ALU.mult))
                dve.wait_ge(sm["l_inv"], v)
                p0, p1 = prob[:, st[0] % 4, :], prob[:, st[1] % 4, :]
                V.scalar_tensor_tensor(out=p0, in0=p1, scalar=coef[:, n:n + 1], in1=p0, op0=ALU.mult,
                                       op1=ALU.add).then_inc(sm["w_done"], 1)

            def turned(n):
                for gi, (s, w) in enumerate(KSEG):
                    q = 3 * n + gi
                    if q % 2 == 0:
                        continue
                    dve.wait_ge(sm["wt_mm"], q + 1)
                    need(dve, sm["pv_mm"], n - 1)
                    V.tensor_copy(wT[:, n % 2, s:s + w], ps[:, 6, 0:w]).then_inc(sm["wt_ev_d"], 1)

            def out_part(n):
                qb, u = UNITS[n]
                dve.wait_ge(sm["pv_mm"], n + 1)
                dve.wait_ge(sm["l_inv"], linv[0])
                V.tensor_scalar(o_tok[:, qb % 2, u * 64:u * 64 + 64], ps[:, 7, u * 64:u * 64 + 64],
                                rinv[:, n:n + 1], None, ALU.mult).then_inc(sm["pv_ev"], 1)

            def finish(qb):
                od = o_tok[:, qb % 2, H * 64:].rearrange("p (h n) -> p h n", n=64)
                dve.wait_ge(sm["pv_ev"], 8 * (qb + 1))
                V.tensor_tensor(d_sq, od, od, ALU.mult).then_inc(sm["d_sqd"], 1)
                dve.wait_ge(sm["d_sqd"], qb + 1)
                V.tensor_reduce(dss[:, 4 * qb:4 * qb + 4], d_sq, AX.X, ALU.add).then_inc(sm["d_red"], 1)
                dve.wait_ge(sm["d_exp"], qb + 1)
                V.tensor_tensor(od, od, drs[:, 4 * qb:4 * qb + 4].unsqueeze(2).broadcast_to([P, H, 64]),
                                ALU.mult).then_inc(sm["d_norm"], 1)
                dve.wait_ge(sm["ot_mm"], qb + 1)
                mx = mixT[:, :, qb * P:(qb + 1) * P]
                pso = ps[:, 6, :].rearrange("p (i n) -> p i n", n=P)
                V.tensor_tensor(mx[:, 4:6, :], pso[:, 0:2, :], mx[:, 4:6, :], ALU.mult).then_inc(sm["mix_b"], 1)
                V.scalar_tensor_tensor(out=mx[:, 6:8, :], in0=pso[:, 2:4, :], scalar=lamt[:, 4:5],
                                       in1=mx[:, 6:8, :], op0=ALU.mult, op1=ALU.mult).then_inc(sm["mix_b"], 1)

            row_max(0)
            for n in range(len(UNITS)):
                combine(n)
                if n + 1 < len(UNITS):
                    row_max(n + 1)
                turned(n)
                out_part(n)
                if n % 8 == 7:
                    finish(n // 8)

            for t in range(NLAT):
                dve.wait_ge(sm["y_exp"], t + 1)
                if t >= 2:
                    dve.wait_ge(y_out[t % 2], 16 * (t // 2))
                if t == 0:
                    dve.wait_ge(sm["wt_mm"], 3 * len(UNITS))
                b = 2 * (t % 2)
                V.scalar_tensor_tensor(out=y_buf[:, t % 2, :].rearrange("p (a b) -> p a b", a=2),
                                       in0=ps[:, b:b + 2, :], scalar=yst[:, NLAT + t:NLAT + t + 1],
                                       in1=GP[:, :].rearrange("p (a b) -> p a b", a=2),
                                       op0=ALU.mult, op1=ALU.mult).then_inc(sm["y_scaled"], 1)

        @block.gpsimd
        def _(pool):
            G = nc.gpsimd
            pool.wait_ge(sm["ada_gate"], 1)
            for r in raw:
                G.memset(r[:, 0:2], 0.0).then_inc(sm["pad_done"], 1)
                G.memset(r[:, LAT + 2:LAT + 6], 0.0).then_inc(sm["pad_done"], 1)
                G.memset(r[:, RAW_W - 2:RAW_W], 0.0).then_inc(sm["pad_done"], 1)

            for i in range(NG + 3):
                t = i - 1
                if 1 <= t < NG:
                    q = GDN_TILES[t] == "q"
                    n = LAT if q else CV_W
                    pool.wait_ge(sm["exp_done"], t)
                    G.tensor_scalar(ebuf[:, 0:n], ebuf[:, 0:n], 1.0, None, ALU.add).then_inc(sm["add1"], 1)
                    pool.wait_ge(sm["rec"], t)
                    y = y_of(t)
                    if GDN_TILES[t] == "v" and t >= 2 and GDN_TILES[t - 2] == "v":
                        pool.wait_ge(sm["aux_mm"], max(j for j, a in enumerate(AUX) if a[1] == t - 2) + 1)
                    op = G.tensor_tensor(y[:, 0:LAT], cv[t % 2][:, 0:LAT], ebuf[:, 0:LAT], ALU.mult)
                    if not q:
                        op = G.tensor_tensor(y[:, LAT:TOK], cv[t % 2][:, CTX_CV:CTX_CV + CTX],
                                             ebuf[:, CTX_CV:CTX_CV + CTX], ALU.mult)
                    op.then_inc(sm["silu_done"], 1)
                    if GDN_TILES[t] in "qk":
                        n = ntok(GDN_TILES[t])
                        pool.wait_ge(sm["silu_done"], t)
                        need(pool, sm["fin_done"], QKI.index(t) - 1)
                        G.tensor_tensor(sqb[t % 2][:, 0:n], y[:, 0:n], y[:, 0:n], ALU.mult).then_inc(sm["sq_done"], 1)
                t = i - 2
                if t in QKI:
                    n = ntok(GDN_TILES[t])
                    y = y_of(t)
                    pool.wait_ge(sm["rn_done"], QKI.index(t) + 1)
                    G.tensor_tensor(y[:, 0:n], y[:, 0:n], sqb[t % 2][:, 0:n], ALU.mult).then_inc(sm["fin_done"], 1)

            for pair in range(NT // 2):
                for s in range(2):
                    c = 2 * pair + s
                    if pair == 0:
                        pool.wait_ge(sm["gt_d"], 10)
                        pool.wait_ge(sm["in_mm"], NG)
                        pool.wait_ge(sm["spill"], 16)
                        pool.wait_ge(sm["spill_kr"], 16)
                    if pair > 0:
                        pool.wait_ge(sm["upd"], 2 * (((pair - 1) * 6 + 5) * 2 + s + 1))
                    G.tensor_tensor(iv[s]["gbc"], ones.unsqueeze(1).broadcast_to([P, 8, P]),
                                    g_[:, c, :].unsqueeze(2).broadcast_to([P, 8, P]), ALU.mult
                                    ).then_inc(sm["gbc_done"], 1)
                for s in range(2):
                    c = 2 * pair + s
                    b = iv[s]
                    pool.wait_ge(sm["e_done"], c + 1)
                    G.tensor_tensor(b["tmp"], b["E"][:, 0:4, :], per_head(beta[:, c, 0:4]), ALU.mult
                                    ).then_inc(sm["pool_w"], 1)
                    G.tensor_tensor(b["At"], b["E"][:, 4:8, :], per_head(beta[:, c, 4:8]), ALU.mult
                                    ).then_inc(sm["pool_w"], 1)
                    pool.wait_ge(sm["pool_w"], 3 * c + 2)
                    G.tensor_tensor(b["At"], b["At"], b["tmp"], ALU.add).then_inc(sm["pool_w"], 1)
                for s in range(2):
                    c = 2 * pair + s
                    b = iv[s]
                    Qc = Q_all[:, c, :].rearrange("p (h n) -> p h n", n=P)
                    pool.wait_ge(sm["at_done"], c + 1)
                    G.tensor_tensor(Qc, b["At"], heads(cst("sib1")), ALU.mult).then_inc(sm["pool_q"], 1)
                    pool.wait_ge(sm["pool_q"], 2 * c + 1)
                    G.tensor_tensor(Qc, heads(ident), Qc, ALU.subtract).then_inc(sm["pool_q"], 1)
                for lev in range(6):
                    for s in range(2):
                        c = 2 * pair + s
                        n = (pair * 6 + lev) * 2 + s
                        b = iv[s]
                        mask = heads(cst(f"alt{LEVELS[lev + 1]}"))
                        Qc = Q_all[:, c, :].rearrange("p (h n) -> p h n", n=P)
                        if lev == 0:
                            pool.wait_ge(sm["p_done"], c + 1)
                        else:
                            pool.wait_ge(sm["upd"], 2 * (n - 2) + 2)
                        G.tensor_tensor(b["M"], b["P"], mask, ALU.mult).then_inc(sm["mn_done"], 1)
                        G.tensor_tensor(b["N"], Qc, mask, ALU.mult).then_inc(sm["mn_done"], 1)

            pool.wait_ge(sm["upd"], 2 * 60)
            G.memset(view(20, 4 * 256), 0.0).then_inc(sm["s_init"], 1)
            G.memset(view(148, 16 * 256), 0.0).then_inc(sm["s_init"], 1)
            pool.wait_ge(sm["s_init"], 2)

            def h3(ap):
                return ap.rearrange("p (h n) -> p h n", n=P)
            for i in range(NT + 1):
                for d in range(2):
                    m = 2 * i + d
                    if i < NT:
                        c = order[d][i]
                        need(pool, sm["tr4_mm"], m - 1)
                        G.tensor_tensor(h3(Um[:, d, :]), h3(Q_all[:, c, :]), heads(cst("triu" if d == 0 else "tril")),
                                        ALU.mult).then_inc(sm["um_done"], 1)
                        need(pool, sm["s_upd"], m - 1)
                        G.tensor_tensor(h3(Sg[:, d, :]), h3(S[:, d, :]), per_head(GL[:, c, 4 * d:4 * d + 4]),
                                        ALU.mult).then_inc(sm["sg_done"], 1)
                    if m - 2 in LATSTEP:
                        li = LATSTEP.index(m - 2)
                        c = order[d][i - 1]
                        pool.wait_ge(sm["o1_done"], li + 1)
                        need(pool, sm["oa_done"], li)
                        G.tensor_tensor(o_acc[:, c, :], o_acc[:, c, :], t2[:, d, :], ALU.add
                                        ).then_inc(sm["oa_done"], 1)
            pool.wait_ge(sm["oa_done"], 16)
            pool.wait_ge(sm["tr4_mm"], 20)
            oa = view(148, NLAT * H, P)
            G.tensor_tensor(o_sq, oa, oa, ALU.mult).then_inc(sm["osq_done"], 1)

            for j, kind in enumerate(REST_TILES + [""]):
                if j in ZT:
                    z = ZT.index(j)
                    pool.wait_ge(sm["z_exp"], z + 1)
                    G.tensor_scalar(zexp[:, z % 2, :], zexp[:, z % 2, :], 1.0, None, ALU.add
                                    ).then_inc(sm["z_add"], 1)
                if j - 1 in ROPED:
                    t = j - 1
                    kind = REST_TILES[t]
                    r = ROPED.index(t)
                    a = max(q for q, e in enumerate(AUX2) if e[1] == t)
                    dst = (dq if kind == "dq" else dk)[:, t - first_of[kind], 0:LAT]
                    pool.wait_ge(sm["aux2_mm"], a + 1)
                    pool.wait_ge(sm["rope_in"], 16)
                    G.tensor_tensor(dst, dst, rope[:, 0, :], ALU.mult).then_inc(sm["rope_done"], 1)
                    pool.wait_ge(sm["rope_done"], 2 * r + 1)
                    pool.wait_ge(sm["aux2_read"], a + 1)
                    G.tensor_tensor(dst, dst, rbuf, ALU.add).then_inc(sm["rope_done"], 1)
            pool.wait_ge(sm["z_done"], len(ZT))
            pool.wait_ge(sm["aux2_read"], len(AUX2))
            pool.wait_ge(sm["c_evac"], len(CT))
            for k in range(2):
                G.tensor_tensor(cq_sq[:, k, :], cq[:, k, :], cq[:, k, :], ALU.mult).then_inc(sm["n_sq"], 1)
            G.tensor_tensor(kv_sq, ckv, ckv, ALU.mult).then_inc(sm["n_sq"], 1)

            for t in range(NLAT):
                pool.wait_ge(sm["y_scaled"], t + 1)
                pool.wait_ge(x2_in[t % 2], 16 * (t // 2 + 1))
                G.tensor_tensor(y_buf[:, t % 2, :], y_buf[:, t % 2, :], x_buf[:, t % 2, :], ALU.add
                                ).then_inc(sm["y_added"], 1)


def constants():
    i = np.arange(P)
    r, c = i[:, None], i[None, :]
    m = {"ident": r == c, "triu": r <= c, "tril": r >= c, "ones": np.ones((P, P)),
         "swap": (r // 32 == c // 32) & ((r + 16) % 32 == c % 32),
         "neg_f": np.where(r <= c, 0.0, NEG), "neg_b": np.where(r >= c, 0.0, NEG)}
    for b in LEVELS:
        m[f"sib{b}"] = (r // (2 * b) == c // (2 * b)) & (r // b != c // b)
        even = (r // b) % 2 == 0
        m[f"alt{b}"] = (r // b == c // b) & np.where(even, r >= c, r <= c)
    const = np.ascontiguousarray(np.stack([np.asarray(m[n], np.float32) for n in CONSTS], axis=1))
    t = np.arange(LAT)
    half = MLA_ROPE // 2
    inv = 1.0 / (ROPE_BASE ** (np.arange(0, half, 2, dtype=np.float32) / half))
    ang = np.concatenate([(t // GRID_W)[:, None].astype(np.float32) * inv,
                          (t % GRID_W)[:, None].astype(np.float32) * inv], axis=1).astype(np.float32)
    cos, sin = np.cos(ang).T, np.sin(ang).T
    rope = np.stack([np.tile(np.concatenate([cos, cos]), (4, 1)), np.tile(np.concatenate([-sin, sin]), (4, 1))],
                    axis=1)
    return const, np.ascontiguousarray(rope, dtype=np.float32)


def column_order():
    gdn = 4 * QK_COLS + 16
    mla = Q_RANK + KV_RANK + MLA_ROPE + H * MLA_V
    a, b = gdn, gdn + mla
    misc = np.full(P, -1)
    misc[0:16] = np.arange(4 * QK_COLS, gdn)
    misc[KR0:KR0 + MLA_ROPE] = a + Q_RANK + KV_RANK + np.arange(MLA_ROPE)
    qkv = np.arange(3 * QK_COLS)
    za = 3 * QK_COLS + np.arange(QK_COLS)
    return np.concatenate([misc, qkv, za, a + np.arange(Q_RANK + KV_RANK),
                           a + Q_RANK + KV_RANK + MLA_ROPE + np.arange(H * MLA_V), b + np.arange(1024)])


def kernel(x, c, ctx, c_ctx, ada_w, ada_b, pre_gain, post_gain, w_in, gdn_conv, gdn_a_log, gdn_dt_bias,
           gdn_out_gain, mla_q_gain, mla_w_uq, mla_kv_gain, mla_w_ukv, diff_lambda, diff_sub_gain, w_out):
    import concourse.bacc as _bacc
    from concourse.bass_utils import run_bass_kernel_spmd as _run

    f = lambda a: np.asarray(a)
    tiles = lambda v: f(v).reshape(-1, P).T
    spread = lambda v: np.broadcast_to(f(v).reshape(1, -1), (P, f(v).size))
    const, rope = constants()
    conv = f(gdn_conv)[0].T.reshape(3 * H, P, CONV_W).transpose(1, 0, 2).reshape(P, -1)
    cols = np.concatenate([
        np.stack([tiles(c), tiles(c_ctx)], axis=2).reshape(P, -1), tiles(ada_b[0]), tiles(pre_gain[0]),
        tiles(post_gain[0]), conv, tiles(gdn_out_gain[0]), tiles(mla_q_gain[0]), tiles(mla_kv_gain[0]),
        np.tile(f(diff_sub_gain)[0], 2).reshape(P, 1), spread(gdn_a_log[0]), spread(gdn_dt_bias[0]),
        spread(diff_lambda[0])], axis=1)
    order = column_order()
    wi = np.zeros((D, len(order)), f(w_in).dtype)
    wi[:, order >= 0] = f(w_in)[0][:, order[order >= 0]]
    arrays = {
        "x": f(x)[0], "ctx": f(ctx)[0], "cols": cols, "const": const, "rope": rope,
        "ada_w": f(ada_w)[0].reshape(KD, P, 3, D).transpose(2, 1, 0, 3),
        "w_in": wi.reshape(KD, P, len(TILES), P).transpose(2, 1, 0, 3),
        "w_uq": f(mla_w_uq)[0].reshape(2, P, -1).transpose(1, 0, 2), "w_ukv": f(mla_w_ukv)[0],
        "w_out": f(w_out)[0].reshape(KD, P, D),
    }
    nc = _bacc.Bacc("TRN2", target_bir_lowering=False, num_devices=1)
    args, feeds = [], {}
    for name, a in arrays.items():
        a = np.ascontiguousarray(a)
        feeds[f"in_{name}"] = a
        args.append(nc.dram_tensor(f"in_{name}", a.shape, mybir.dt.from_np(a.dtype), kind="ExternalInput").ap())
    out = nc.dram_tensor("out_0", (LAT, D), F32, kind="ExternalOutput").ap()
    hybrid_block(nc, *args, out)
    r = _run(nc, [feeds], core_ids=[0])
    return r.results[0]["out_0"].reshape(1, LAT, D)
```

```python
import math
from contextlib import ExitStack

import numpy as np

import concourse.bass as bass
from concourse import mybir

F32 = mybir.dt.float32
ALU = mybir.AluOpType
ACT = mybir.ActivationFunctionType
AX = mybir.AxisListType

P = 128
D = 1024
KD = D // P
LAT, CTX = 1024, 256
TOK = LAT + CTX
NT = TOK // P
NLAT = LAT // P
SEG = 512
H = 4
DK = 128
QK_COLS = H * DK
CONV_W = 5
EPS = 1e-6
GRID_W = 64
ROPE_BASE = 10000.0
MLA_NOPE, MLA_ROPE, MLA_V = 64, 32, 64
MLA_QK = MLA_NOPE + MLA_ROPE
MLA_SCALE = MLA_QK ** -0.5
Q_RANK, KV_RANK = 256, 128
DIFF_QK, DIFF_V = 32, 64
DIFF_SCALE = DIFF_QK ** -0.5
LAM_INIT = 0.8 - 0.6 * math.exp(0.0)
NEG = -1e30

GDN_TILES = ["misc"] + ["k"] * H + ["q"] * H + ["v"] * H
REST_TILES = ["za"] * 4 + ["cq"] * 2 + ["ckv"] + ["zb"] * 2 + ["dq"] * 2 + ["dk"] * 2 + ["dv"] * 2 + ["dz"] * 2
TILES = GDN_TILES + REST_TILES
LAT_ONLY = {"q", "za", "cq", "zb", "dq", "dz"}
W_RING = 3

GATES_AT = 7
KR0 = 64
LEVELS = [1 << i for i in range(7)]

COLS = {}
_at = 0
for _n, _c in (("c", 16), ("ada_b", 24), ("pre", 8), ("post", 8), ("conv", 60), ("og", 1), ("qg", 2),
               ("kvg", 1), ("sg", 1), ("alog", 8), ("dt", 8), ("lam", 128), ("quad", 4)):
    COLS[_n] = (_at, _c)
    _at += _c
NCOLS = _at
CONSTS = ["ident", "triu", "tril", "ones", "swap", "neg_f", "neg_b"] + [f"sib{b}" for b in LEVELS] + \
    [f"alt{b}" for b in LEVELS[1:]]


def segments(n):
    return [(s, min(SEG, n - s)) for s in range(0, n, SEG)]


def hybrid_block(nc, x, ctx_in, cols_d, const_d, rope_d, ada_w, w_in, w_uq, w_ukv, w_out, out):
    es = ExitStack()
    with es:
        def sb(name, shape):
            return es.enter_context(nc.sbuf_tensor(name, shape, F32))

        def sem(name):
            return es.enter_context(nc.semaphore(name))

        def need(eng, s, n):
            if n > 0:
                eng.wait_ge(s, n)

        ps = es.enter_context(nc.psum_tensor("ps", [P, 8, SEG], F32))
        hT_spill = nc.dram_tensor("hT_spill", [P, KD * TOK], F32, kind="Internal").ap()
        kr_spill = nc.dram_tensor("kr_spill", [MLA_ROPE, TOK], F32, kind="Internal").ap()

        cols = sb("cols", [P, NCOLS])
        const = sb("const", [P, len(CONSTS), P])
        GP = sb("GP", [P, D])
        ARENA_KB = 184
        arena = sb("arena", [P, ARENA_KB * 256])

        def view(kb, *shape):
            n = int(np.prod(shape))
            lo = int(kb * 256)
            assert lo + n <= ARENA_KB * 256
            v = arena[:, lo:lo + n]
            if len(shape) == 2:
                v = v.rearrange("p (a b) -> p a b", b=shape[1])
            if len(shape) == 3:
                v = v.rearrange("p (a b c) -> p a b c", b=shape[1], c=shape[2])
            return v

        def col(name, i=0, n=1):
            return cols[:, COLS[name][0] + i:COLS[name][0] + i + n]

        def cst(name):
            return const[:, CONSTS.index(name), :]

        def heads(ap):
            return ap.unsqueeze(1).broadcast_to([P, H, P])

        def per_head(ap):
            return ap.unsqueeze(2).broadcast_to([P, H, P])

        ident, ones = cst("ident"), cst("ones")
        small = sb("small", [P, 16 + 16 + 48 + 16 + 8 + 2 * NT + 6])
        _o = [0]

        def take(n):
            _o[0] += n
            return small[:, _o[0] - n:_o[0]]
        cs = take(16)
        cs_e = take(16)
        mod = take(48)
        mA = take(16)
        gp_col = take(8)
        ssq = take(NT)
        rstd = take(NT)
        eps_col = take(1)
        one_col = take(1)
        eps_q = take(1)
        eps_k = take(1)
        og_half = take(1)

        hT = view(0, KD, TOK)
        ada = [view(40 + 32 * i, KD, D) for i in range(3)]
        xin = view(136, 4, D)
        junk = view(152, D)
        gp_diag = view(156, KD, P)
        mod_row = view(160, D)
        w_ring = view(172, W_RING, KD, P)

        kT = view(40, H, TOK)
        qT = view(60, H, LAT)
        k_tok = view(76, NT, H * P)
        v_tok = view(96, NT, H * P)
        W0 = 116 * 256
        RAW_W, CV_W = LAT + CTX + 8, LAT + CTX + 4
        CTX_RAW, CTX_CV = LAT + 6, LAT + 4

        def words(off, n):
            return arena[:, W0 + off:W0 + off + n]
        raw = [words(i * RAW_W, RAW_W) for i in range(2)]
        cv = [words(2 * RAW_W + i * CV_W, CV_W) for i in range(2)]
        ebuf = words(2 * RAW_W + 2 * CV_W, CV_W)
        sqb = [words(2 * RAW_W + 3 * CV_W + i * TOK, TOK) for i in range(2)]
        yv = [words(2 * RAW_W + 3 * CV_W + (2 + i) * TOK, TOK) for i in range(2)]
        misc = view(162, TOK)

        gates = sb("gates", [P, 16 * NT + 13 * 8 * NT])
        lg = gates[:, 0:16 * NT].rearrange("p (c n) -> p c n", n=16)

        def gate(i):
            lo = 16 * NT + i * 8 * NT
            return gates[:, lo:lo + 8 * NT].rearrange("p (c n) -> p c n", n=8)
        xa, na, en, sp, g_, beta, gam, tot, dtk, EG, EKD, GL, bek = [gate(i) for i in range(13)]
        ea = sb("ea", [P, 8])

        Q_all = view(0, NT, H * P)
        QK = view(116, 2 * NLAT, H * P)
        INVERSES = [[0, 1, 2, 3], [4, 5, 6, 7], [8, 9]]

        def inv_buf(b):
            return {"gbc": view(b, 8, P), "M": view(b, H, P), "N": view(b + 2, H, P), "tmp": view(b, H, P),
                    "At": view(b + 4, H, P), "E": view(b + 6, 8, P), "P": view(b + 6, H, P), "X": view(b + 8, H, P)}
        iv = [inv_buf(b) for b in (20, 30, 148, 158)]

        def inv_index(g, lev, s):
            return 6 * sum(len(q) for q in INVERSES[:g]) + lev * len(INVERSES[g]) + s
        S = view(20, 2, H * P)
        Sg = view(24, 2, H * P)
        R = view(28, 2, H * P)
        Vn = view(32, 2, H * P)
        Vs = view(36, 2, H * P)
        t2 = view(164, 2, H * P)
        Um = view(168, 2, H * P)
        o_acc = view(148, NLAT, H * P)
        o_sq = view(0, NLAT * H, P)
        o_stat = sb("o_stat", [P, 2 * NLAT * H])

        mixT = view(40, 8, LAT)
        cq = view(72, 2, LAT)
        ckv = view(80, TOK)
        krT = view(85, TOK)
        dq = view(90, 2, LAT)
        dk = view(98, 2, TOK)
        dv_tok = view(108, NT, H * DIFF_V)
        zexp = view(118, 2, LAT)
        zbuf = view(126, 2, LAT)
        dvT = view(134, TOK)
        rbuf = view(139, LAT)
        uq_sb = view(143, 2, H * MLA_QK)
        ukv_sb = view(146, H * P)
        rope = view(164, 2, LAT)
        QTm = view(0, H, LAT)
        KTm = view(16, H, TOK)
        V_tok = view(148, NT, H * MLA_V)
        cq_sq = view(118, 2, LAT)
        kv_sq = view(126, TOK)
        cq_rn = view(131, LAT)
        kv_rn = view(135, TOK)

        prob = view(118, 4, TOK)
        wT = view(138, 2, TOK)
        o_tok = view(158, 2, 2 * H * 64)
        d_sq = view(162, H, 64)
        dqz = [view(36, 2 * H, P), view(85, 2 * H, P)]
        NSET = NLAT * 3 * H
        stat = sb("stat", [P, 2 * NSET + 4 * NLAT * 2 * H + 2 * NLAT * H + 16])
        nmax = stat[:, 0:NSET]
        lsum = stat[:, NSET:2 * NSET]
        _s = 2 * NSET
        rinv = stat[:, _s:_s + NLAT * 8]
        rinv1 = stat[:, _s + NLAT * 8:_s + NLAT * 16]
        coef = stat[:, _s + NLAT * 16:_s + NLAT * 24]
        dss = stat[:, _s + NLAT * 24:_s + NLAT * 28]
        drs = stat[:, _s + NLAT * 28:_s + NLAT * 32]
        lamt = stat[:, _s + NLAT * 32:_s + NLAT * 32 + 8]
        lam_p = sb("lam_p", [P, 64])

        wo_sb = [view(164 + 4 * k, D) if k < 5 else view(72 + 4 * (k - 5), D) for k in range(KD)]
        y_buf = view(118, 2, D)
        x_buf = view(126, 2, D)
        y_junk = view(134, D)
        yst = sb("yst", [P, 2 * NLAT])

        names = """cols_in const_in rope_in uq_in x_in0 x_in1 x_in2 x_in3 ada_in0 ada_in1 ada_in2 w_in0 w_in1 w_in2
        setup c_exp c_one c_rec c_silu ada_mm row_read mod_turn mod_add mod_A gp_done ssq_done rs_done xn_done xT_mm hT_dve hT_act
        diag_done gp_mm GP_done in_mm evac_done conv_step exp_done silu_done sq_done aux_mm aux_read rn_done
        fin_done pad_done misc_out spill spill_kr gt_d gt_a
        gbc_done gb_mm pre_mm ex_done e_done pool_w at_done qk_done q_step tr_mm p_done mn_done x_mm xs_done pq_mm upd
        s_init um_done sg_done ks_mm qs_mm r_done tr4_mm vv_done ds_mm qkv_mm s_upd t2_done o1_done oa_done
        osq_done ostat_d ostat_a o_ready hT_back kr_back in2_mm z_exp z_done c_evac aux2_mm aux2_read
        raw_cos rope_t rope_done lam_d lam_a
        n_sq n_mm n_ln n_exp n_done mq_mm mq_ev mq_swap mq_t mq_c mq_done mk_mm mk_ev mk_rope mv_mm mv_ev kr_mm kr_t kr_c kr_done
        qz_done sc_mm mx_done p_exp l_inv w_done wt_mm wt_ev_a wt_ev_d pv_mm pv_ev d_sqd d_red d_ln d_exp d_norm ot_mm mix_b
        wo_in y_mm y_sq y_ln y_exp y_scaled x2_in0 x2_in1 y_out0 y_out1 y_added""".split()
        sm = {n: sem(n) for n in names}
        x_in = [sm[f"x_in{i}"] for i in range(4)]
        ada_in = [sm[f"ada_in{i}"] for i in range(3)]
        w_in_s = [sm[f"w_in{i}"] for i in range(W_RING)]
        x2_in = [sm["x2_in0"], sm["x2_in1"]]
        y_out = [sm["y_out0"], sm["y_out1"]]

        xv = x.rearrange("(t p) d -> t p d", p=P)
        cv_d = ctx_in.rearrange("(t p) d -> t p d", p=P)
        out_v = out.rearrange("(t p) d -> t p d", p=P)

        NG = len(GDN_TILES)
        GROUPS = [(0, 4), (4, 4), (8, 2)]

        def ntok(kind):
            return LAT if kind in LAT_ONLY else TOK

        def aux_jobs():
            jobs = []
            for i in range(NG + 3):
                if 0 <= i - 2 < NG and GDN_TILES[i - 2] in "qk":
                    for s, w in segments(ntok(GDN_TILES[i - 2])):
                        jobs.append(("ones", i - 2, s, w, i))
                if i == GATES_AT:
                    jobs.append(("gates", -9, 0, 0, i))
                t = i - 3
                if 0 <= t < NG and GDN_TILES[t] == "misc":
                    jobs.append(("logits", t, 0, TOK, i))
                if 0 <= t < NG and GDN_TILES[t] in "kv":
                    for s, w in segments(TOK):
                        jobs.append(("turn", t, s, w, i))
            return jobs
        AUX = aux_jobs()

        def aux_at(i, what):
            return [(j, a) for j, a in enumerate(AUX) if a[4] == i and a[0] in what]

        def head_of(t):
            return (t - 1) % H

        def y_of(t):
            kind = GDN_TILES[t]
            return {"q": lambda: qT[:, head_of(t), :], "k": lambda: kT[:, head_of(t), :],
                    "v": lambda: yv[t % 2]}[kind]()

        QKI = [t for t in range(NG) if GDN_TILES[t] in "qk"]
        AUX2 = []
        for j in range(len(REST_TILES) + 1):
            if j >= 1:
                kind = REST_TILES[j - 1]
                if kind in ("za", "dq", "dk"):
                    for s, w in segments(LAT):
                        AUX2.append((kind, j - 1, s, w, j))
                if kind == "dv":
                    for s, w in segments(TOK):
                        AUX2.append((kind, j - 1, s, w, j))
        first_of = {k: REST_TILES.index(k) for k in set(REST_TILES)}
        ROPED = [j for j, k in enumerate(REST_TILES) if k in ("dq", "dk")]
        ZT = [j for j, k in enumerate(REST_TILES) if k[0] == "z" or k == "dz"]
        CT = [j for j, k in enumerate(REST_TILES) if j not in ZT]

        order = [[8, 9] + list(range(8)), [9, 8] + list(range(7, -1, -1))]
        LATSTEP = [[m for m in range(20) if order[m % 2][m // 2] < NLAT]][0]

        UNITS = [(qb, u) for qb in range(NLAT) for i in range(H) for u in (i, H + i)]

        def sets_of(n):
            qb, u = UNITS[n]
            st = 3 * (qb * H + u % H)
            return [st] if u < H else [st + 1, st + 2]
        KSEG = segments(TOK)

        block = es.enter_context(nc.Block())

        @block.sync
        def _(sp):
            sp.dma_start(cols[:, :], cols_d).then_inc(sm["cols_in"], 16)
            sp.dma_start(ada[0], ada_w[0]).then_inc(ada_in[0], 16)
            for t in range(4):
                sp.dma_start(xin[:, t, :], xv[t]).then_inc(x_in[t], 16)
            sp.dma_start(const[:, :, :], const_d).then_inc(sm["const_in"], 16)
            sp.dma_start(ada[1], ada_w[1]).then_inc(ada_in[1], 16)
            for t in range(4, NT):
                sp.wait_ge(sm["xT_mm"], 8 * (t // 4))
                src = xv[t] if t < NLAT else cv_d[t - NLAT]
                sp.dma_start(xin[:, t % 4, :], src).then_inc(x_in[t % 4], 16)
                if t == 4:
                    sp.dma_start(w_ring[:, 0, :, :], w_in[0]).then_inc(w_in_s[0], 16)
                    sp.dma_start(ada[2], ada_w[2]).then_inc(ada_in[2], 16)
            for i in range(1, W_RING):
                sp.dma_start(w_ring[:, i, :, :], w_in[i]).then_inc(w_in_s[i], 16)
            for i in range(W_RING, NG):
                sp.wait_ge(sm["in_mm"], i - W_RING + 1)
                sp.dma_start(w_ring[:, i % W_RING, :, :], w_in[i]).then_inc(w_in_s[i % W_RING], 16)
            sp.wait_ge(sm["hT_dve"], 12)
            sp.wait_ge(sm["hT_act"], 12)
            sp.dma_start(hT_spill, arena[:, 0:KD * TOK]).then_inc(sm["spill"], 16)
            sp.wait_ge(sm["evac_done"], 1)
            sp.dma_start(kr_spill, misc[KR0:KR0 + MLA_ROPE, :]).then_inc(sm["spill_kr"], 16)
            for i in range(NG, NG + W_RING):
                sp.wait_ge(sm["in_mm"], min(i - W_RING + 1, NG))
                sp.dma_start(w_ring[:, i % W_RING, :, :], w_in[i]).then_inc(w_in_s[i % W_RING], 16)
            sp.wait_ge(sm["spill"], 16)
            sp.wait_ge(sm["spill_kr"], 16)
            sp.wait_ge(sm["ostat_d"], 1)
            sp.wait_ge(sm["s_upd"], 20)
            sp.wait_ge(sm["o1_done"], 16)
            sp.wait_ge(sm["oa_done"], 16)
            sp.dma_start(arena[:, 0:KD * TOK], hT_spill).then_inc(sm["hT_back"], 16)
            sp.dma_start(rope, rope_d).then_inc(sm["rope_in"], 16)
            sp.dma_start(krT[KR0:KR0 + MLA_ROPE, :], kr_spill).then_inc(sm["kr_back"], 16)
            sp.dma_start(uq_sb, w_uq).then_inc(sm["uq_in"], 16)
            sp.dma_start(ukv_sb, w_ukv).then_inc(sm["uq_in"], 16)
            for i in range(NG + W_RING, len(TILES)):
                sp.wait_ge(sm["in2_mm"], i - W_RING + 1 - NG)
                sp.dma_start(w_ring[:, i % W_RING, :, :], w_in[i]).then_inc(w_in_s[i % W_RING], 16)
            sp.wait_ge(sm["mq_done"], H)
            sp.wait_ge(sm["kr_done"], 1)
            sp.wait_ge(sm["mv_mm"], 5)
            sp.wait_ge(sm["mk_mm"], H)
            for k in range(KD):
                sp.dma_start(wo_sb[k], w_out[k]).then_inc(sm["wo_in"], 16)
            for t in range(NLAT):
                if t == 0:
                    sp.wait_ge(sm["wt_mm"], 3 * len(UNITS))
                if t >= 2:
                    sp.wait_ge(sm["y_added"], t - 1)
                sp.dma_start(x_buf[:, t % 2, :], xv[t]).then_inc(x2_in[t % 2], 16)
                if t >= 1:
                    sp.wait_ge(sm["y_added"], t)
                    sp.dma_start(out_v[t - 1], y_buf[:, (t - 1) % 2, :]).then_inc(y_out[(t - 1) % 2], 16)
            sp.wait_ge(sm["y_added"], NLAT)
            sp.dma_start(out_v[NLAT - 1], y_buf[:, (NLAT - 1) % 2, :]).then_inc(y_out[(NLAT - 1) % 2], 16)
            sp.wait_ge(y_out[0], 16 * (NLAT // 2))
            sp.wait_ge(y_out[1], 16 * (NLAT // 2))

        def wait_aux(pe, j):
            strict = "gates" in (AUX[j][0], AUX[j - 1][0], AUX[j - 2][0])
            need(pe, sm["aux_read"], j if strict else j - 1)

        def turn_x(pe, gi):
            t0, n = GROUPS[gi]
            for k in range(KD):
                q = gi * KD + k
                if k == 0:
                    pe.wait_ge(sm["const_in"], 16)
                    pe.wait_ge(sm["xn_done"], t0 + n)
                if q >= 4:
                    pe.wait_ge(sm["hT_dve"] if q % 2 == 0 else sm["hT_act"], (q - 4) // 2 + 1)
                for t in range(n):
                    last = nc.tensor.transpose(ps[:, 4 + q % 4, t * P:(t + 1) * P],
                                               xin[:, (t0 + t) % 4, k * P:(k + 1) * P], ident)
                last.then_inc(sm["xT_mm"], 1)

        def project(pe, i, n, free_sem, free_n, done, parity=None):
            parity = i % 2 if parity is None else parity
            pe.wait_ge(w_in_s[i % W_RING], 16 * (i // W_RING + 1))
            if free_sem is not None:
                need(pe, free_sem, free_n)
            for s, w in segments(n):
                for k in range(KD):
                    last = nc.tensor.matmul(ps[:, 3 * parity + s // SEG, 0:w], w_ring[:, i % W_RING, k, :],
                                            hT[:, k, s:s + w], start=(k == 0), stop=(k == KD - 1))
            last.then_inc(done, 1)

        def swap_q(pe, h):
            pe.wait_ge(sm["mq_ev"], h + 1)
            if h == 0:
                pe.wait_ge(sm["kr_t"], 1)
            need(pe, sm["mq_t"], h)
            for s, w in segments(LAT):
                last = nc.tensor.matmul(ps[KR0:KR0 + 32, 6 + s // SEG, 0:w],
                                        cst("swap")[KR0:KR0 + 32, KR0:KR0 + 32],
                                        QTm[KR0:KR0 + 32, h, s:s + w], start=True, stop=True)
            last.then_inc(sm["mq_swap"], 1)

        @block.tensor
        def _(pe):
            mm, tr = nc.tensor.matmul, nc.tensor.transpose

            pe.wait_ge(sm["c_silu"], 1)

            def modulate(piece):
                pe.wait_ge(ada_in[piece], 16)
                if piece == 2:
                    pe.wait_ge(sm["row_read"], 2)
                for i in range(2):
                    for k in range(KD):
                        last = mm(ps[0:2, i, :], cs[:, 2 * k:2 * k + 2], ada[piece][:, k, i * SEG:(i + 1) * SEG],
                                  start=(k == 0), stop=(k == KD - 1))
                last.then_inc(sm["ada_mm"], 1)

            def turn_mod(piece):
                if piece == 0:
                    pe.wait_ge(sm["const_in"], 16)
                pe.wait_ge(sm["row_read"], piece + 1)
                need(pe, sm["mod_add"], piece)
                for j in range(KD):
                    last = tr(ps[:, 2, 2 * j:2 * j + 2], mod_row[0:2, j * P:(j + 1) * P], ident[0:2, 0:2])
                last.then_inc(sm["mod_turn"], 1)

            modulate(0)
            turn_mod(0)
            pe.wait_ge(sm["row_read"], 1)
            modulate(1)
            turn_mod(1)
            for gi in range(3):
                turn_x(pe, gi)
            modulate(2)
            turn_mod(2)
            pe.wait_ge(sm["diag_done"], 1)
            for i in range(2):
                last = mm(ps[:, i, :], ones, gp_diag[:, 4 * i:4 * i + 4, :], start=True, stop=True)
            last.then_inc(sm["gp_mm"], 1)

            for i in range(NG + 3):
                if i < NG:
                    if i == 0:
                        pe.wait_ge(sm["hT_dve"], 12)
                        pe.wait_ge(sm["hT_act"], 12)
                        pe.wait_ge(sm["GP_done"], 1)
                    project(pe, i, ntok(GDN_TILES[i]), sm["evac_done"], i - 1, sm["in_mm"])
                for j, (_, t, s, w, _) in aux_at(i, ("ones",)):
                    if s == 0:
                        pe.wait_ge(sm["sq_done"], QKI.index(t) + 1)
                    wait_aux(pe, j)
                    mm(ps[:, 6 + j % 2, 0:w], ones, sqb[t % 2][:, s:s + w], start=True,
                       stop=True).then_inc(sm["aux_mm"], 1)
                for j, (what, t, s, w, _) in aux_at(i, ("gates", "turn", "logits")):
                    wait_aux(pe, j)
                    bank = 6 + j % 2
                    if what == "gates":
                        pe.wait_ge(sm["gt_d"], 4)
                        g8 = ps[:, bank, 0:8 * NT].rearrange("p (c n) -> p c n", n=8)
                        mm(g8[:, :, 0:4], cst("triu"), g_[:, :, 0:4], start=True, stop=True)
                        mm(g8[:, :, 4:8], cst("tril"), g_[:, :, 4:8], start=True, stop=True)
                        last = mm(ps[:, bank, 128:128 + 8 * NT].rearrange("p (c n) -> p c n", n=8), ones, g_,
                                  start=True, stop=True)
                    elif what == "logits":
                        for c in range(NT):
                            last = tr(ps[:, bank, 16 * c:16 * c + 16], misc[0:16, c * P:(c + 1) * P],
                                      ident[0:16, 0:16])
                    else:
                        if s == 0 and GDN_TILES[t] == "k":
                            pe.wait_ge(sm["fin_done"], QKI.index(t) + 1)
                        if s == 0:
                            pe.wait_ge(sm["silu_done"], t)
                        src = y_of(t)
                        for c in range(w // P):
                            last = tr(ps[:, bank, c * P:(c + 1) * P], src[:, s + c * P:s + (c + 1) * P], ident)
                    last.then_inc(sm["aux_mm"], 1)

            for g, group in enumerate(INVERSES):
                for s, c in enumerate(group):
                    pe.wait_ge(sm["gbc_done"], c + 1)
                    if g == 0:
                        pe.wait_ge(sm["aux_read"], len(AUX))
                        pe.wait_ge(sm["evac_done"], NG)
                    for d in range(2):
                        for h in range(H):
                            last = mm(ps[:, 2 * s + d, h * P:(h + 1) * P], iv[s]["gbc"][:, 4 * d + h, :],
                                      cst("triu") if d == 0 else cst("tril"), start=True, stop=True)
                    last.then_inc(sm["gb_mm"], 1)
                for s, c in enumerate(group):
                    cc = slice(c * P, (c + 1) * P)
                    pe.wait_ge(sm["ex_done"], 8 * (c + 1))
                    for h in range(H):
                        last = mm(ps[:, 2 * s, h * P:(h + 1) * P], kT[:, h, cc], kT[:, h, cc], start=True, stop=True)
                    if c < NLAT:
                        for h in range(H):
                            last = mm(ps[:, 2 * s + 1, h * P:(h + 1) * P], kT[:, h, cc], qT[:, h, cc],
                                      start=True, stop=True)
                    last.then_inc(sm["pre_mm"], 1)
                for s, c in enumerate(group):
                    pe.wait_ge(sm["q_step"], 2 * (c + 1))
                    for h in range(H):
                        last = tr(ps[:, 2 * s, h * P:(h + 1) * P], Q_all[:, c, h * P:(h + 1) * P], ident)
                    last.then_inc(sm["tr_mm"], 1)
                for lev in range(6):
                    for s, c in enumerate(group):
                        n = inv_index(g, lev, s)
                        pe.wait_ge(sm["mn_done"], 2 * n + 1)
                        for h in range(H):
                            last = mm(ps[:, 2 * s, h * P:(h + 1) * P], iv[s]["At"][:, h, :], iv[s]["M"][:, h, :],
                                      start=True, stop=True)
                        last.then_inc(sm["x_mm"], 1)
                    for s, c in enumerate(group):
                        n = inv_index(g, lev, s)
                        pe.wait_ge(sm["xs_done"], n + 1)
                        pe.wait_ge(sm["mn_done"], 2 * n + 2)
                        if lev < 5:
                            for h in range(H):
                                last = mm(ps[:, 2 * s, h * P:(h + 1) * P], iv[s]["N"][:, h, :], iv[s]["X"][:, h, :],
                                          start=True, stop=True)
                            last.then_inc(sm["pq_mm"], 1)
                        if lev == 0:
                            pe.wait_ge(sm["qk_done"], 2 * min(c + 1, NLAT))
                        for h in range(H):
                            last = mm(ps[:, 2 * s + 1, h * P:(h + 1) * P], iv[s]["X"][:, h, :], iv[s]["N"][:, h, :],
                                      start=True, stop=True)
                        last.then_inc(sm["pq_mm"], 1 if lev < 5 else 2)

            pe.wait_ge(sm["upd"], 2 * 60)
            for i in range(NT):
                for d in range(2):
                    m = 2 * i + d
                    c = order[d][i]
                    cc = slice(c * P, (c + 1) * P)
                    if i == 0:
                        pe.wait_ge(sm["s_init"], 2)
                    need(pe, sm["s_upd"], m - 1)
                    lat_before = len([q for q in LATSTEP if q <= m - 2])
                    need(pe, sm["o1_done"], lat_before)
                    for h in range(H):
                        last = mm(ps[:, 4 * d, h * P:(h + 1) * P], kT[:, h, cc], S[:, d, h * P:(h + 1) * P],
                                  start=True, stop=True)
                    last.then_inc(sm["ks_mm"], 1)
                    if c < NLAT:
                        need(pe, sm["t2_done"], lat_before)
                        for h in range(H):
                            last = mm(ps[:, 4 * d + 3, h * P:(h + 1) * P], qT[:, h, cc], S[:, d, h * P:(h + 1) * P],
                                      start=True, stop=True)
                        last.then_inc(sm["qs_mm"], 1)
                for d in range(2):
                    m = 2 * i + d
                    pe.wait_ge(sm["r_done"], 2 * (m + 1))
                    pe.wait_ge(sm["um_done"], m + 1)
                    for h in range(H):
                        last = mm(ps[:, 4 * d + 1, h * P:(h + 1) * P], Um[:, d, h * P:(h + 1) * P],
                                  R[:, d, h * P:(h + 1) * P], start=True, stop=True)
                    last.then_inc(sm["tr4_mm"], 1)
                for d in range(2):
                    m = 2 * i + d
                    c = order[d][i]
                    pe.wait_ge(sm["vv_done"], 2 * (m + 1))
                    for h in range(H):
                        last = mm(ps[:, 4 * d + 2, h * P:(h + 1) * P], k_tok[:, c, h * P:(h + 1) * P],
                                  Vs[:, d, h * P:(h + 1) * P], start=True, stop=True)
                    last.then_inc(sm["ds_mm"], 1)
                    if c < NLAT:
                        for h in range(H):
                            last = mm(ps[:, 4 * d, h * P:(h + 1) * P], QK[:, d * NLAT + c, h * P:(h + 1) * P],
                                      Vn[:, d, h * P:(h + 1) * P], start=True, stop=True)
                        last.then_inc(sm["qkv_mm"], 1)

            NR = len(REST_TILES)
            for j in range(NR + 1):
                if j < NR:
                    if j == 0:
                        pe.wait_ge(sm["hT_back"], 16)
                        pe.wait_ge(sm["o1_done"], 16)
                    if j >= 2:
                        if j - 2 in ZT:
                            pe.wait_ge(sm["z_done"], ZT.index(j - 2) + 1)
                        else:
                            pe.wait_ge(sm["c_evac"], CT.index(j - 2) + 1)
                    project(pe, NG + j, ntok(REST_TILES[j]), None, 0, sm["in2_mm"], parity=j % 2)
                for a, (kind, t, s, w, jj) in enumerate(AUX2):
                    if jj != j:
                        continue
                    need(pe, sm["aux2_read"], a - 1)
                    bank = 6 + a % 2
                    if kind == "za":
                        pe.wait_ge(sm["o_ready"], 1)
                        h = t - first_of["za"]
                        for c in range(w // P):
                            cc = s // P + c
                            last = tr(ps[:, bank, c * P:(c + 1) * P], o_acc[:, cc, h * P:(h + 1) * P], ident)
                    else:
                        pe.wait_ge(sm["c_evac"], CT.index(t) + 1)
                        if kind == "dv":
                            for c in range(w // P):
                                last = tr(ps[:, bank, c * P:(c + 1) * P], dvT[:, s + c * P:s + (c + 1) * P], ident)
                        else:
                            src = (dq if kind == "dq" else dk)[:, t - first_of[kind], :]
                            last = mm(ps[:, bank, 0:w], cst("swap"), src[:, s:s + w], start=True, stop=True)
                    last.then_inc(sm["aux2_mm"], 1)

            pe.wait_ge(sm["n_sq"], 3)
            pe.wait_ge(sm["z_done"], len(ZT))
            pe.wait_ge(sm["c_evac"], len(CT))
            for s, w in segments(LAT):
                for k in range(2):
                    mm(ps[:, s // SEG, 0:w], ones, cq_sq[:, k, s:s + w], start=(k == 0), stop=(k == 1))
            for s, w in segments(TOK):
                last = mm(ps[:, 2 + s // SEG, 0:w], ones, kv_sq[:, s:s + w], start=True, stop=True)
            last.then_inc(sm["n_mm"], 1)
            pe.wait_ge(sm["kr_back"], 16)
            for s, w in segments(LAT):
                last = mm(ps[KR0:KR0 + 32, 6 + s // SEG, 0:w], cst("swap")[KR0:KR0 + 32, KR0:KR0 + 32],
                          krT[KR0:KR0 + 32, s:s + w], start=True, stop=True)
                if s == 0:
                    need(pe, sm["aux2_read"], len(AUX2))
            last.then_inc(sm["kr_mm"], 1)
            pe.wait_ge(sm["n_done"], 3)
            pe.wait_ge(sm["uq_in"], 32)
            for h in range(H):
                b = 2 * (h % 2)
                need(pe, sm["mq_ev"], h - 1)
                for s, w in segments(LAT):
                    for k in range(2):
                        last = mm(ps[0:MLA_QK, b + s // SEG, 0:w], uq_sb[:, k, h * MLA_QK:(h + 1) * MLA_QK],
                                  cq[:, k, s:s + w], start=(k == 0), stop=(k == 1))
                last.then_inc(sm["mq_mm"], 1)
                if h >= 1:
                    swap_q(pe, h - 1)
            for v in range(NT // 2):
                if v < 2:
                    pe.wait_ge(sm["mq_ev"], H)
                else:
                    pe.wait_ge(sm["mv_ev"], v - 1)
                for e in range(2):
                    c = 2 * v + e
                    last = mm(ps[:, v % 2, 256 * e:256 * e + 256], ckv[:, c * P:(c + 1) * P],
                              ukv_sb.rearrange("p (h a) -> p h a", h=H)[:, :, MLA_NOPE:], start=True, stop=True)
                last.then_inc(sm["mv_mm"], 1)
            swap_q(pe, H - 1)
            for h in range(H):
                if h == 0:
                    pe.wait_ge(sm["mv_ev"], NT // 2)
                    pe.wait_ge(sm["n_ln"], 2)
                need(pe, sm["mk_ev"], h - 1)
                b = 3 * (h % 2)
                for s, w in segments(TOK):
                    last = mm(ps[0:MLA_NOPE, b + s // SEG, 0:w], ukv_sb[:, h * P:h * P + MLA_NOPE],
                              ckv[:, s:s + w], start=True, stop=True)
                last.then_inc(sm["mk_mm"], 1)

            def scores(n):
                qb, u = UNITS[n]
                qc = slice(qb * P, (qb + 1) * P)
                for e, st in enumerate(sets_of(n)):
                    if st >= 2:
                        pe.wait_ge(sm["p_exp"], st - 1)
                    if st < 2:
                        pe.wait_ge(sm["mk_ev"], H)
                        pe.wait_ge(sm["mk_rope"], H)
                        pe.wait_ge(sm["mq_done"], H)
                    if e == 0 and u == H:
                        pe.wait_ge(sm["qz_done"], 2 * (qb + 1))
                    b = 3 * (st % 2)
                    for s, w in KSEG:
                        if u < H:
                            last = mm(ps[:, b + s // SEG, 0:w], QTm[0:MLA_QK, u, qc], KTm[0:MLA_QK, u, s:s + w],
                                      start=True, stop=True)
                        else:
                            g = 2 * (u - H) + e
                            last = mm(ps[:, b + s // SEG, 0:w], dqz[qb % 2][:, g, :], dk[:, g // 4, s:s + w],
                                      start=True, stop=True)
                    last.then_inc(sm["sc_mm"], 1)

            def turn_probs(n, gi):
                qb, u = UNITS[n]
                slot = sets_of(n)[0] % 4
                s, w = KSEG[gi]
                if gi == 0:
                    if u < H:
                        pe.wait_ge(sm["p_exp"], sets_of(n)[0] + 1)
                    else:
                        pe.wait_ge(sm["w_done"], qb * H + u - H + 1)
                    if n == 0:
                        pe.wait_ge(sm["kr_t"], 1)
                    need(pe, sm["wt_ev_d"], n)
                    if n % 8 == 3 and n > 8:
                        pe.wait_ge(sm["mix_b"], 2 * (n // 8))
                else:
                    pe.wait_ge(sm["wt_ev_a"], 2 * n + gi)
                for c in range(w // P):
                    last = tr(ps[:, 6, c * P:(c + 1) * P], prob[:, slot, s + c * P:s + (c + 1) * P], ident)
                last.then_inc(sm["wt_mm"], 1)

            def pv(n, gi):
                qb, u = UNITS[n]
                s, w = KSEG[gi]
                if gi == 0:
                    need(pe, sm["pv_ev"], n)
                if gi < 2:
                    pe.wait_ge(sm["wt_ev_a"], 2 * n + gi + 1)
                else:
                    pe.wait_ge(sm["wt_ev_d"], n + 1)
                V = V_tok if u < H else dv_tok
                h = u % H
                for c in range(s // P, (s + w) // P):
                    last = mm(ps[:, 7, u * 64:u * 64 + 64], wT[:, n % 2, c * P:(c + 1) * P],
                              V[:, c, h * 64:h * 64 + 64], start=(c == 0), stop=(c == NT - 1))
                if gi == 2:
                    last.then_inc(sm["pv_mm"], 1)

            def turn_out(qb, n):
                pe.wait_ge(sm["d_norm"], qb + 1)
                pe.wait_ge(sm["wt_ev_d"], n)
                for i in range(4):
                    last = tr(ps[:, 6, i * P:(i + 1) * P], o_tok[:, qb % 2, i * P:(i + 1) * P], ident)
                last.then_inc(sm["ot_mm"], 1)

            NU = len(UNITS)
            scores(0)
            for n in range(NU + 1):
                if n + 1 < NU:
                    scores(n + 1)
                for gi in range(len(KSEG)):
                    if n < NU:
                        turn_probs(n, gi)
                    if n >= 1:
                        pv(n - 1, gi)
                if n >= 8 and n % 8 == 2:
                    turn_out(n // 8 - 1, n + 1)
            turn_out(NLAT - 1, NU)

            for t in range(NLAT):
                if t == 0:
                    pe.wait_ge(sm["wo_in"], 16 * KD)
                    pe.wait_ge(sm["mix_b"], 2 * NLAT)
                    pe.wait_ge(sm["p_exp"], NSET)
                b = 2 * (t % 2)
                need(pe, sm["y_scaled"], t - 1)
                for i in range(2):
                    for k in range(KD):
                        last = mm(ps[:, b + i, :], mixT[:, k, t * P:(t + 1) * P], wo_sb[k][:, i * SEG:(i + 1) * SEG],
                                  start=(k == 0), stop=(k == KD - 1))
                last.then_inc(sm["y_mm"], 1)

        @block.scalar
        def _(act):
            A = nc.scalar.activation
            act.wait_ge(sm["cols_in"], 16)
            A(cs_e, col("c", 0, 16), ACT.Exp, scale=-1.0).then_inc(sm["c_exp"], 1)
            act.wait_ge(sm["setup"], 1)

            def x_stat(t):
                act.wait_ge(x_in[t % 4], 16 * (t // 4 + 1))
                need(act, sm["ssq_done"], t)
                A(junk, xin[:, t % 4, :], ACT.Square, accum_out=ssq[:, t:t + 1]).then_inc(sm["ssq_done"], 1)
                act.wait_ge(sm["ssq_done"], t + 1)
                A(rstd[:, t:t + 1], ssq[:, t:t + 1], ACT.Ln, scale=1.0 / D, bias=eps_col).then_inc(sm["rs_done"], 1)
                act.wait_ge(sm["rs_done"], 2 * t + 1)
                A(rstd[:, t:t + 1], rstd[:, t:t + 1], ACT.Exp, scale=-0.5).then_inc(sm["rs_done"], 1)

            def rows_out(piece):
                act.wait_ge(sm["ada_mm"], piece + 1)
                need(act, sm["mod_turn"], piece)
                A(mod_row[0:2, :], ps[0:2, 0:2, :].rearrange("p a b -> p (a b)"), ACT.Copy
                  ).then_inc(sm["row_read"], 1)

            for gi, (t0, n) in enumerate(GROUPS):
                for t in range(t0, t0 + n):
                    x_stat(t)
                if gi == 0:
                    rows_out(0)
                    rows_out(1)
                for k in range(1, KD, 2):
                    q = gi * KD + k
                    act.wait_ge(sm["xT_mm"], q + 1)
                    act.wait_ge(sm["mod_A"], 2)
                    m = 0 if t0 < NLAT else 1
                    A(hT[:, k, t0 * P:(t0 + n) * P], ps[:, 4 + q % 4, 0:n * P], ACT.Identity,
                      scale=mA[:, 2 * k + m:2 * k + m + 1], bias=mod[:, 2 * k + m:2 * k + m + 1]
                      ).then_inc(sm["hT_act"], 1)
            rows_out(2)
            act.wait_ge(sm["gp_mm"], 1)
            A(GP[:, :], ps[:, 0:2, :], ACT.Copy).then_inc(sm["GP_done"], 1)

            def turned_out(i):
                for j, (what, t, s, w, _) in aux_at(i, ("turn", "logits")):
                    act.wait_ge(sm["aux_mm"], j + 1)
                    bank = 6 + j % 2
                    if what == "logits":
                        A(gates[:, 0:16 * NT], ps[:, bank, 0:16 * NT], ACT.Copy).then_inc(sm["aux_read"], 1)
                        continue
                    h = head_of(t)
                    dst = k_tok if GDN_TILES[t] == "k" else v_tok
                    A(dst[:, s // P:(s + w) // P, h * P:(h + 1) * P],
                      ps[:, bank, 0:w].rearrange("p (c n) -> p c n", n=P), ACT.Copy,
                      scale=0.5 if GDN_TILES[t] == "v" else 1.0).then_inc(sm["aux_read"], 1)

            def gates_a(part):
                if part == 0:
                    act.wait_ge(sm["gt_d"], 2)
                    A(en, na, ACT.Exp, scale=-1.0).then_inc(sm["gt_a"], 1)
                    act.wait_ge(sm["gt_a"], 1)
                    A(en, en, ACT.Ln, bias=one_col).then_inc(sm["gt_a"], 1)
                    A(beta, lg[:, :, 0:8], ACT.Exp, scale=-1.0).then_inc(sm["gt_a"], 1)
                    A(ea[:, :], col("alog", 0, 8), ACT.Exp).then_inc(sm["gt_a"], 1)
                else:
                    act.wait_ge(sm["gt_d"], 7)
                    A(EG, gam, ACT.Exp).then_inc(sm["gt_a"], 1)
                    A(EKD, dtk, ACT.Exp).then_inc(sm["gt_a"], 1)
                    A(GL, tot, ACT.Exp).then_inc(sm["gt_a"], 1)

            for i in range(NG + 3):
                if i == GATES_AT - 2:
                    gates_a(0)
                if i == GATES_AT + 2:
                    gates_a(1)
                if i < NG:
                    act.wait_ge(sm["in_mm"], i + 1)
                    b = 3 * (i % 2)
                    if i == 0:
                        A(misc[:, 0:LAT], ps[:, b:b + 2, :], ACT.Copy)
                        A(misc[:, LAT:TOK], ps[:, b + 2, 0:CTX], ACT.Copy).then_inc(sm["evac_done"], 1)
                    else:
                        if i < 3:
                            act.wait_ge(sm["pad_done"], 6)
                        need(act, sm["conv_step"], 5 * (i - 2))
                        op = A(raw[i % 2][:, 2:2 + LAT], ps[:, b:b + 2, :], ACT.Copy)
                        if GDN_TILES[i] != "q":
                            op = A(raw[i % 2][:, CTX_RAW:CTX_RAW + CTX], ps[:, b + 2, 0:CTX], ACT.Copy)
                        op.then_inc(sm["evac_done"], 1)
                t = i - 1
                if 1 <= t < NG:
                    n = LAT if GDN_TILES[t] == "q" else CV_W
                    act.wait_ge(sm["conv_step"], 5 * t)
                    need(act, sm["silu_done"], t - 1)
                    A(ebuf[:, 0:n], cv[t % 2][:, 0:n], ACT.Tanh, scale=0.5).then_inc(sm["exp_done"], 1)
                jobs = aux_at(i, ("ones",))
                for j, (_, t, s, w, _) in jobs:
                    act.wait_ge(sm["aux_mm"], j + 1)
                    big = float(DK) if GDN_TILES[t] == "q" else 1.0
                    A(sqb[t % 2][:, s:s + w], ps[:, 6 + j % 2, 0:w], ACT.Ln, scale=big,
                      bias=eps_q if GDN_TILES[t] == "q" else eps_k).then_inc(sm["aux_read"], 1)
                if jobs:
                    j, (_, t, _, _, _) = jobs[-1]
                    n = ntok(GDN_TILES[t])
                    act.wait_ge(sm["aux_read"], j + 1)
                    A(sqb[t % 2][:, 0:n], sqb[t % 2][:, 0:n], ACT.Exp, scale=-0.5).then_inc(sm["rn_done"], 1)
                turned_out(i)

            for g, group in enumerate(INVERSES):
                for s, c in enumerate(group):
                    if g == 0:
                        act.wait_ge(sm["gt_d"], 9)
                        act.wait_ge(sm["in_mm"], NG)
                        act.wait_ge(sm["aux_mm"], len(AUX))
                        act.wait_ge(sm["fin_done"], len(QKI))
                        act.wait_ge(sm["spill"], 16)
                        act.wait_ge(sm["spill_kr"], 16)
                    else:
                        act.wait_ge(sm["upd"], 2 * (inv_index(g - 1, 5, s) + 1))
                    A(iv[s]["gbc"], g_[:, c, :].unsqueeze(2).broadcast_to([P, 8, P]), ACT.Copy
                      ).then_inc(sm["gbc_done"], 1)
                for s, c in enumerate(group):
                    act.wait_ge(sm["ex_done"], 8 * (c + 1))
                    A(iv[s]["E"], iv[s]["E"], ACT.Exp).then_inc(sm["e_done"], 1)
                for s, c in enumerate(group):
                    act.wait_ge(sm["tr_mm"], c + 1)
                    act.wait_ge(sm["qk_done"], 2 * min(c + 1, NLAT))
                    A(iv[s]["P"], ps[:, 2 * s, :], ACT.Copy).then_inc(sm["p_done"], 1)

            for m in LATSTEP:
                i, d = m // 2, m % 2
                c = order[d][i]
                act.wait_ge(sm["qs_mm"], LATSTEP.index(m) + 1)
                need(act, sm["oa_done"], len([q for q in LATSTEP if q <= m - 2]))
                for h in range(H):
                    op = A(t2[:, d, h * P:(h + 1) * P], ps[:, 4 * d + 3, h * P:(h + 1) * P], ACT.Copy,
                           scale=EG[:, c, 4 * d + h:4 * d + h + 1])
                op.then_inc(sm["t2_done"], 1)
            o_ss, o_rs = o_stat[:, 0:NLAT * H], o_stat[:, NLAT * H:]
            act.wait_ge(sm["ostat_d"], 1)
            A(o_rs, o_ss, ACT.Ln, scale=1.0 / P, bias=eps_col).then_inc(sm["ostat_a"], 1)
            act.wait_ge(sm["ostat_a"], 1)
            A(o_rs, o_rs, ACT.Exp, scale=-0.5).then_inc(sm["ostat_a"], 1)

            for j, kind in enumerate(REST_TILES):
                act.wait_ge(sm["in2_mm"], j + 1)
                b = 3 * (j % 2)
                i = j - first_of[kind]
                if j in ZT:
                    z = ZT.index(j)
                    need(act, sm["z_done"], z - 1)
                    A(zexp[:, z % 2, :], ps[:, b:b + 2, :], ACT.Tanh, scale=0.5).then_inc(sm["z_exp"], 1)
                    continue
                if kind == "dv":
                    need(act, sm["aux2_mm"], len([a for a in AUX2 if a[4] <= j]) if i else 0)
                dst = {"cq": lambda: cq[:, i, :], "ckv": lambda: ckv, "dq": lambda: dq[:, i, :],
                       "dk": lambda: dk[:, i, :], "dv": lambda: dvT}[kind]()
                op = A(dst[:, 0:LAT], ps[:, b:b + 2, :], ACT.Copy, scale=DIFF_SCALE if kind == "dq" else 1.0)
                if kind not in LAT_ONLY:
                    op = A(dst[:, LAT:TOK], ps[:, b + 2, 0:CTX], ACT.Copy)
                op.then_inc(sm["c_evac"], 1)

            act.wait_ge(sm["lam_d"], 4)
            A(lamt[:, 0:2], lamt[:, 0:2], ACT.Exp).then_inc(sm["lam_a"], 1)

            act.wait_ge(sm["n_mm"], 1)
            A(cq_rn, ps[:, 0:2, :], ACT.Ln, scale=1.0 / Q_RANK, bias=eps_col).then_inc(sm["n_ln"], 1)
            A(kv_rn[:, 0:LAT], ps[:, 2:4, :], ACT.Ln, scale=1.0 / KV_RANK, bias=eps_col)
            A(kv_rn[:, LAT:TOK], ps[:, 4, 0:CTX], ACT.Ln, scale=1.0 / KV_RANK,
              bias=eps_col).then_inc(sm["n_ln"], 1)
            act.wait_ge(sm["n_ln"], 2)
            A(cq_rn, cq_rn, ACT.Exp, scale=-0.5).then_inc(sm["n_exp"], 1)
            A(kv_rn, kv_rn, ACT.Exp, scale=-0.5).then_inc(sm["n_exp"], 1)
            for h in range(H):
                act.wait_ge(sm["mq_mm"], h + 1)
                b = 2 * (h % 2)
                A(QTm[0:MLA_QK, h, :], ps[0:MLA_QK, b:b + 2, :], ACT.Copy, scale=MLA_SCALE).then_inc(sm["mq_ev"], 1)
            for v in range(NT // 2):
                act.wait_ge(sm["mv_mm"], v + 1)
                A(V_tok[:, 2 * v:2 * v + 2, :], ps[:, v % 2, :].rearrange("p (a b) -> p a b", a=2),
                  ACT.Copy).then_inc(sm["mv_ev"], 1)
            for h in range(H):
                act.wait_ge(sm["mk_mm"], h + 1)
                b = 3 * (h % 2)
                A(KTm[0:MLA_NOPE, h, 0:LAT], ps[0:MLA_NOPE, b:b + 2, :], ACT.Copy)
                A(KTm[0:MLA_NOPE, h, LAT:TOK], ps[0:MLA_NOPE, b + 2, 0:CTX], ACT.Copy).then_inc(sm["mk_ev"], 1)
                if h == 0:
                    act.wait_ge(sm["kr_done"], 1)
                A(KTm[KR0:MLA_QK, h, :], krT[KR0:MLA_QK, :], ACT.Copy).then_inc(sm["mk_rope"], 1)

            def exps(st):
                act.wait_ge(sm["mx_done"], st + 1)
                if st >= 4:
                    prev = [q for q in range(len(UNITS)) if st - 4 in sets_of(q)][0]
                    act.wait_ge(sm["wt_mm"], 3 * (prev + 1))
                if st < 4:
                    act.wait_ge(sm["n_done"], 3)
                b = 3 * (st % 2)
                A(prob[:, st % 4, :], ps[:, b:b + 3, :].rearrange("p a b -> p (a b)")[:, 0:TOK], ACT.Exp,
                  bias=nmax[:, st:st + 1], accum_out=lsum[:, st:st + 1]).then_inc(sm["p_exp"], 1)

            def turned(n, gi):
                s, w = KSEG[gi]
                act.wait_ge(sm["wt_mm"], 3 * n + gi + 1)
                if gi == 0:
                    need(act, sm["pv_mm"], n - 1)
                A(wT[:, n % 2, s:s + w], ps[:, 6, 0:w], ACT.Copy).then_inc(sm["wt_ev_a"], 1)

            def d_stat(qb):
                act.wait_ge(sm["d_red"], qb + 1)
                A(drs[:, 4 * qb:4 * qb + 4], dss[:, 4 * qb:4 * qb + 4], ACT.Ln, scale=1.0 / DIFF_V,
                  bias=eps_col).then_inc(sm["d_ln"], 1)
                act.wait_ge(sm["d_ln"], qb + 1)
                A(drs[:, 4 * qb:4 * qb + 4], drs[:, 4 * qb:4 * qb + 4], ACT.Exp, scale=-0.5).then_inc(sm["d_exp"], 1)

            exps(0)
            for n in range(len(UNITS)):
                if n >= 8 and n % 8 == 1:
                    d_stat(n // 8 - 1)
                coming = sets_of(n + 1) if n + 1 < len(UNITS) else []
                if len(coming) == 2:
                    exps(coming[0])
                turned(n, 0)
                turned(n, 1)
                if coming:
                    exps(coming[-1])
            d_stat(NLAT - 1)

            for t in range(NLAT):
                act.wait_ge(sm["y_mm"], t + 1)
                b = 2 * (t % 2)
                need(act, sm["y_sq"], t)
                A(y_junk, ps[:, b:b + 2, :], ACT.Square, accum_out=yst[:, t:t + 1]).then_inc(sm["y_sq"], 1)
                act.wait_ge(sm["y_sq"], t + 1)
                r = yst[:, NLAT + t:NLAT + t + 1]
                A(r, yst[:, t:t + 1], ACT.Ln, scale=1.0 / D, bias=eps_col).then_inc(sm["y_ln"], 1)
                act.wait_ge(sm["y_ln"], t + 1)
                A(r, r, ACT.Exp, scale=-0.5).then_inc(sm["y_exp"], 1)

        @block.vector
        def _(dve):
            V = nc.vector
            V.memset(eps_col, EPS)
            V.memset(one_col, 1.0)
            V.memset(eps_k, 4 * EPS)
            V.memset(eps_q, 4 * EPS * DK).then_inc(sm["setup"], 1)
            dve.wait_ge(sm["c_exp"], 1)
            V.tensor_scalar(cs_e, cs_e, 1.0, None, ALU.add).then_inc(sm["c_one"], 1)
            dve.wait_ge(sm["c_one"], 1)
            V.reciprocal(cs_e, cs_e).then_inc(sm["c_rec"], 1)
            dve.wait_ge(sm["c_rec"], 1)
            V.tensor_tensor(cs, cs_e, col("c", 0, 16), ALU.mult).then_inc(sm["c_silu"], 1)

            def xn(gi):
                t0, n = GROUPS[gi]
                for t in range(t0, t0 + n):
                    dve.wait_ge(sm["rs_done"], 2 * t + 2)
                    V.tensor_scalar(xin[:, t % 4, :], xin[:, t % 4, :], rstd[:, t:t + 1], None,
                                    ALU.mult).then_inc(sm["xn_done"], 1)

            def hT_even(gi):
                t0, n = GROUPS[gi]
                m = 0 if t0 < NLAT else 1
                for k in range(0, KD, 2):
                    q = gi * KD + k
                    dve.wait_ge(sm["xT_mm"], q + 1)
                    V.tensor_scalar(hT[:, k, t0 * P:(t0 + n) * P], ps[:, 4 + q % 4, 0:n * P],
                                    mA[:, 2 * k + m:2 * k + m + 1], mod[:, 2 * k + m:2 * k + m + 1],
                                    ALU.mult, ALU.add).then_inc(sm["hT_dve"], 1)

            xn(0)
            mod3 = mod.rearrange("p (j c) -> p j c", c=2)

            def add_bias(piece):
                dve.wait_ge(sm["mod_turn"], piece + 1)
                V.tensor_tensor(mod3[:, 8 * piece:8 * piece + 8, :],
                                ps[:, 2, 0:16].rearrange("p (j c) -> p j c", c=2),
                                col("ada_b", 8 * piece, 8).unsqueeze(2).broadcast_to([P, 8, 2]), ALU.add
                                ).then_inc(sm["mod_add"], 1)
                dve.wait_ge(sm["mod_add"], piece + 1)

            add_bias(0)
            add_bias(1)
            mA3 = mA.rearrange("p (j c) -> p j c", c=2)
            V.tensor_scalar(mA, mod[:, 16:32], 1.0, None, ALU.add).then_inc(sm["mod_A"], 1)
            dve.wait_ge(sm["mod_A"], 1)
            V.tensor_tensor(mA3, mA3, col("pre", 0, 8).unsqueeze(2).broadcast_to([P, 8, 2]),
                            ALU.mult).then_inc(sm["mod_A"], 1)
            dve.wait_ge(sm["mod_A"], 2)
            hT_even(0)
            xn(1)
            hT_even(1)
            xn(2)
            hT_even(2)
            add_bias(2)
            V.tensor_tensor(gp_col, mod3[:, 16:24, 0], col("post", 0, 8), ALU.mult).then_inc(sm["gp_done"], 1)
            dve.wait_ge(sm["gp_done"], 1)
            V.tensor_tensor(gp_diag, ident.unsqueeze(1).broadcast_to([P, KD, P]),
                            gp_col.unsqueeze(2).broadcast_to([P, KD, P]), ALU.mult).then_inc(sm["diag_done"], 1)

            def gates_d0():
                logits_read = [j for j, a in enumerate(AUX) if a[0] == "logits"][0] + 1
                dve.wait_ge(sm["aux_read"], logits_read)
                V.tensor_tensor(xa, lg[:, :, 8:16], col("dt", 0, 8).unsqueeze(1).broadcast_to([P, NT, 8]),
                                ALU.add).then_inc(sm["gt_d"], 1)
                dve.wait_ge(sm["gt_d"], 1)
                V.scalar_tensor_tensor(out=na, in0=xa, scalar=-1.0, in1=xa, op0=ALU.mult,
                                       op1=ALU.max).then_inc(sm["gt_d"], 1)
                dve.wait_ge(sm["gt_a"], 4)
                V.scalar_tensor_tensor(out=sp, in0=xa, scalar=0.0, in1=en, op0=ALU.max,
                                       op1=ALU.add).then_inc(sm["gt_d"], 1)
                dve.wait_ge(sm["gt_d"], 3)
                V.scalar_tensor_tensor(out=g_, in0=sp, scalar=-1.0, in1=ea[:, :].unsqueeze(1).broadcast_to([P, NT, 8]),
                                       op0=ALU.mult, op1=ALU.mult).then_inc(sm["gt_d"], 1)

            def gates_d1():
                gj = [j for j, a in enumerate(AUX) if a[0] == "gates"][0]
                gb = 6 + gj % 2
                dve.wait_ge(sm["aux_mm"], gj + 1)
                V.tensor_copy(gam, ps[:, gb, 0:8 * NT].rearrange("p (c n) -> p c n", n=8)).then_inc(sm["gt_d"], 1)
                V.tensor_copy(tot, ps[:, gb, 128:128 + 8 * NT].rearrange("p (c n) -> p c n", n=8)).then_inc(sm["gt_d"], 1)
                dve.wait_ge(sm["gt_d"], 6)
                V.tensor_scalar(beta, beta, 1.0, None, ALU.add).then_inc(sm["aux_read"], 1)
                V.tensor_tensor(dtk, tot, gam, ALU.subtract).then_inc(sm["gt_d"], 1)
                dve.wait_ge(sm["aux_read"], gj + 1)
                dve.wait_ge(sm["gt_d"], 7)
                V.reciprocal(beta, beta).then_inc(sm["gt_d"], 1)
                dve.wait_ge(sm["gt_d"], 8)
                dve.wait_ge(sm["gt_a"], 7)
                V.tensor_tensor(bek, beta, EKD, ALU.mult).then_inc(sm["gt_d"], 1)


            for i in range(NG + 1):
                if i == GATES_AT - 2:
                    gates_d0()
                if i == GATES_AT + 1:
                    gates_d1()
                if 1 <= i < NG:
                    n = LAT if GDN_TILES[i] == "q" else CV_W
                    dve.wait_ge(sm["evac_done"], i + 1)
                    need(dve, sm["silu_done"], i - 2)
                    src, dst = raw[i % 2], cv[i % 2]
                    for j in range(CONV_W):
                        wj = col("conv", (i - 1) * CONV_W + j)
                        if j == 0:
                            op = V.tensor_scalar(dst[:, 0:n], src[:, 0:n], wj, None, ALU.mult)
                        else:
                            dve.wait_ge(sm["conv_step"], 5 * (i - 1) + j)
                            op = V.scalar_tensor_tensor(out=dst[:, 0:n], in0=src[:, j:j + n], scalar=wj,
                                                        in1=dst[:, 0:n], op0=ALU.mult, op1=ALU.add)
                        op.then_inc(sm["conv_step"], 1)
                t = i - 1
                if 1 <= t < NG:
                    n = LAT if GDN_TILES[t] == "q" else CV_W
                    dve.wait_ge(sm["exp_done"], t)
                    y = y_of(t)
                    if GDN_TILES[t] == "v" and t >= 2 and GDN_TILES[t - 2] == "v":
                        dve.wait_ge(sm["aux_mm"], max(j for j, a in enumerate(AUX) if a[1] == t - 2) + 1)
                    op = V.scalar_tensor_tensor(out=y[:, 0:LAT], in0=ebuf[:, 0:LAT], scalar=1.0,
                                                in1=cv[t % 2][:, 0:LAT], op0=ALU.add, op1=ALU.mult)
                    if GDN_TILES[t] != "q":
                        op = V.scalar_tensor_tensor(out=y[:, LAT:TOK], in0=ebuf[:, CTX_CV:CTX_CV + CTX], scalar=1.0,
                                                    in1=cv[t % 2][:, CTX_CV:CTX_CV + CTX], op0=ALU.add, op1=ALU.mult)
                    op.then_inc(sm["silu_done"], 1)

            for g, group in enumerate(INVERSES):
                for s, c in enumerate(group):
                    dve.wait_ge(sm["gb_mm"], c + 1)
                    for d in range(2):
                        for h in range(H):
                            V.scalar_tensor_tensor(
                                out=iv[s]["E"][:, 4 * d + h, :], in0=ps[:, 2 * s + d, h * P:(h + 1) * P],
                                scalar=gam[:, c, 4 * d + h:4 * d + h + 1], in1=cst("neg_f" if d == 0 else "neg_b"),
                                op0=ALU.subtract, op1=ALU.min).then_inc(sm["ex_done"], 1)
                for s, c in enumerate(group):
                    kk = ps[:, 2 * s, :].rearrange("p (h n) -> p h n", n=P)
                    qk = ps[:, 2 * s + 1, :].rearrange("p (h n) -> p h n", n=P)
                    Qc = Q_all[:, c, :].rearrange("p (h n) -> p h n", n=P)
                    dve.wait_ge(sm["pool_w"], 3 * (c + 1))
                    dve.wait_ge(sm["pre_mm"], c + 1)
                    V.tensor_tensor(iv[s]["At"], kk, iv[s]["At"], ALU.mult).then_inc(sm["at_done"], 1)
                    dve.wait_ge(sm["at_done"], c + 1)
                    V.tensor_tensor(Qc, iv[s]["At"], heads(cst("sib1")), ALU.mult).then_inc(sm["q_step"], 1)
                    dve.wait_ge(sm["q_step"], 2 * c + 1)
                    V.tensor_tensor(Qc, heads(ident), Qc, ALU.subtract).then_inc(sm["q_step"], 1)
                    if c < NLAT:
                        for d in range(2):
                            V.tensor_tensor(QK[:, d * NLAT + c, :].rearrange("p (h n) -> p h n", n=P), qk,
                                            iv[s]["E"][:, 4 * d:4 * d + 4, :], ALU.mult).then_inc(sm["qk_done"], 1)
                for lev in range(6):
                    for s, c in enumerate(group):
                        n = inv_index(g, lev, s)
                        dve.wait_ge(sm["x_mm"], n + 1)
                        V.tensor_tensor(iv[s]["X"], ps[:, 2 * s, :].rearrange("p (h n) -> p h n", n=P),
                                        heads(cst(f"sib{LEVELS[lev + 1]}")), ALU.mult).then_inc(sm["xs_done"], 1)
                    for s, c in enumerate(group):
                        n = inv_index(g, lev, s)
                        if lev < 5:
                            dve.wait_ge(sm["pq_mm"], 2 * n + 1)
                            V.tensor_tensor(iv[s]["P"], iv[s]["P"],
                                            ps[:, 2 * s, :].rearrange("p (h n) -> p h n", n=P),
                                            ALU.subtract).then_inc(sm["upd"], 1)
                        dve.wait_ge(sm["pq_mm"], 2 * n + 2)
                        V.tensor_tensor(Q_all[:, c, :], Q_all[:, c, :], ps[:, 2 * s + 1, :],
                                        ALU.subtract).then_inc(sm["upd"], 1 if lev < 5 else 2)

            def h3(ap):
                return ap.rearrange("p (h n) -> p h n", n=P)
            dve.wait_ge(sm["gt_d"], 9)
            for i in range(NT):
                for d in range(2):
                    m = 2 * i + d
                    c = order[d][i]
                    dve.wait_ge(sm["ks_mm"], m + 1)
                    V.tensor_tensor(h3(R[:, d, :]), h3(ps[:, 4 * d, :]), per_head(EG[:, c, 4 * d:4 * d + 4]),
                                    ALU.mult).then_inc(sm["r_done"], 1)
                    dve.wait_ge(sm["r_done"], 2 * m + 1)
                    V.tensor_tensor(R[:, d, :], v_tok[:, c, :], R[:, d, :], ALU.subtract).then_inc(sm["r_done"], 1)
                for d in range(2):
                    m = 2 * i + d
                    c = order[d][i]
                    dve.wait_ge(sm["tr4_mm"], m + 1)
                    V.tensor_tensor(h3(Vs[:, d, :]), h3(ps[:, 4 * d + 1, :]), per_head(bek[:, c, 4 * d:4 * d + 4]),
                                    ALU.mult).then_inc(sm["vv_done"], 1)
                    need(dve, sm["qkv_mm"], len([q for q in LATSTEP if q <= m - 2]))
                    V.tensor_tensor(h3(Vn[:, d, :]), h3(ps[:, 4 * d + 1, :]), per_head(beta[:, c, 4 * d:4 * d + 4]),
                                    ALU.mult).then_inc(sm["vv_done"], 1)
                for d in range(2):
                    m = 2 * i + d
                    c = order[d][i]
                    dve.wait_ge(sm["ds_mm"], m + 1)
                    dve.wait_ge(sm["sg_done"], m + 1)
                    V.tensor_tensor(S[:, d, :], Sg[:, d, :], ps[:, 4 * d + 2, :], ALU.add).then_inc(sm["s_upd"], 1)
                    if c < NLAT:
                        li = LATSTEP.index(m)
                        dve.wait_ge(sm["qkv_mm"], li + 1)
                        dve.wait_ge(sm["t2_done"], li + 1)
                        V.tensor_tensor(t2[:, d, :], t2[:, d, :], ps[:, 4 * d, :], ALU.add).then_inc(sm["o1_done"], 1)
            dve.wait_ge(sm["osq_done"], 1)
            V.tensor_reduce(o_stat[:, 0:NLAT * H], o_sq, AX.X, ALU.add).then_inc(sm["ostat_d"], 1)
            dve.wait_ge(sm["ostat_a"], 2)
            oa3 = o_acc.rearrange("p c (h n) -> p (c h) n", n=P)
            V.tensor_tensor(oa3, oa3, o_stat[:, NLAT * H:].unsqueeze(2).broadcast_to([P, NLAT * H, P]),
                            ALU.mult).then_inc(sm["o_ready"], 1)

            lam4 = col("lam", 0, 128).rearrange("p (a b n) -> p a b n", a=2, b=2)
            lp = lam_p[:, :].rearrange("p (a n) -> p a n", a=2)
            V.tensor_tensor(lp, lam4[:, :, 0, :], lam4[:, :, 1, :], ALU.mult).then_inc(sm["lam_d"], 1)
            dve.wait_ge(sm["lam_d"], 1)
            V.tensor_reduce(lamt[:, 0:2], lp, AX.X, ALU.add).then_inc(sm["lam_d"], 1)
            V.tensor_scalar(og_half, col("og"), 0.5, None, ALU.mult).then_inc(sm["lam_d"], 1)
            V.tensor_scalar(lamt[:, 4:5], col("sg"), 0.5 * (1.0 - LAM_INIT), None, ALU.mult).then_inc(sm["lam_d"], 1)
            dve.wait_ge(sm["lam_d"], 4)

            def z_dest(j):
                kind = REST_TILES[j]
                i = j - first_of[kind]
                return {"za": lambda: zbuf[:, i % 2, :], "zb": lambda: mixT[:, 4 + i, :],
                        "dz": lambda: mixT[:, 6 + i, :]}[kind]()

            for j in range(len(REST_TILES) + 1):
                if j < len(REST_TILES) and j in ZT:
                    z = ZT.index(j)
                    b = 3 * (j % 2)
                    dve.wait_ge(sm["z_exp"], z + 1)
                    need(dve, sm["aux2_read"], len([e for e in AUX2 if e[0] == "za" and e[1] <= j - 2]))
                    V.scalar_tensor_tensor(out=z_dest(j).rearrange("p (a b) -> p a b", a=2),
                                           in0=zexp[:, z % 2, :].rearrange("p (a b) -> p a b", a=2), scalar=1.0,
                                           in1=ps[:, b:b + 2, :], op0=ALU.add, op1=ALU.mult).then_inc(sm["z_done"], 1)
                for a, (kind, t, s, w, jj) in enumerate(AUX2):
                    if jj != j:
                        continue
                    dve.wait_ge(sm["aux2_mm"], a + 1)
                    bank = 6 + a % 2
                    if kind == "za":
                        h = t - first_of["za"]
                        dve.wait_ge(sm["z_done"], ZT.index(t) + 1)
                        V.scalar_tensor_tensor(out=mixT[:, h, s:s + w], in0=ps[:, bank, 0:w], scalar=og_half,
                                               in1=zbuf[:, h % 2, s:s + w], op0=ALU.mult,
                                               op1=ALU.mult).then_inc(sm["aux2_read"], 1)
                    elif kind == "dv":
                        i = t - first_of["dv"]
                        V.tensor_copy(dv_tok[:, s // P:(s + w) // P, i * P:(i + 1) * P],
                                      ps[:, bank, 0:w].rearrange("p (c n) -> p c n", n=P)
                                      ).then_inc(sm["aux2_read"], 1)
                    else:
                        dve.wait_ge(sm["rope_in"], 16)
                        r = ROPED.index(t)
                        if s == 0:
                            need(dve, sm["rope_done"], 2 * r)
                        V.tensor_tensor(rbuf[:, s:s + w], ps[:, bank, 0:w], rope[:, 1, s:s + w],
                                        ALU.mult).then_inc(sm["aux2_read"], 1)

            dve.wait_ge(sm["n_exp"], 2)
            for k in range(2):
                V.scalar_tensor_tensor(out=cq[:, k, :], in0=cq[:, k, :], scalar=col("qg", k), in1=cq_rn,
                                       op0=ALU.mult, op1=ALU.mult).then_inc(sm["n_done"], 1)
            V.scalar_tensor_tensor(out=ckv, in0=ckv, scalar=col("kvg"), in1=kv_rn,
                                   op0=ALU.mult, op1=ALU.mult).then_inc(sm["n_done"], 1)
            rows = slice(KR0, KR0 + MLA_ROPE)
            dve.wait_ge(sm["n_done"], 3)
            dve.wait_ge(sm["kr_mm"], 1)
            dve.wait_ge(sm["rope_done"], 2 * len(ROPED))
            V.tensor_tensor(rbuf[rows, :].rearrange("p (a b) -> p a b", a=2), ps[rows, 6:8, :],
                            rope[rows, 1, :].rearrange("p (a b) -> p a b", a=2), ALU.mult).then_inc(sm["kr_t"], 1)
            V.tensor_tensor(krT[rows, 0:LAT], krT[rows, 0:LAT], rope[rows, 0, :], ALU.mult).then_inc(sm["kr_c"], 1)
            dve.wait_ge(sm["kr_t"], 1)
            dve.wait_ge(sm["kr_c"], 1)
            V.tensor_tensor(krT[rows, 0:LAT], krT[rows, 0:LAT], rbuf[rows, :], ALU.add).then_inc(sm["kr_done"], 1)
            for h in range(H):
                dve.wait_ge(sm["mq_swap"], h + 1)
                dve.wait_ge(sm["mq_done"], h) if h else dve.wait_ge(sm["kr_done"], 1)
                V.tensor_tensor(rbuf[rows, :].rearrange("p (a b) -> p a b", a=2), ps[rows, 6:8, :],
                                rope[rows, 1, :].rearrange("p (a b) -> p a b", a=2), ALU.mult).then_inc(sm["mq_t"], 1)
                V.tensor_tensor(QTm[rows, h, :], QTm[rows, h, :], rope[rows, 0, :], ALU.mult).then_inc(sm["mq_c"], 1)
                dve.wait_ge(sm["mq_t"], h + 1)
                dve.wait_ge(sm["mq_c"], h + 1)
                V.tensor_tensor(QTm[rows, h, :], QTm[rows, h, :], rbuf[rows, :], ALU.add).then_inc(sm["mq_done"], 1)

            dve.wait_ge(sm["lam_a"], 1)
            V.tensor_tensor(lamt[:, 5:6], lamt[:, 1:2], lamt[:, 0:1], ALU.subtract).then_inc(sm["lam_d"], 1)
            dve.wait_ge(sm["lam_d"], 5)
            V.tensor_scalar(lamt[:, 6:7], lamt[:, 5:6], -LAM_INIT, None, ALU.add).then_inc(sm["lam_d"], 1)
            dve.wait_ge(sm["lam_d"], 6)

            def row_max(n):
                for st in sets_of(n):
                    dve.wait_ge(sm["sc_mm"], st + 1)
                    b = 3 * (st % 2)
                    V.tensor_reduce(nmax[:, st:st + 1], ps[:, b:b + 3, :].rearrange("p a b -> p (a b)")[:, 0:TOK],
                                    AX.X, ALU.max, negate=True).then_inc(sm["mx_done"], 1)

            linv = [0]

            def counted(op):
                linv[0] += 1
                op.then_inc(sm["l_inv"], 1)
                return linv[0]

            def combine(n):
                qb, u = UNITS[n]
                st = sets_of(n)
                dve.wait_ge(sm["p_exp"], st[-1] + 1)
                v = counted(V.reciprocal(rinv[:, n:n + 1], lsum[:, st[0]:st[0] + 1]))
                if u < H:
                    return
                v = counted(V.reciprocal(rinv1[:, n:n + 1], lsum[:, st[1]:st[1] + 1]))
                dve.wait_ge(sm["l_inv"], v)
                v = counted(V.scalar_tensor_tensor(out=coef[:, n:n + 1], in0=lsum[:, st[0]:st[0] + 1],
                                                   scalar=lamt[:, 6:7], in1=rinv1[:, n:n + 1],
                                                   op0=ALU.mult, op1=ALU.mult))
                dve.wait_ge(sm["l_inv"], v)
                p0, p1 = prob[:, st[0] % 4, :], prob[:, st[1] % 4, :]
                V.scalar_tensor_tensor(out=p0, in0=p1, scalar=coef[:, n:n + 1], in1=p0, op0=ALU.mult,
                                       op1=ALU.add).then_inc(sm["w_done"], 1)

            def turned(n):
                s, w = KSEG[2]
                dve.wait_ge(sm["wt_mm"], 3 * n + 3)
                need(dve, sm["pv_mm"], n - 1)
                V.tensor_copy(wT[:, n % 2, s:s + w], ps[:, 6, 0:w]).then_inc(sm["wt_ev_d"], 1)

            def out_part(n):
                qb, u = UNITS[n]
                dve.wait_ge(sm["pv_mm"], n + 1)
                dve.wait_ge(sm["l_inv"], linv[0])
                V.tensor_scalar(o_tok[:, qb % 2, u * 64:u * 64 + 64], ps[:, 7, u * 64:u * 64 + 64],
                                rinv[:, n:n + 1], None, ALU.mult).then_inc(sm["pv_ev"], 1)

            def diff_out(qb):
                return o_tok[:, qb % 2, H * 64:].rearrange("p (h n) -> p h n", n=64)

            def square(qb):
                dve.wait_ge(sm["pv_ev"], 8 * (qb + 1))
                V.tensor_tensor(d_sq, diff_out(qb), diff_out(qb), ALU.mult).then_inc(sm["d_sqd"], 1)
                dve.wait_ge(sm["d_sqd"], qb + 1)
                V.tensor_reduce(dss[:, 4 * qb:4 * qb + 4], d_sq, AX.X, ALU.add).then_inc(sm["d_red"], 1)

            def normalise(qb):
                dve.wait_ge(sm["d_exp"], qb + 1)
                V.tensor_tensor(diff_out(qb), diff_out(qb),
                                drs[:, 4 * qb:4 * qb + 4].unsqueeze(2).broadcast_to([P, H, 64]),
                                ALU.mult).then_inc(sm["d_norm"], 1)

            def mix(qb):
                dve.wait_ge(sm["ot_mm"], qb + 1)
                mx = mixT[:, :, qb * P:(qb + 1) * P]
                pso = ps[:, 6, :].rearrange("p (i n) -> p i n", n=P)
                V.scalar_tensor_tensor(out=mx[:, 4:6, :], in0=pso[:, 0:2, :], scalar=0.5,
                                       in1=mx[:, 4:6, :], op0=ALU.mult, op1=ALU.mult).then_inc(sm["mix_b"], 1)
                V.scalar_tensor_tensor(out=mx[:, 6:8, :], in0=pso[:, 2:4, :], scalar=lamt[:, 4:5],
                                       in1=mx[:, 6:8, :], op0=ALU.mult, op1=ALU.mult).then_inc(sm["mix_b"], 1)

            NU = len(UNITS)
            row_max(0)
            for n in range(NU + 1):
                if n < NU:
                    combine(n)
                if n > 8 and n % 8 == 3:
                    mix(n // 8 - 1)
                if n + 1 < NU:
                    row_max(n + 1)
                if n < NU:
                    turned(n)
                if n >= 1:
                    out_part(n - 1)
                if n >= 8 and n % 8 == 0:
                    square(n // 8 - 1)
                if n >= 8 and n % 8 == 1:
                    normalise(n // 8 - 1)
            normalise(NLAT - 1)
            mix(NLAT - 1)

            for t in range(NLAT):
                dve.wait_ge(sm["y_exp"], t + 1)
                if t >= 2:
                    dve.wait_ge(y_out[t % 2], 16 * (t // 2))
                if t == 0:
                    dve.wait_ge(sm["wt_mm"], 3 * len(UNITS))
                b = 2 * (t % 2)
                V.scalar_tensor_tensor(out=y_buf[:, t % 2, :].rearrange("p (a b) -> p a b", a=2),
                                       in0=ps[:, b:b + 2, :], scalar=yst[:, NLAT + t:NLAT + t + 1],
                                       in1=GP[:, :].rearrange("p (a b) -> p a b", a=2),
                                       op0=ALU.mult, op1=ALU.mult).then_inc(sm["y_scaled"], 1)

        @block.gpsimd
        def _(pool):
            G = nc.gpsimd
            pool.wait_ge(sm["ada_mm"], 3)
            for r in raw:
                G.memset(r[:, 0:2], 0.0).then_inc(sm["pad_done"], 1)
                G.memset(r[:, LAT + 2:LAT + 6], 0.0).then_inc(sm["pad_done"], 1)
                G.memset(r[:, RAW_W - 2:RAW_W], 0.0).then_inc(sm["pad_done"], 1)

            for i in range(NG + 3):
                t = i - 1
                if 1 <= t < NG:
                    y = y_of(t)
                    if GDN_TILES[t] in "qk":
                        n = ntok(GDN_TILES[t])
                        pool.wait_ge(sm["silu_done"], t)
                        need(pool, sm["fin_done"], QKI.index(t) - 1)
                        G.tensor_tensor(sqb[t % 2][:, 0:n], y[:, 0:n], y[:, 0:n], ALU.mult).then_inc(sm["sq_done"], 1)
                t = i - 2
                if t in QKI:
                    n = ntok(GDN_TILES[t])
                    y = y_of(t)
                    pool.wait_ge(sm["rn_done"], QKI.index(t) + 1)
                    G.tensor_tensor(y[:, 0:n], y[:, 0:n], sqb[t % 2][:, 0:n], ALU.mult).then_inc(sm["fin_done"], 1)

            for g, group in enumerate(INVERSES):
                for s, c in enumerate(group):
                    b = iv[s]
                    pool.wait_ge(sm["e_done"], c + 1)
                    G.tensor_tensor(b["tmp"], b["E"][:, 0:4, :], per_head(beta[:, c, 0:4]), ALU.mult
                                    ).then_inc(sm["pool_w"], 1)
                    G.tensor_tensor(b["At"], b["E"][:, 4:8, :], per_head(beta[:, c, 4:8]), ALU.mult
                                    ).then_inc(sm["pool_w"], 1)
                    pool.wait_ge(sm["pool_w"], 3 * c + 2)
                    G.tensor_tensor(b["At"], b["At"], b["tmp"], ALU.add).then_inc(sm["pool_w"], 1)
                for lev in range(6):
                    for s, c in enumerate(group):
                        n = inv_index(g, lev, s)
                        b = iv[s]
                        mask = heads(cst(f"alt{LEVELS[lev + 1]}"))
                        Qc = Q_all[:, c, :].rearrange("p (h n) -> p h n", n=P)
                        if lev == 0:
                            pool.wait_ge(sm["p_done"], c + 1)
                        else:
                            pool.wait_ge(sm["upd"], 2 * (n - len(group)) + 1)
                        G.tensor_tensor(b["M"], b["P"], mask, ALU.mult).then_inc(sm["mn_done"], 1)
                        if lev > 0:
                            pool.wait_ge(sm["upd"], 2 * (n - len(group)) + 2)
                        G.tensor_tensor(b["N"], Qc, mask, ALU.mult).then_inc(sm["mn_done"], 1)

            pool.wait_ge(sm["upd"], 2 * 60)
            G.memset(view(20, 4 * 256), 0.0).then_inc(sm["s_init"], 1)
            G.memset(view(148, 16 * 256), 0.0).then_inc(sm["s_init"], 1)
            pool.wait_ge(sm["s_init"], 2)

            def h3(ap):
                return ap.rearrange("p (h n) -> p h n", n=P)
            for i in range(NT + 1):
                for d in range(2):
                    m = 2 * i + d
                    if i < NT:
                        c = order[d][i]
                        need(pool, sm["tr4_mm"], m - 1)
                        G.tensor_tensor(h3(Um[:, d, :]), h3(Q_all[:, c, :]), heads(cst("triu" if d == 0 else "tril")),
                                        ALU.mult).then_inc(sm["um_done"], 1)
                        need(pool, sm["s_upd"], m - 1)
                        G.tensor_tensor(h3(Sg[:, d, :]), h3(S[:, d, :]), per_head(GL[:, c, 4 * d:4 * d + 4]),
                                        ALU.mult).then_inc(sm["sg_done"], 1)
                    if m - 2 in LATSTEP:
                        li = LATSTEP.index(m - 2)
                        c = order[d][i - 1]
                        pool.wait_ge(sm["o1_done"], li + 1)
                        need(pool, sm["oa_done"], li)
                        G.tensor_tensor(o_acc[:, c, :], o_acc[:, c, :], t2[:, d, :], ALU.add
                                        ).then_inc(sm["oa_done"], 1)
            pool.wait_ge(sm["oa_done"], 16)
            pool.wait_ge(sm["tr4_mm"], 20)
            oa = view(148, NLAT * H, P)
            G.tensor_tensor(o_sq, oa, oa, ALU.mult).then_inc(sm["osq_done"], 1)

            for j, kind in enumerate(REST_TILES + [""]):
                if j - 1 in ROPED:
                    t = j - 1
                    kind = REST_TILES[t]
                    r = ROPED.index(t)
                    a = max(q for q, e in enumerate(AUX2) if e[1] == t)
                    dst = (dq if kind == "dq" else dk)[:, t - first_of[kind], 0:LAT]
                    pool.wait_ge(sm["aux2_mm"], a + 1)
                    pool.wait_ge(sm["rope_in"], 16)
                    G.tensor_tensor(dst, dst, rope[:, 0, :], ALU.mult).then_inc(sm["rope_done"], 1)
                    pool.wait_ge(sm["rope_done"], 2 * r + 1)
                    pool.wait_ge(sm["aux2_read"], a + 1)
                    G.tensor_tensor(dst, dst, rbuf, ALU.add).then_inc(sm["rope_done"], 1)
            pool.wait_ge(sm["z_done"], len(ZT))
            pool.wait_ge(sm["aux2_read"], len(AUX2))
            pool.wait_ge(sm["c_evac"], len(CT))
            for k in range(2):
                G.tensor_tensor(cq_sq[:, k, :], cq[:, k, :], cq[:, k, :], ALU.mult).then_inc(sm["n_sq"], 1)
            G.tensor_tensor(kv_sq, ckv, ckv, ALU.mult).then_inc(sm["n_sq"], 1)

            for qb in range(NLAT):
                if qb == 0:
                    pool.wait_ge(sm["rope_done"], 2 * len(ROPED))
                if qb == 1:
                    pool.wait_ge(sm["mk_rope"], H)
                if qb >= 2:
                    pool.wait_ge(sm["sc_mm"], 3 * H * (qb - 1))
                for i in range(2):
                    G.tensor_tensor(dqz[qb % 2][:, 4 * i:4 * i + 4, :],
                                    dq[:, i, qb * P:(qb + 1) * P].unsqueeze(1).broadcast_to([P, 4, P]),
                                    col("quad", 0, 4).unsqueeze(2).broadcast_to([P, 4, P]),
                                    ALU.mult).then_inc(sm["qz_done"], 1)

            for t in range(NLAT):
                pool.wait_ge(sm["y_scaled"], t + 1)
                pool.wait_ge(x2_in[t % 2], 16 * (t // 2 + 1))
                G.tensor_tensor(y_buf[:, t % 2, :], y_buf[:, t % 2, :], x_buf[:, t % 2, :], ALU.add
                                ).then_inc(sm["y_added"], 1)


def constants():
    i = np.arange(P)
    r, c = i[:, None], i[None, :]
    m = {"ident": r == c, "triu": r <= c, "tril": r >= c, "ones": np.ones((P, P)),
         "swap": (r // 32 == c // 32) & ((r + 16) % 32 == c % 32),
         "neg_f": np.where(r <= c, 0.0, NEG), "neg_b": np.where(r >= c, 0.0, NEG)}
    for b in LEVELS:
        m[f"sib{b}"] = (r // (2 * b) == c // (2 * b)) & (r // b != c // b)
        even = (r // b) % 2 == 0
        m[f"alt{b}"] = (r // b == c // b) & np.where(even, r >= c, r <= c)
    const = np.ascontiguousarray(np.stack([np.asarray(m[n], np.float32) for n in CONSTS], axis=1))
    t = np.arange(LAT)
    half = MLA_ROPE // 2
    inv = 1.0 / (ROPE_BASE ** (np.arange(0, half, 2, dtype=np.float32) / half))
    ang = np.concatenate([(t // GRID_W)[:, None].astype(np.float32) * inv,
                          (t % GRID_W)[:, None].astype(np.float32) * inv], axis=1).astype(np.float32)
    cos, sin = np.cos(ang).T, np.sin(ang).T
    rope = np.stack([np.tile(np.concatenate([cos, cos]), (4, 1)), np.tile(np.concatenate([-sin, sin]), (4, 1))],
                    axis=1)
    return const, np.ascontiguousarray(rope, dtype=np.float32)


def column_order():
    gdn = 4 * QK_COLS + 16
    mla = Q_RANK + KV_RANK + MLA_ROPE + H * MLA_V
    a, b = gdn, gdn + mla
    misc = np.full(P, -1)
    misc[0:16] = np.arange(4 * QK_COLS, gdn)
    misc[KR0:KR0 + MLA_ROPE] = a + Q_RANK + KV_RANK + np.arange(MLA_ROPE)
    qkv = np.concatenate([QK_COLS + np.arange(QK_COLS), np.arange(QK_COLS), 2 * QK_COLS + np.arange(QK_COLS)])
    za = 3 * QK_COLS + np.arange(QK_COLS)
    return np.concatenate([misc, qkv, za, a + np.arange(Q_RANK + KV_RANK),
                           a + Q_RANK + KV_RANK + MLA_ROPE + np.arange(H * MLA_V), b + np.arange(1024)])


def kernel(x, c, ctx, c_ctx, ada_w, ada_b, pre_gain, post_gain, w_in, gdn_conv, gdn_a_log, gdn_dt_bias,
           gdn_out_gain, mla_q_gain, mla_w_uq, mla_kv_gain, mla_w_ukv, diff_lambda, diff_sub_gain, w_out):
    import concourse.bacc as _bacc
    from concourse.bass_utils import run_bass_kernel_spmd as _run

    f = lambda a: np.asarray(a)
    tiles = lambda v: f(v).reshape(-1, P).T
    spread = lambda v: np.broadcast_to(f(v).reshape(1, -1), (P, f(v).size))
    const, rope = constants()
    conv = f(gdn_conv)[0].T.reshape(3, H, P, CONV_W)[[1, 0, 2]].transpose(2, 0, 1, 3).reshape(P, -1)
    cols = np.concatenate([
        np.stack([tiles(c), tiles(c_ctx)], axis=2).reshape(P, -1), tiles(ada_b[0]), tiles(pre_gain[0]),
        tiles(post_gain[0]), conv, tiles(gdn_out_gain[0]), tiles(mla_q_gain[0]), tiles(mla_kv_gain[0]),
        np.tile(f(diff_sub_gain)[0], 2).reshape(P, 1), spread(gdn_a_log[0]), spread(gdn_dt_bias[0]),
        spread(diff_lambda[0]), (np.arange(P)[:, None] // 32 == np.arange(4)).astype(np.float32)], axis=1)
    order = column_order()
    wi = np.zeros((D, len(order)), f(w_in).dtype)
    wi[:, order >= 0] = f(w_in)[0][:, order[order >= 0]]
    arrays = {
        "x": f(x)[0], "ctx": f(ctx)[0], "cols": cols, "const": const, "rope": rope,
        "ada_w": f(ada_w)[0].reshape(KD, P, 3, D).transpose(2, 1, 0, 3),
        "w_in": wi.reshape(KD, P, len(TILES), P).transpose(2, 1, 0, 3),
        "w_uq": f(mla_w_uq)[0].reshape(2, P, -1).transpose(1, 0, 2), "w_ukv": f(mla_w_ukv)[0],
        "w_out": f(w_out)[0].reshape(KD, P, D),
    }
    nc = _bacc.Bacc("TRN2", target_bir_lowering=False, num_devices=1)
    args, feeds = [], {}
    for name, a in arrays.items():
        a = np.ascontiguousarray(a)
        feeds[f"in_{name}"] = a
        args.append(nc.dram_tensor(f"in_{name}", a.shape, mybir.dt.from_np(a.dtype), kind="ExternalInput").ap())
    out = nc.dram_tensor("out_0", (LAT, D), F32, kind="ExternalOutput").ap()
    hybrid_block(nc, *args, out)
    r = _run(nc, [feeds], core_ids=[0])
    return r.results[0]["out_0"].reshape(1, LAT, D)
```

```python
import math
from contextlib import ExitStack

import numpy as np

import concourse.bass as bass
from concourse import mybir

F32 = mybir.dt.float32
F32R = mybir.dt.float32r
ALU = mybir.AluOpType
ACT = mybir.ActivationFunctionType
AX = mybir.AxisListType

P = 128
D = 1024
KD = D // P
LAT, CTX = 1024, 256
TOK = LAT + CTX
NT = TOK // P
NLAT = LAT // P
SEG = 512
H = 4
DK = 128
QK_COLS = H * DK
CONV_W = 5
EPS = 1e-6
GRID_W = 64
ROPE_BASE = 10000.0
MLA_NOPE, MLA_ROPE, MLA_V = 64, 32, 64
MLA_QK = MLA_NOPE + MLA_ROPE
MLA_SCALE = MLA_QK ** -0.5
Q_RANK, KV_RANK = 256, 128
DIFF_QK, DIFF_V = 32, 64
DIFF_SCALE = DIFF_QK ** -0.5
LAM_INIT = 0.8 - 0.6 * math.exp(0.0)
NEG = -1e30

GDN_TILES = ["misc"] + ["k"] * H + ["q"] * H + ["v"] * H
REST_TILES = ["cq"] * 2 + ["ckv"] + ["dq"] * 2 + ["dk"] * 2 + ["dv"] * 2 + ["za"] * 4 + ["zb"] * 2 + ["dz"] * 2
TILES = GDN_TILES + REST_TILES
LAT_ONLY = {"q", "za", "cq", "zb", "dq", "dz"}
W_RING = 3

GATES_AT = 7
KR0 = 64
LEVELS = [1 << i for i in range(7)]

COLS = {}
_at = 0
for _n, _c in (("c", 16), ("ada_b", 24), ("pre", 8), ("post", 8), ("conv", 60), ("og", 1), ("qg", 2),
               ("kvg", 1), ("sg", 1), ("alog", 8), ("dt", 8), ("lam", 128)):
    COLS[_n] = (_at, _c)
    _at += _c
NCOLS = _at
CONSTS = ["ident", "triu", "tril", "ones", "swap", "neg_f", "neg_b"] + [f"sib{b}" for b in LEVELS] + \
    [f"alt{b}" for b in LEVELS[1:]]


def segments(n):
    return [(s, min(SEG, n - s)) for s in range(0, n, SEG)]


def hybrid_block(nc, x, ctx_in, cols_d, const_d, rope_d, ada_w, w_in, w_uq, w_ukv, w_out, out):
    es = ExitStack()
    with es:
        def sb(name, shape):
            return es.enter_context(nc.sbuf_tensor(name, shape, F32))

        def sem(name):
            return es.enter_context(nc.semaphore(name))

        def need(eng, s, n):
            if n > 0:
                eng.wait_ge(s, n)

        ps = es.enter_context(nc.psum_tensor("ps", [P, 8, SEG], F32))
        hT_spill = nc.dram_tensor("hT_spill", [P, KD * TOK], F32, kind="Internal").ap()
        dq_spill = nc.dram_tensor("dq_spill", [2, P, LAT], F32, kind="Internal").ap()
        dk_spill = nc.dram_tensor("dk_spill", [2, P, TOK], F32, kind="Internal").ap()
        kr_spill = nc.dram_tensor("kr_spill", [MLA_ROPE, TOK], F32, kind="Internal").ap()

        cols = sb("cols", [P, NCOLS])
        const = sb("const", [P, len(CONSTS), P])
        GP = sb("GP", [P, D])
        ARENA_KB = 184
        arena_at = -(-nc.sbuf_base // 32) * 32
        arena = sb("arena", [P, ARENA_KB * 256])

        def view(kb, *shape):
            n = int(np.prod(shape))
            lo = int(kb * 256)
            assert lo + n <= ARENA_KB * 256
            v = arena[:, lo:lo + n]
            if len(shape) == 2:
                v = v.rearrange("p (a b) -> p a b", b=shape[1])
            if len(shape) == 3:
                v = v.rearrange("p (a b c) -> p a b c", b=shape[1], c=shape[2])
            return v

        def rounded(name, kb, *shape):
            n = int(np.prod(shape))
            t = nc.alloc_sbuf_tensor_at(name, [P, n], F32R, offset=arena_at + kb * 1024)
            return t[:, :].rearrange("p (a b) -> p a b", b=shape[1]) if len(shape) == 2 else t[:, :]

        def col(name, i=0, n=1):
            return cols[:, COLS[name][0] + i:COLS[name][0] + i + n]

        def cst(name):
            return const[:, CONSTS.index(name), :]

        def heads(ap):
            return ap.unsqueeze(1).broadcast_to([P, H, P])

        def per_head(ap):
            return ap.unsqueeze(2).broadcast_to([P, H, P])

        ident, ones = cst("ident"), cst("ones")
        small = sb("small", [P, 16 + 16 + 48 + 16 + 8 + 2 * NT + 6])
        _o = [0]

        def take(n):
            _o[0] += n
            return small[:, _o[0] - n:_o[0]]
        cs = take(16)
        cs_e = take(16)
        mod = take(48)
        mA = take(16)
        gp_col = take(8)
        ssq = take(NT)
        rstd = take(NT)
        eps_col = take(1)
        one_col = take(1)
        eps_q = take(1)
        eps_k = take(1)
        og_half = take(1)

        hT = view(0, KD, TOK)
        ada = [view(40, KD, D), view(72, KD, D), view(72, KD, D)]
        xin = view(104, NT, D)
        junk = view(144, D)
        gp_diag = view(156, KD, P)
        mod_row = view(168, D)
        w_ring = view(172, W_RING, KD, P)

        kT = view(40, H, TOK)
        qT = view(60, H, LAT)
        k_tok = view(76, NT, H * P)
        v_tok = view(96, NT, H * P)
        W0 = 116 * 256
        RAW_W, CV_W = LAT + CTX + 8, LAT + CTX + 4
        CTX_RAW, CTX_CV = LAT + 6, LAT + 4

        def words(off, n):
            return arena[:, W0 + off:W0 + off + n]
        raw = [words(i * RAW_W, RAW_W) for i in range(2)]
        cv = [words(2 * RAW_W + i * CV_W, CV_W) for i in range(2)]
        tanh_buf = words(2 * RAW_W + 2 * CV_W, CV_W)
        sqb = [words(2 * RAW_W + 3 * CV_W + i * TOK, TOK) for i in range(2)]
        yv = [words(2 * RAW_W + 3 * CV_W + (2 + i) * TOK, TOK) for i in range(2)]
        misc = view(162, TOK)

        gates = sb("gates", [P, 16 * NT + 13 * 8 * NT])
        lg = gates[:, 0:16 * NT].rearrange("p (c n) -> p c n", n=16)

        def gate(i):
            lo = 16 * NT + i * 8 * NT
            return gates[:, lo:lo + 8 * NT].rearrange("p (c n) -> p c n", n=8)
        xa, na, en, sp, g_, beta, gam, tot, dtk, EG, EKD, GL, bek = [gate(i) for i in range(13)]
        ea = sb("ea", [P, 8])

        Q_all = view(0, NT, H * P)
        QK = view(116, 2 * NLAT, H * P)
        INVERSES = [[0, 1, 2, 3], [4, 5, 6], [7, 8, 9]]

        def inv_buf(b):
            return {"gbc": view(b, 8, P), "M": view(b, H, P), "N": view(b + 2, H, P), "tmp": view(b, H, P),
                    "At": view(b + 4, H, P), "E": view(b + 6, 8, P), "P": view(b + 6, H, P), "X": view(b + 8, H, P)}
        iv = [inv_buf(b) for b in (20, 30, 148, 158)]

        def inv_index(g, lev, s):
            return 6 * sum(len(q) for q in INVERSES[:g]) + lev * len(INVERSES[g]) + s
        S = view(20, 2, H * P)
        Sg = view(24, 2, H * P)
        R = view(28, 2, H * P)
        Vn = view(32, 2, H * P)
        Vs = view(36, 2, H * P)
        t2 = view(164, 2, H * P)
        Um = view(168, 2, H * P)
        o_acc = view(148, NLAT, H * P)
        o_sq = view(40, NLAT * H, P)
        o_stat = sb("o_stat", [P, 2 * NLAT * H])

        mixT = view(40, 8, LAT)
        cq = view(72, 2, LAT)
        ckv = view(80, TOK)
        krT = view(85, TOK)
        dq = view(90, 2, LAT)
        dk = view(98, 2, TOK)
        dv_tok = view(108, NT, H * DIFF_V)
        z_half = view(118, 2, LAT)
        zbuf = view(126, 2, LAT)
        dvT = view(134, TOK)
        rbuf = view(139, LAT)
        uq_sb = view(143, 2, H * MLA_QK)
        ukv_sb = view(146, H * P)
        rope = view(164, 2, LAT)
        QTm = view(0, H, LAT)
        KTm = view(16, H, TOK)
        V_tok = view(148, NT, H * MLA_V)
        cq_sq = view(118, 2, LAT)
        kv_sq = view(126, TOK)
        cq_rn = view(118, LAT)
        kv_rn = view(126, TOK)
        kr_buf = view(122, LAT)

        prob = view(118, 4, TOK)
        wT = view(138, 2, TOK)
        o_tok = view(158, 2, 2 * H * 64)
        d_sq = view(162, H, 64)
        KST_KB = [98, 103, 164, 169, 174, 179, 72, 77]
        QST_KB = [36, 86]
        k_stage = [view(kb, TOK) for kb in KST_KB]
        k_stack = [rounded(f"k_stack{g}", kb, TOK) for g, kb in enumerate(KST_KB)]
        q_stage = [view(kb, 2 * H, P) for kb in QST_KB]
        q_stack = [rounded(f"q_stack{i}", kb, 2 * H, P) for i, kb in enumerate(QST_KB)]
        k_hi = rounded("k_hi", 90, TOK)
        q_hi = [rounded("q_hi0", 133, 2 * H, P), rounded("q_hi1", 82, 2 * H, P)]
        NSET = NLAT * 3 * H
        stat = sb("stat", [P, 2 * NSET + 4 * NLAT * 2 * H + 2 * NLAT * H + 16])
        nmax = stat[:, 0:NSET]
        lsum = stat[:, NSET:2 * NSET]
        _s = 2 * NSET
        rinv = stat[:, _s:_s + NLAT * 8]
        rinv1 = stat[:, _s + NLAT * 8:_s + NLAT * 16]
        coef = stat[:, _s + NLAT * 16:_s + NLAT * 24]
        dss = stat[:, _s + NLAT * 24:_s + NLAT * 28]
        drs = stat[:, _s + NLAT * 28:_s + NLAT * 32]
        lamt = stat[:, _s + NLAT * 32:_s + NLAT * 32 + 8]
        lam_p = sb("lam_p", [P, 64])

        wo_sb = [view(164 + 4 * k, D) if k < 5 else view(72 + 4 * (k - 5), D) for k in range(KD)]
        y_buf = view(118, 2, D)
        x_buf = view(126, 2, D)
        y_junk = view(134, D)
        yst = sb("yst", [P, 2 * NLAT])

        names = """cols_in const_in rope_in uq_in x_in0 x_in1 x_in2 ada_in0 ada_in1 ada_in2 w_in0 w_in1 w_in2
        setup c_exp c_one c_rec c_silu ada_mm row_read mod_turn mod_add mod_A gp_done ssq_done rs_done xn_done xT_mm hT_dve hT_act
        diag_done gp_mm GP_done in_mm evac_done conv_step tanh_done silu_done sq_done aux_mm aux_read rn_done
        fin_done pad_done spill spill_kr gt_d gt_a
        gbc_done gb_mm pre_mm ex_done e_done pool_w at_done qk_done q_step tr_mm p_done mn_done x_mm xs_done pq_mm upd
        s_init um_done sg_done ks_mm qs_mm r_done tr4_mm vv_done ds_mm qkv_mm s_upd t2_done o1_done oa_done
        osq_done ostat_d ostat_a o_ready hT_back0 hT_back1 kr_back in2_mm z_tanh z_done c_evac aux2_mm aux2_read norm_read
        rope_done lam_d lam_a
        n_sq n_exp n_done mq_mm mq_ev mq_swap mq_t mq_c mq_done mk_mm mk_ev mk_rope mv_mm mv_ev kr_c kr_done
        q_spill k_spill q_in0 q_in1 k_in0 k_in1 k_in2 k_in3 k_in4 k_in5 k_in6 k_in7 kh_done kst_done kup_done
        qh_done qst_done sc_mm mx_done p_exp l_inv w_done wt_mm wt_ev pv_mm pv_ev d_sqd d_red d_ln d_exp d_norm ot_mm mix_b
        wo_in y_mm y_sq y_ln y_exp y_scaled x2_in0 x2_in1 y_out0 y_out1 y_added""".split()
        sm = {n: sem(n) for n in names}
        x_in = [sm[f"x_in{i}"] for i in range(3)]
        ada_in = [sm[f"ada_in{i}"] for i in range(3)]
        w_in_s = [sm[f"w_in{i}"] for i in range(W_RING)]
        x2_in = [sm["x2_in0"], sm["x2_in1"]]
        y_out = [sm["y_out0"], sm["y_out1"]]

        xv = x.rearrange("(t p) d -> t p d", p=P)
        cv_d = ctx_in.rearrange("(t p) d -> t p d", p=P)
        out_v = out.rearrange("(t p) d -> t p d", p=P)

        NG = len(GDN_TILES)
        GROUPS = [(0, 4), (4, 4), (8, 2)]

        def ntok(kind):
            return LAT if kind in LAT_ONLY else TOK

        def aux_jobs():
            jobs = []
            for i in range(NG + 3):
                if 0 <= i - 2 < NG and GDN_TILES[i - 2] in "qk":
                    for s, w in segments(ntok(GDN_TILES[i - 2])):
                        jobs.append(("ones", i - 2, s, w, i))
                if i == GATES_AT:
                    jobs.append(("gates", -9, 0, 0, i))
                t = i - 3
                if 0 <= t < NG and GDN_TILES[t] == "misc":
                    jobs.append(("logits", t, 0, TOK, i))
                if 0 <= t < NG and GDN_TILES[t] in "kv":
                    for s, w in segments(TOK):
                        jobs.append(("turn", t, s, w, i))
            return jobs
        AUX = aux_jobs()

        def aux_at(i, what):
            return [(j, a) for j, a in enumerate(AUX) if a[4] == i and a[0] in what]

        def head_of(t):
            return (t - 1) % H

        def y_of(t):
            kind = GDN_TILES[t]
            return {"q": lambda: qT[:, head_of(t), :], "k": lambda: kT[:, head_of(t), :],
                    "v": lambda: yv[t % 2]}[kind]()

        QKI = [t for t in range(NG) if GDN_TILES[t] in "qk"]
        NORM_AT = 4
        AUX2 = []
        for j in range(len(REST_TILES) + 1):
            if j >= 1:
                kind = REST_TILES[j - 1]
                if kind in ("za", "dq", "dk"):
                    for s, w in segments(LAT):
                        AUX2.append((kind, j - 1, s, w, j))
                if kind == "dv":
                    for s, w in segments(TOK):
                        AUX2.append((kind, j - 1, s, w, j))
                if j == NORM_AT:
                    AUX2 += [("sum_q", -1, s, w, j) for s, w in segments(LAT)]
                    AUX2 += [("sum_kv", -1, s, w, j) for s, w in segments(TOK)]
                    AUX2 += [("swap_kr", -1, s, w, j) for s, w in segments(LAT)]

        def by_act(e):
            return e[0] in ("sum_q", "sum_kv")

        def wait_read2(eng, a):
            if a >= 0:
                mine = [e for e in AUX2[:a + 1] if by_act(e) == by_act(AUX2[a])]
                eng.wait_ge(sm["norm_read"] if by_act(AUX2[a]) else sm["aux2_read"], len(mine))
        first_of = {k: REST_TILES.index(k) for k in set(REST_TILES)}
        ROPED = [j for j, k in enumerate(REST_TILES) if k in ("dq", "dk")]
        ZT = [j for j, k in enumerate(REST_TILES) if k[0] == "z" or k == "dz"]
        CT = [j for j, k in enumerate(REST_TILES) if j not in ZT]

        order = [[8, 9] + list(range(8)), [9, 8] + list(range(7, -1, -1))]
        LATSTEP = [[m for m in range(20) if order[m % 2][m // 2] < NLAT]][0]

        UNITS = [(qb, u) for qb in range(NLAT) for i in range(H) for u in (i, H + i)]

        def sets_of(n):
            qb, u = UNITS[n]
            st = 3 * (qb * H + u % H)
            return [st] if u < H else [st + 1, st + 2]
        KSEG = segments(TOK)
        NU = len(UNITS)
        PAIRS = NU // 2

        block = es.enter_context(nc.Block())

        @block.sync
        def _(sp):
            def fetch_keys(g):
                rows_of = dk_spill.rearrange("t p c -> (t p) c")[32 * g:32 * g + 32, :]
                for r in range(4):
                    sp.dma_start(k_stage[g][32 * r:32 * r + 32, :], rows_of).then_inc(sm[f"k_in{g}"], 16)

            def fetch_queries(qb):
                src = dq_spill.rearrange("t p c -> (t p) c").rearrange("(g x) c -> x g c", x=32)
                for r in range(4):
                    sp.dma_start(q_stage[qb % 2][32 * r:32 * r + 32, :, :], src[:, :, qb * P:(qb + 1) * P]
                                 ).then_inc(sm[f"q_in{qb % 2}"], 16)

            sp.dma_start(cols[:, :], cols_d).then_inc(sm["cols_in"], 16)
            sp.dma_start(const[:, :, :], const_d).then_inc(sm["const_in"], 16)
            sp.dma_start(ada[0], ada_w[0]).then_inc(ada_in[0], 16)
            sp.dma_start(ada[1], ada_w[1]).then_inc(ada_in[1], 16)
            for gi, (t0, n) in enumerate(GROUPS):
                for t in range(t0, t0 + n):
                    sp.dma_start(xin[:, t, :], xv[t] if t < NLAT else cv_d[t - NLAT]).then_inc(x_in[gi], 16)
            for i in range(W_RING):
                sp.dma_start(w_ring[:, i, :, :], w_in[i]).then_inc(w_in_s[i], 16)
            sp.wait_ge(sm["ada_mm"], 2)
            sp.dma_start(ada[2], ada_w[2]).then_inc(ada_in[2], 16)
            for i in range(W_RING, NG):
                sp.wait_ge(sm["in_mm"], i - W_RING + 1)
                sp.dma_start(w_ring[:, i % W_RING, :, :], w_in[i]).then_inc(w_in_s[i % W_RING], 16)
            sp.wait_ge(sm["hT_dve"], 12)
            sp.wait_ge(sm["hT_act"], 12)
            sp.dma_start(hT_spill, arena[:, 0:KD * TOK]).then_inc(sm["spill"], 16)
            sp.wait_ge(sm["evac_done"], 1)
            sp.dma_start(kr_spill, misc[KR0:KR0 + MLA_ROPE, :]).then_inc(sm["spill_kr"], 16)
            for i in range(NG, NG + W_RING):
                sp.wait_ge(sm["in_mm"], min(i - W_RING + 1, NG))
                sp.dma_start(w_ring[:, i % W_RING, :, :], w_in[i]).then_inc(w_in_s[i % W_RING], 16)
            half = KD // 2 * TOK
            sp.wait_ge(sm["spill"], 16)
            sp.wait_ge(sm["spill_kr"], 16)
            sp.wait_ge(sm["um_done"], 20)
            sp.dma_start(arena[:, 0:half], hT_spill[:, 0:half]).then_inc(sm["hT_back0"], 16)
            sp.wait_ge(sm["s_upd"], 20)
            sp.wait_ge(sm["o1_done"], 16)
            sp.dma_start(arena[:, half:2 * half], hT_spill[:, half:2 * half]).then_inc(sm["hT_back1"], 16)
            sp.wait_ge(sm["oa_done"], 16)
            sp.dma_start(rope, rope_d).then_inc(sm["rope_in"], 16)
            sp.dma_start(krT[KR0:KR0 + MLA_ROPE, :], kr_spill).then_inc(sm["kr_back"], 16)
            sp.dma_start(uq_sb, w_uq).then_inc(sm["uq_in"], 16)
            sp.dma_start(ukv_sb, w_ukv).then_inc(sm["uq_in"], 16)
            for i in range(NG + W_RING, len(TILES)):
                sp.wait_ge(sm["in2_mm"], i - W_RING + 1 - NG)
                sp.dma_start(w_ring[:, i % W_RING, :, :], w_in[i]).then_inc(w_in_s[i % W_RING], 16)
                if i == NG + W_RING + first_of["za"] + 1:
                    sp.wait_ge(sm["rope_done"], 2 * len(ROPED))
                    sp.dma_start(dq_spill.rearrange("t p c -> p t c"), dq).then_inc(sm["q_spill"], 16)
                    sp.dma_start(dk_spill.rearrange("t p c -> p t c"), dk).then_inc(sm["k_spill"], 16)
                    sp.wait_ge(sm["q_spill"], 16)
                    sp.wait_ge(sm["k_spill"], 16)
                    fetch_keys(0)
                    fetch_keys(1)
            sp.wait_ge(sm["in2_mm"], len(REST_TILES))
            fetch_queries(0)
            fetch_keys(4)
            fetch_keys(5)
            sp.wait_ge(sm["mq_done"], H)
            fetch_keys(2)
            fetch_keys(3)
            sp.wait_ge(sm["mv_mm"], 5)
            sp.wait_ge(sm["mk_mm"], H)
            fetch_keys(6)
            fetch_keys(7)
            sp.wait_ge(sm["mk_rope"], H)
            for qb in range(1, NLAT):
                if qb >= 2:
                    sp.wait_ge(sm["sc_mm"], 3 * H * (qb - 1))
                fetch_queries(qb)
            sp.wait_ge(sm["sc_mm"], NSET)
            for k in range(KD):
                sp.dma_start(wo_sb[k], w_out[k]).then_inc(sm["wo_in"], 16)
            for t in range(NLAT):
                if t == 0:
                    sp.wait_ge(sm["wt_mm"], 3 * len(UNITS))
                if t >= 2:
                    sp.wait_ge(sm["y_added"], t - 1)
                sp.dma_start(x_buf[:, t % 2, :], xv[t]).then_inc(x2_in[t % 2], 16)
                if t >= 1:
                    sp.wait_ge(sm["y_added"], t)
                    sp.dma_start(out_v[t - 1], y_buf[:, (t - 1) % 2, :]).then_inc(y_out[(t - 1) % 2], 16)
            sp.wait_ge(sm["y_added"], NLAT)
            sp.dma_start(out_v[NLAT - 1], y_buf[:, (NLAT - 1) % 2, :]).then_inc(y_out[(NLAT - 1) % 2], 16)
            sp.wait_ge(y_out[0], 16 * (NLAT // 2))
            sp.wait_ge(y_out[1], 16 * (NLAT // 2))

        def wait_aux(pe, j):
            strict = "gates" in (AUX[j][0], AUX[j - 1][0], AUX[j - 2][0])
            need(pe, sm["aux_read"], j if strict else j - 1)

        def turn_x(pe, gi):
            t0, n = GROUPS[gi]
            for k in range(KD):
                q = gi * KD + k
                if k == 0:
                    pe.wait_ge(sm["const_in"], 16)
                    pe.wait_ge(sm["xn_done"], t0 + n)
                if q >= 4:
                    pe.wait_ge(sm["hT_dve"] if q % 2 == 0 else sm["hT_act"], (q - 4) // 2 + 1)
                for t in range(n):
                    last = nc.tensor.transpose(ps[:, 4 + q % 4, t * P:(t + 1) * P],
                                               xin[:, t0 + t, k * P:(k + 1) * P], ident)
                last.then_inc(sm["xT_mm"], 1)

        def project(pe, i, n, free_sem, free_n, done, parity=None, late_half=None):
            parity = i % 2 if parity is None else parity
            pe.wait_ge(w_in_s[i % W_RING], 16 * (i // W_RING + 1))
            if free_sem is not None:
                need(pe, free_sem, free_n)
            for s, w in segments(n):
                for k in range(KD):
                    if late_half is not None and s == 0 and k == KD // 2:
                        pe.wait_ge(late_half, 16)
                    last = nc.tensor.matmul(ps[:, 3 * parity + s // SEG, 0:w], w_ring[:, i % W_RING, k, :],
                                            hT[:, k, s:s + w], start=(k == 0), stop=(k == KD - 1))
            last.then_inc(done, 1)

        def swap_q(pe, h):
            pe.wait_ge(sm["mq_ev"], h + 1)
            if h == 0:
                wait_read2(pe, len(AUX2) - 1)
                wait_read2(pe, len(AUX2) - 2)
            need(pe, sm["mq_t"], h)
            for s, w in segments(LAT):
                last = nc.tensor.matmul(ps[KR0:KR0 + 32, 6 + s // SEG, 0:w],
                                        cst("swap")[KR0:KR0 + 32, KR0:KR0 + 32],
                                        QTm[KR0:KR0 + 32, h, s:s + w], start=True, stop=True)
            last.then_inc(sm["mq_swap"], 1)

        @block.tensor
        def _(pe):
            mm, tr = nc.tensor.matmul, nc.tensor.transpose

            pe.wait_ge(sm["c_silu"], 1)

            def modulate(piece):
                pe.wait_ge(ada_in[piece], 16)
                need(pe, sm["row_read"], piece)
                b = 6 if piece == 2 else 0
                for k in range(KD):
                    for i in range(2):
                        last = mm(ps[64 * i:64 * i + 2, b + i, :], cs[:, 2 * k:2 * k + 2],
                                  ada[piece][:, k, i * SEG:(i + 1) * SEG], start=(k == 0), stop=(k == KD - 1))
                last.then_inc(sm["ada_mm"], 1)

            def turn_mod(piece):
                if piece == 0:
                    pe.wait_ge(sm["const_in"], 16)
                pe.wait_ge(sm["row_read"], piece + 1)
                need(pe, sm["mod_add"], piece)
                b = 6 if piece == 2 else 2
                for j in range(KD):
                    r = 64 * (j // 4)
                    last = tr(ps[:, b + j // 4, 2 * (j % 4):2 * (j % 4) + 2], mod_row[r:r + 2, j * P:(j + 1) * P],
                              ident[r:r + 2, r:r + 2])
                last.then_inc(sm["mod_turn"], 1)

            modulate(0)
            turn_mod(0)
            modulate(1)
            turn_mod(1)
            for gi in range(3):
                turn_x(pe, gi)

            for i in range(NG + 3):
                if i < NG:
                    if i == 0:
                        pe.wait_ge(sm["hT_dve"], 12)
                        pe.wait_ge(sm["hT_act"], 12)
                    project(pe, i, ntok(GDN_TILES[i]), sm["evac_done"], i - 1, sm["in_mm"])
                if i == 1:
                    modulate(2)
                if i == 2:
                    turn_mod(2)
                if i == 3:
                    pe.wait_ge(sm["diag_done"], 1)
                    for b in range(2):
                        last = mm(ps[:, 6 + b, :], ones, gp_diag[:, 4 * b:4 * b + 4, :], start=True, stop=True)
                    last.then_inc(sm["gp_mm"], 1)
                    pe.wait_ge(sm["GP_done"], 1)
                for j, (_, t, s, w, _) in aux_at(i, ("ones",)):
                    if s == 0:
                        pe.wait_ge(sm["sq_done"], QKI.index(t) + 1)
                    wait_aux(pe, j)
                    mm(ps[:, 6 + j % 2, 0:w], ones, sqb[t % 2][:, s:s + w], start=True,
                       stop=True).then_inc(sm["aux_mm"], 1)
                for j, (what, t, s, w, _) in aux_at(i, ("gates", "turn", "logits")):
                    wait_aux(pe, j)
                    bank = 6 + j % 2
                    if what == "gates":
                        pe.wait_ge(sm["gt_d"], 4)
                        g8 = ps[:, bank, 0:8 * NT].rearrange("p (c n) -> p c n", n=8)
                        mm(g8[:, :, 0:4], cst("triu"), g_[:, :, 0:4], start=True, stop=True)
                        mm(g8[:, :, 4:8], cst("tril"), g_[:, :, 4:8], start=True, stop=True)
                        last = mm(ps[:, bank, 128:128 + 8 * NT].rearrange("p (c n) -> p c n", n=8), ones, g_,
                                  start=True, stop=True)
                    elif what == "logits":
                        for c in range(NT):
                            last = tr(ps[:, bank, 16 * c:16 * c + 16], misc[0:16, c * P:(c + 1) * P],
                                      ident[0:16, 0:16])
                    else:
                        if s == 0 and GDN_TILES[t] == "k":
                            pe.wait_ge(sm["fin_done"], QKI.index(t) + 1)
                        if s == 0:
                            pe.wait_ge(sm["silu_done"], t)
                        src = y_of(t)
                        for c in range(w // P):
                            last = tr(ps[:, bank, c * P:(c + 1) * P], src[:, s + c * P:s + (c + 1) * P], ident)
                    last.then_inc(sm["aux_mm"], 1)

            for g, group in enumerate(INVERSES):
                for s, c in enumerate(group):
                    pe.wait_ge(sm["gbc_done"], c + 1)
                    if g == 0:
                        pe.wait_ge(sm["aux_read"], len(AUX))
                        pe.wait_ge(sm["evac_done"], NG)
                    for d in range(2):
                        for h in range(H):
                            last = mm(ps[:, 2 * s + d, h * P:(h + 1) * P], iv[s]["gbc"][:, 4 * d + h, :],
                                      cst("triu") if d == 0 else cst("tril"), start=True, stop=True)
                    last.then_inc(sm["gb_mm"], 1)
                for s, c in enumerate(group):
                    cc = slice(c * P, (c + 1) * P)
                    pe.wait_ge(sm["ex_done"], 8 * (c + 1))
                    for h in range(H):
                        last = mm(ps[:, 2 * s, h * P:(h + 1) * P], kT[:, h, cc], kT[:, h, cc], start=True, stop=True)
                    if c < NLAT:
                        for h in range(H):
                            last = mm(ps[:, 2 * s + 1, h * P:(h + 1) * P], kT[:, h, cc], qT[:, h, cc],
                                      start=True, stop=True)
                    last.then_inc(sm["pre_mm"], 1)
                for s, c in enumerate(group):
                    pe.wait_ge(sm["q_step"], 2 * (c + 1))
                    for h in range(H):
                        last = tr(ps[:, 2 * s, h * P:(h + 1) * P], Q_all[:, c, h * P:(h + 1) * P], ident)
                    last.then_inc(sm["tr_mm"], 1)
                for lev in range(6):
                    for s, c in enumerate(group):
                        n = inv_index(g, lev, s)
                        pe.wait_ge(sm["mn_done"], 2 * n + 1)
                        for h in range(H):
                            last = mm(ps[:, 2 * s, h * P:(h + 1) * P], iv[s]["At"][:, h, :], iv[s]["M"][:, h, :],
                                      start=True, stop=True)
                        last.then_inc(sm["x_mm"], 1)
                    for s, c in enumerate(group):
                        n = inv_index(g, lev, s)
                        pe.wait_ge(sm["xs_done"], n + 1)
                        pe.wait_ge(sm["mn_done"], 2 * n + 2)
                        if lev < 5:
                            for h in range(H):
                                last = mm(ps[:, 2 * s, h * P:(h + 1) * P], iv[s]["N"][:, h, :], iv[s]["X"][:, h, :],
                                          start=True, stop=True)
                            last.then_inc(sm["pq_mm"], 1)
                        if lev == 0:
                            pe.wait_ge(sm["qk_done"], 2 * min(c + 1, NLAT))
                        for h in range(H):
                            last = mm(ps[:, 2 * s + 1, h * P:(h + 1) * P], iv[s]["X"][:, h, :], iv[s]["N"][:, h, :],
                                      start=True, stop=True)
                        last.then_inc(sm["pq_mm"], 1 if lev < 5 else 2)

            pe.wait_ge(sm["upd"], 2 * 60)
            for i in range(NT):
                for d in range(2):
                    m = 2 * i + d
                    c = order[d][i]
                    cc = slice(c * P, (c + 1) * P)
                    if i == 0:
                        pe.wait_ge(sm["s_init"], 2)
                    need(pe, sm["s_upd"], m - 1)
                    lat_before = len([q for q in LATSTEP if q <= m - 2])
                    need(pe, sm["o1_done"], lat_before)
                    for h in range(H):
                        last = mm(ps[:, 4 * d, h * P:(h + 1) * P], kT[:, h, cc], S[:, d, h * P:(h + 1) * P],
                                  start=True, stop=True)
                    last.then_inc(sm["ks_mm"], 1)
                    if c < NLAT:
                        need(pe, sm["t2_done"], lat_before)
                        for h in range(H):
                            last = mm(ps[:, 4 * d + 3, h * P:(h + 1) * P], qT[:, h, cc], S[:, d, h * P:(h + 1) * P],
                                      start=True, stop=True)
                        last.then_inc(sm["qs_mm"], 1)
                for d in range(2):
                    m = 2 * i + d
                    pe.wait_ge(sm["r_done"], 2 * (m + 1))
                    pe.wait_ge(sm["um_done"], m + 1)
                    for h in range(H):
                        last = mm(ps[:, 4 * d + 1, h * P:(h + 1) * P], Um[:, d, h * P:(h + 1) * P],
                                  R[:, d, h * P:(h + 1) * P], start=True, stop=True)
                    last.then_inc(sm["tr4_mm"], 1)
                for d in range(2):
                    m = 2 * i + d
                    c = order[d][i]
                    pe.wait_ge(sm["vv_done"], 2 * (m + 1))
                    for h in range(H):
                        last = mm(ps[:, 4 * d + 2, h * P:(h + 1) * P], k_tok[:, c, h * P:(h + 1) * P],
                                  Vs[:, d, h * P:(h + 1) * P], start=True, stop=True)
                    last.then_inc(sm["ds_mm"], 1)
                    if c < NLAT:
                        for h in range(H):
                            last = mm(ps[:, 4 * d, h * P:(h + 1) * P], QK[:, d * NLAT + c, h * P:(h + 1) * P],
                                      Vn[:, d, h * P:(h + 1) * P], start=True, stop=True)
                        last.then_inc(sm["qkv_mm"], 1)

            NR = len(REST_TILES)
            for j in range(NR + 1):
                if j < NR:
                    if j == 0:
                        pe.wait_ge(sm["hT_back0"], 16)
                        pe.wait_ge(sm["o1_done"], 16)
                    if j >= 2:
                        if j - 2 in ZT:
                            pe.wait_ge(sm["z_done"], ZT.index(j - 2) + 1)
                        else:
                            pe.wait_ge(sm["c_evac"], CT.index(j - 2) + 1)
                    project(pe, NG + j, ntok(REST_TILES[j]), None, 0, sm["in2_mm"], parity=j % 2,
                            late_half=sm["hT_back1"] if j == 0 else None)
                for a, (kind, t, s, w, jj) in enumerate(AUX2):
                    if jj != j:
                        continue
                    wait_read2(pe, a - 2)
                    bank = 6 + a % 2
                    if kind == "za":
                        pe.wait_ge(sm["o_ready"], 1)
                        h = t - first_of["za"]
                        for c in range(w // P):
                            cc = s // P + c
                            last = tr(ps[:, bank, c * P:(c + 1) * P], o_acc[:, cc, h * P:(h + 1) * P], ident)
                    elif kind == "sum_q":
                        pe.wait_ge(sm["n_sq"], 3)
                        for k in range(2):
                            last = mm(ps[:, bank, 0:w], ones, cq_sq[:, k, s:s + w], start=(k == 0), stop=(k == 1))
                    elif kind == "sum_kv":
                        last = mm(ps[:, bank, 0:w], ones, kv_sq[:, s:s + w], start=True, stop=True)
                    elif kind == "swap_kr":
                        pe.wait_ge(sm["kr_back"], 16)
                        last = mm(ps[KR0:KR0 + 32, bank, 0:w], cst("swap")[KR0:KR0 + 32, KR0:KR0 + 32],
                                  krT[KR0:KR0 + 32, s:s + w], start=True, stop=True)
                    else:
                        pe.wait_ge(sm["c_evac"], CT.index(t) + 1)
                        if kind == "dv":
                            for c in range(w // P):
                                last = tr(ps[:, bank, c * P:(c + 1) * P], dvT[:, s + c * P:s + (c + 1) * P], ident)
                        else:
                            src = (dq if kind == "dq" else dk)[:, t - first_of[kind], :]
                            last = mm(ps[:, bank, 0:w], cst("swap"), src[:, s:s + w], start=True, stop=True)
                    last.then_inc(sm["aux2_mm"], 1)

            pe.wait_ge(sm["z_done"], len(ZT))
            pe.wait_ge(sm["n_done"], 3)
            pe.wait_ge(sm["uq_in"], 32)
            for h in range(H):
                b = 2 * (h % 2)
                need(pe, sm["mq_ev"], h - 1)
                for s, w in segments(LAT):
                    for k in range(2):
                        last = mm(ps[0:MLA_QK, b + s // SEG, 0:w], uq_sb[:, k, h * MLA_QK:(h + 1) * MLA_QK],
                                  cq[:, k, s:s + w], start=(k == 0), stop=(k == 1))
                last.then_inc(sm["mq_mm"], 1)
                if h >= 1:
                    swap_q(pe, h - 1)
            for v in range(NT // 2):
                if v < 2:
                    pe.wait_ge(sm["mq_ev"], H)
                else:
                    pe.wait_ge(sm["mv_ev"], v - 1)
                for e in range(2):
                    c = 2 * v + e
                    last = mm(ps[:, v % 2, 256 * e:256 * e + 256], ckv[:, c * P:(c + 1) * P],
                              ukv_sb.rearrange("p (h a) -> p h a", h=H)[:, :, MLA_NOPE:], start=True, stop=True)
                last.then_inc(sm["mv_mm"], 1)
            swap_q(pe, H - 1)
            for h in range(H):
                if h == 0:
                    pe.wait_ge(sm["mv_ev"], NT // 2)
                need(pe, sm["mk_ev"], h - 1)
                b = 3 * (h % 2)
                for s, w in segments(TOK):
                    last = mm(ps[0:MLA_NOPE, b + s // SEG, 0:w], ukv_sb[:, h * P:h * P + MLA_NOPE],
                              ckv[:, s:s + w], start=True, stop=True)
                last.then_inc(sm["mk_mm"], 1)

            def scores(st):
                n, e = (2 * (st // 3), 0) if st % 3 == 0 else (2 * (st // 3) + 1, st % 3 - 1)
                qb, u = UNITS[n]
                qc = slice(qb * P, (qb + 1) * P)
                if st >= 2:
                    pe.wait_ge(sm["p_exp"], st - 1)
                if st < 2:
                    pe.wait_ge(sm["mk_ev"], H)
                    pe.wait_ge(sm["mk_rope"], H)
                    pe.wait_ge(sm["mq_done"], H)
                g = 2 * (u - H) + e
                if u >= H:
                    pe.wait_ge(sm["qst_done"], 4 * (qb + 1))
                    if qb == 0:
                        pe.wait_ge(sm["kst_done"], g + 1)
                        pe.wait_ge(sm["kup_done"], g + 1)
                b = 3 * (st % 2)
                for s, w in KSEG:
                    if u < H:
                        last = mm(ps[:, b + s // SEG, 0:w], QTm[0:MLA_QK, u, qc], KTm[0:MLA_QK, u, s:s + w],
                                  start=True, stop=True)
                    else:
                        last = mm(ps[:, b + s // SEG, 0:w], q_stack[qb % 2][:, g, :], k_stack[g][:, s:s + w],
                                  start=True, stop=True)
                last.then_inc(sm["sc_mm"], 1)

            def turn_probs(n, gi):
                qb, u = UNITS[n]
                slot = sets_of(n)[0] % 4
                s, w = KSEG[gi]
                if gi == 0:
                    if u < H:
                        pe.wait_ge(sm["p_exp"], sets_of(n)[0] + 1)
                    else:
                        pe.wait_ge(sm["w_done"], qb * H + u - H + 1)
                    if n == 0:
                        pe.wait_ge(sm["mq_t"], H)
                    need(pe, sm["wt_ev"], 3 * n)
                    if n >= 13 and n % 8 == 5:
                        pe.wait_ge(sm["mix_b"], 2 * (n // 8))
                elif gi == 1:
                    need(pe, sm["pv_ev"], n - 1)
                    if n == 1:
                        pe.wait_ge(sm["wt_ev"], 2)
                else:
                    pe.wait_ge(sm["wt_ev"], 3 * n + 1)
                for c in range(w // P):
                    last = tr(ps[:, 7 if gi == 1 else 6, c * P:(c + 1) * P], prob[:, slot, s + c * P:s + (c + 1) * P],
                              ident)
                last.then_inc(sm["wt_mm"], 1)

            def pv(n):
                qb, u = UNITS[n]
                pe.wait_ge(sm["wt_ev"], min(3 * n + 5, 3 * NU))
                if n == NU - 1:
                    pe.wait_ge(sm["pv_ev"], n)
                V = V_tok if u < H else dv_tok
                h = u % H
                for c in range(NT):
                    last = mm(ps[:, 7, 0:64], wT[:, n % 2, c * P:(c + 1) * P],
                              V[:, c, h * 64:h * 64 + 64], start=(c == 0), stop=(c == NT - 1))
                last.then_inc(sm["pv_mm"], 1)

            def turn_out(qb, n):
                pe.wait_ge(sm["d_norm"], qb + 1)
                pe.wait_ge(sm["wt_ev"], 3 * n)
                for i in range(4):
                    last = tr(ps[:, 6, i * P:(i + 1) * P], o_tok[:, qb % 2, i * P:(i + 1) * P], ident)
                last.then_inc(sm["ot_mm"], 1)

            scores(0)
            for i in range(PAIRS + 1):
                if i < PAIRS:
                    scores(3 * i + 1)
                if i >= 1:
                    turn_probs(2 * i - 1, 0)
                    turn_probs(2 * i - 1, 1)
                if i < PAIRS:
                    scores(3 * i + 2)
                if i >= 1:
                    turn_probs(2 * i - 1, 2)
                    pv(2 * i - 2)
                if i < PAIRS:
                    turn_probs(2 * i, 0)
                    turn_probs(2 * i, 1)
                if i + 1 < PAIRS:
                    scores(3 * i + 3)
                if i < PAIRS:
                    turn_probs(2 * i, 2)
                if i >= 1:
                    pv(2 * i - 1)
                if i >= 6 and i % H == 2:
                    turn_out(i // H - 1, 2 * i + 1)

            for t in range(NLAT):
                if t == 0:
                    pe.wait_ge(sm["wo_in"], 16 * KD)
                    pe.wait_ge(sm["mix_b"], 2 * (NLAT - 1))
                    pe.wait_ge(sm["p_exp"], NSET)
                if t == 1:
                    turn_out(NLAT - 1, NU)
                if t == NLAT - 1:
                    pe.wait_ge(sm["mix_b"], 2 * NLAT)
                b = 2 * (t % 2)
                need(pe, sm["y_scaled"], t - 1)
                for i in range(2):
                    for k in range(KD):
                        last = mm(ps[:, b + i, :], mixT[:, k, t * P:(t + 1) * P], wo_sb[k][:, i * SEG:(i + 1) * SEG],
                                  start=(k == 0), stop=(k == KD - 1))
                last.then_inc(sm["y_mm"], 1)

        @block.scalar
        def _(act):
            A = nc.scalar.activation
            act.wait_ge(sm["cols_in"], 16)
            A(cs_e, col("c", 0, 16), ACT.Exp, scale=-1.0).then_inc(sm["c_exp"], 1)
            act.wait_ge(sm["setup"], 1)

            def x_stat(gi):
                t0, n = GROUPS[gi]
                act.wait_ge(x_in[gi], 16 * n)
                for t in range(t0, t0 + n):
                    need(act, sm["ssq_done"], t)
                    A(junk, xin[:, t, :], ACT.Square, accum_out=ssq[:, t:t + 1]).then_inc(sm["ssq_done"], 1)
                act.wait_ge(sm["ssq_done"], t0 + n)
                r = rstd[:, t0:t0 + n]
                A(r, ssq[:, t0:t0 + n], ACT.Ln, scale=1.0 / D, bias=eps_col).then_inc(sm["rs_done"], 1)
                act.wait_ge(sm["rs_done"], 2 * gi + 1)
                A(r, r, ACT.Exp, scale=-0.5).then_inc(sm["rs_done"], 1)

            def rows_out(piece):
                act.wait_ge(sm["ada_mm"], piece + 1)
                need(act, sm["mod_turn"], piece)
                b = 6 if piece == 2 else 0
                A(mod_row[0:2, 0:SEG], ps[0:2, b, :], ACT.Copy)
                A(mod_row[64:66, SEG:D], ps[64:66, b + 1, :], ACT.Copy).then_inc(sm["row_read"], 1)

            rows_out(0)
            for gi, (t0, n) in enumerate(GROUPS):
                if gi == 0:
                    x_stat(0)
                    rows_out(1)
                if gi + 1 < len(GROUPS):
                    x_stat(gi + 1)
                for k in range(1, KD, 2):
                    q = gi * KD + k
                    act.wait_ge(sm["xT_mm"], q + 1)
                    act.wait_ge(sm["mod_A"], 2)
                    m = 0 if t0 < NLAT else 1
                    A(hT[:, k, t0 * P:(t0 + n) * P], ps[:, 4 + q % 4, 0:n * P], ACT.Identity,
                      scale=mA[:, 2 * k + m:2 * k + m + 1], bias=mod[:, 2 * k + m:2 * k + m + 1]
                      ).then_inc(sm["hT_act"], 1)

            def turned_out(i):
                for j, (what, t, s, w, _) in aux_at(i, ("turn", "logits")):
                    act.wait_ge(sm["aux_mm"], j + 1)
                    bank = 6 + j % 2
                    if what == "logits":
                        A(gates[:, 0:16 * NT], ps[:, bank, 0:16 * NT], ACT.Copy).then_inc(sm["aux_read"], 1)
                        continue
                    h = head_of(t)
                    dst = k_tok if GDN_TILES[t] == "k" else v_tok
                    A(dst[:, s // P:(s + w) // P, h * P:(h + 1) * P],
                      ps[:, bank, 0:w].rearrange("p (c n) -> p c n", n=P), ACT.Copy,
                      scale=0.5 if GDN_TILES[t] == "v" else 1.0).then_inc(sm["aux_read"], 1)

            def gates_a(part):
                if part == 0:
                    act.wait_ge(sm["gt_d"], 2)
                    A(en, na, ACT.Exp, scale=-1.0).then_inc(sm["gt_a"], 1)
                    act.wait_ge(sm["gt_a"], 1)
                    A(en, en, ACT.Ln, bias=one_col).then_inc(sm["gt_a"], 1)
                    A(beta, lg[:, :, 0:8], ACT.Exp, scale=-1.0).then_inc(sm["gt_a"], 1)
                    A(ea[:, :], col("alog", 0, 8), ACT.Exp).then_inc(sm["gt_a"], 1)
                else:
                    act.wait_ge(sm["gt_d"], 7)
                    A(EG, gam, ACT.Exp).then_inc(sm["gt_a"], 1)
                    A(EKD, dtk, ACT.Exp).then_inc(sm["gt_a"], 1)
                    A(GL, tot, ACT.Exp).then_inc(sm["gt_a"], 1)

            for i in range(NG + 3):
                if i == GATES_AT - 2:
                    gates_a(0)
                if i == GATES_AT + 2:
                    gates_a(1)
                if i < NG:
                    act.wait_ge(sm["in_mm"], i + 1)
                    b = 3 * (i % 2)
                    if i == 0:
                        A(misc[:, 0:LAT], ps[:, b:b + 2, :], ACT.Copy)
                        A(misc[:, LAT:TOK], ps[:, b + 2, 0:CTX], ACT.Copy).then_inc(sm["evac_done"], 1)
                    else:
                        if i < 3:
                            act.wait_ge(sm["pad_done"], 6)
                        need(act, sm["conv_step"], 5 * (i - 2))
                        op = A(raw[i % 2][:, 2:2 + LAT], ps[:, b:b + 2, :], ACT.Copy)
                        if GDN_TILES[i] != "q":
                            op = A(raw[i % 2][:, CTX_RAW:CTX_RAW + CTX], ps[:, b + 2, 0:CTX], ACT.Copy)
                        op.then_inc(sm["evac_done"], 1)
                if i == 1:
                    rows_out(2)
                if i == 3:
                    act.wait_ge(sm["gp_mm"], 1)
                    A(GP[:, :], ps[:, 6:8, :], ACT.Copy).then_inc(sm["GP_done"], 1)
                t = i - 1
                if 1 <= t < NG:
                    n = LAT if GDN_TILES[t] == "q" else CV_W
                    act.wait_ge(sm["conv_step"], 5 * t)
                    need(act, sm["silu_done"], t - 1)
                    A(tanh_buf[:, 0:n], cv[t % 2][:, 0:n], ACT.Tanh, scale=0.5).then_inc(sm["tanh_done"], 1)
                jobs = aux_at(i, ("ones",))
                for j, (_, t, s, w, _) in jobs:
                    act.wait_ge(sm["aux_mm"], j + 1)
                    big = float(DK) if GDN_TILES[t] == "q" else 1.0
                    A(sqb[t % 2][:, s:s + w], ps[:, 6 + j % 2, 0:w], ACT.Ln, scale=big,
                      bias=eps_q if GDN_TILES[t] == "q" else eps_k).then_inc(sm["aux_read"], 1)
                if jobs:
                    j, (_, t, _, _, _) = jobs[-1]
                    n = ntok(GDN_TILES[t])
                    act.wait_ge(sm["aux_read"], j + 1)
                    A(sqb[t % 2][:, 0:n], sqb[t % 2][:, 0:n], ACT.Exp, scale=-0.5).then_inc(sm["rn_done"], 1)
                turned_out(i)

            for g, group in enumerate(INVERSES):
                for s, c in enumerate(group):
                    if g == 0:
                        act.wait_ge(sm["gt_d"], 9)
                        act.wait_ge(sm["in_mm"], NG)
                        act.wait_ge(sm["aux_mm"], len(AUX))
                        act.wait_ge(sm["fin_done"], len(QKI))
                        act.wait_ge(sm["spill"], 16)
                        act.wait_ge(sm["spill_kr"], 16)
                    else:
                        act.wait_ge(sm["upd"], 2 * (inv_index(g - 1, 5, s) + 1))
                    A(iv[s]["gbc"], g_[:, c, :].unsqueeze(2).broadcast_to([P, 8, P]), ACT.Copy
                      ).then_inc(sm["gbc_done"], 1)
                for s, c in enumerate(group):
                    act.wait_ge(sm["ex_done"], 8 * (c + 1))
                    A(iv[s]["E"], iv[s]["E"], ACT.Exp).then_inc(sm["e_done"], 1)
                for s, c in enumerate(group):
                    act.wait_ge(sm["tr_mm"], c + 1)
                    act.wait_ge(sm["qk_done"], 2 * min(c + 1, NLAT))
                    A(iv[s]["P"], ps[:, 2 * s, :], ACT.Copy).then_inc(sm["p_done"], 1)

            for m in LATSTEP:
                i, d = m // 2, m % 2
                c = order[d][i]
                act.wait_ge(sm["qs_mm"], LATSTEP.index(m) + 1)
                need(act, sm["oa_done"], len([q for q in LATSTEP if q <= m - 2]))
                for h in range(H):
                    op = A(t2[:, d, h * P:(h + 1) * P], ps[:, 4 * d + 3, h * P:(h + 1) * P], ACT.Copy,
                           scale=EG[:, c, 4 * d + h:4 * d + h + 1])
                op.then_inc(sm["t2_done"], 1)
            o_ss, o_rs = o_stat[:, 0:NLAT * H], o_stat[:, NLAT * H:]
            act.wait_ge(sm["ostat_d"], 1)
            A(o_rs, o_ss, ACT.Ln, scale=1.0 / P, bias=eps_col).then_inc(sm["ostat_a"], 1)
            act.wait_ge(sm["ostat_a"], 1)
            A(o_rs, o_rs, ACT.Exp, scale=-0.5).then_inc(sm["ostat_a"], 1)

            for j, kind in enumerate(REST_TILES):
                act.wait_ge(sm["in2_mm"], j + 1)
                b = 3 * (j % 2)
                i = j - first_of[kind]
                if j in ZT:
                    z = ZT.index(j)
                    need(act, sm["z_done"], z - 1)
                    if z == 0:
                        act.wait_ge(sm["n_done"], 3)
                        act.wait_ge(sm["kr_done"], 1)
                    A(z_half[:, z % 2, :], ps[:, b:b + 2, :], ACT.Tanh, scale=0.5).then_inc(sm["z_tanh"], 1)
                    continue
                if kind == "dv":
                    need(act, sm["aux2_mm"], len([a for a in AUX2 if a[4] <= j]) if i else 0)
                dst = {"cq": lambda: cq[:, i, :], "ckv": lambda: ckv, "dq": lambda: dq[:, i, :],
                       "dk": lambda: dk[:, i, :], "dv": lambda: dvT}[kind]()
                op = A(dst[:, 0:LAT], ps[:, b:b + 2, :], ACT.Copy, scale=DIFF_SCALE if kind == "dq" else 1.0)
                if kind not in LAT_ONLY:
                    op = A(dst[:, LAT:TOK], ps[:, b + 2, 0:CTX], ACT.Copy)
                op.then_inc(sm["c_evac"], 1)
                if j == NORM_AT:
                    sums = [(a, e) for a, e in enumerate(AUX2) if by_act(e)]
                    for a, (what, _, s, w, _) in sums:
                        act.wait_ge(sm["aux2_mm"], a + 1)
                        A((cq_rn if what == "sum_q" else kv_rn)[:, s:s + w], ps[:, 6 + a % 2, 0:w], ACT.Ln,
                          bias=eps_col, scale=1.0 / (Q_RANK if what == "sum_q" else KV_RANK)
                          ).then_inc(sm["norm_read"], 1)
                    act.wait_ge(sm["norm_read"], len(sums))
                    A(cq_rn, cq_rn, ACT.Exp, scale=-0.5).then_inc(sm["n_exp"], 1)
                    A(kv_rn, kv_rn, ACT.Exp, scale=-0.5).then_inc(sm["n_exp"], 1)

            act.wait_ge(sm["lam_d"], 4)
            A(lamt[:, 0:2], lamt[:, 0:2], ACT.Exp).then_inc(sm["lam_a"], 1)

            for h in range(H):
                act.wait_ge(sm["mq_mm"], h + 1)
                b = 2 * (h % 2)
                A(QTm[0:MLA_QK, h, :], ps[0:MLA_QK, b:b + 2, :], ACT.Copy, scale=MLA_SCALE).then_inc(sm["mq_ev"], 1)
            for v in range(NT // 2):
                act.wait_ge(sm["mv_mm"], v + 1)
                A(V_tok[:, 2 * v:2 * v + 2, :], ps[:, v % 2, :].rearrange("p (a b) -> p a b", a=2),
                  ACT.Copy).then_inc(sm["mv_ev"], 1)
            for h in range(H):
                act.wait_ge(sm["mk_mm"], h + 1)
                b = 3 * (h % 2)
                A(KTm[0:MLA_NOPE, h, 0:LAT], ps[0:MLA_NOPE, b:b + 2, :], ACT.Copy)
                A(KTm[0:MLA_NOPE, h, LAT:TOK], ps[0:MLA_NOPE, b + 2, 0:CTX], ACT.Copy).then_inc(sm["mk_ev"], 1)
                if h == 0:
                    act.wait_ge(sm["kr_done"], 1)
                A(KTm[KR0:MLA_QK, h, :], krT[KR0:MLA_QK, :], ACT.Copy).then_inc(sm["mk_rope"], 1)

            def exps(st):
                act.wait_ge(sm["mx_done"], st + 1)
                if st >= 4:
                    prev = [q for q in range(len(UNITS)) if st - 4 in sets_of(q)][0]
                    act.wait_ge(sm["wt_mm"], 3 * (prev + 1))
                if st < 4:
                    act.wait_ge(sm["n_done"], 3)
                b = 3 * (st % 2)
                A(prob[:, st % 4, :], ps[:, b:b + 3, :].rearrange("p a b -> p (a b)")[:, 0:TOK], ACT.Exp,
                  bias=nmax[:, st:st + 1], accum_out=lsum[:, st:st + 1]).then_inc(sm["p_exp"], 1)

            def turned(n, gi):
                s, w = KSEG[gi]
                act.wait_ge(sm["wt_mm"], 3 * n + gi + 1)
                if gi == 0:
                    need(act, sm["pv_mm"], n - 1)
                A(wT[:, n % 2, s:s + w], ps[:, 7 if gi == 1 else 6, 0:w], ACT.Copy).then_inc(sm["wt_ev"], 1)

            def out_part(n):
                qb, u = UNITS[n]
                act.wait_ge(sm["pv_mm"], n + 1)
                act.wait_ge(sm["l_inv"], 4 * (n // 2) + 1 + n % 2)
                if n % 8 == 0:
                    need(act, sm["ot_mm"], qb - 1)
                A(o_tok[:, qb % 2, u * 64:u * 64 + 64], ps[:, 7, 0:64], ACT.Copy,
                  scale=rinv[:, n:n + 1]).then_inc(sm["pv_ev"], 1)

            def d_stat(qb):
                act.wait_ge(sm["d_red"], qb + 1)
                r = drs[:, 4 * qb:4 * qb + 4]
                A(r, dss[:, 4 * qb:4 * qb + 4], ACT.Ln, scale=1.0 / DIFF_V, bias=eps_col).then_inc(sm["d_ln"], 1)
                act.wait_ge(sm["d_ln"], qb + 1)
                A(r, r, ACT.Exp, scale=-0.5).then_inc(sm["d_exp"], 1)

            exps(0)
            for i in range(PAIRS + 1):
                if i >= 1:
                    turned(2 * i - 1, 0)
                    turned(2 * i - 1, 1)
                if i < PAIRS:
                    exps(3 * i + 1)
                if i >= 1:
                    turned(2 * i - 1, 2)
                if i < PAIRS:
                    exps(3 * i + 2)
                if i >= 1:
                    out_part(2 * i - 2)
                if i < PAIRS:
                    turned(2 * i, 0)
                    turned(2 * i, 1)
                    if i >= 5 and i % H == 1:
                        d_stat(i // H - 1)
                    turned(2 * i, 2)
                if i + 1 < PAIRS:
                    exps(3 * i + 3)
                if i >= 1:
                    out_part(2 * i - 1)
            d_stat(NLAT - 1)

            for t in range(NLAT):
                act.wait_ge(sm["y_mm"], t + 1)
                b = 2 * (t % 2)
                need(act, sm["y_sq"], t)
                A(y_junk, ps[:, b:b + 2, :], ACT.Square, accum_out=yst[:, t:t + 1]).then_inc(sm["y_sq"], 1)
                act.wait_ge(sm["y_sq"], t + 1)
                r = yst[:, NLAT + t:NLAT + t + 1]
                A(r, yst[:, t:t + 1], ACT.Ln, scale=1.0 / D, bias=eps_col).then_inc(sm["y_ln"], 1)
                act.wait_ge(sm["y_ln"], t + 1)
                A(r, r, ACT.Exp, scale=-0.5).then_inc(sm["y_exp"], 1)

        @block.vector
        def _(dve):
            V = nc.vector
            V.memset(eps_col, EPS)
            V.memset(one_col, 1.0)
            V.memset(eps_k, 4 * EPS)
            V.memset(eps_q, 4 * EPS * DK).then_inc(sm["setup"], 1)
            dve.wait_ge(sm["c_exp"], 1)
            V.tensor_scalar(cs_e, cs_e, 1.0, None, ALU.add).then_inc(sm["c_one"], 1)
            dve.wait_ge(sm["c_one"], 1)
            V.reciprocal(cs_e, cs_e).then_inc(sm["c_rec"], 1)
            dve.wait_ge(sm["c_rec"], 1)
            V.tensor_tensor(cs, cs_e, col("c", 0, 16), ALU.mult).then_inc(sm["c_silu"], 1)

            def xn(gi):
                t0, n = GROUPS[gi]
                for t in range(t0, t0 + n):
                    dve.wait_ge(sm["rs_done"], 2 * gi + 2)
                    V.tensor_scalar(xin[:, t, :], xin[:, t, :], rstd[:, t:t + 1], None,
                                    ALU.mult).then_inc(sm["xn_done"], 1)

            def hT_even(gi):
                t0, n = GROUPS[gi]
                m = 0 if t0 < NLAT else 1
                for k in range(0, KD, 2):
                    q = gi * KD + k
                    dve.wait_ge(sm["xT_mm"], q + 1)
                    V.tensor_scalar(hT[:, k, t0 * P:(t0 + n) * P], ps[:, 4 + q % 4, 0:n * P],
                                    mA[:, 2 * k + m:2 * k + m + 1], mod[:, 2 * k + m:2 * k + m + 1],
                                    ALU.mult, ALU.add).then_inc(sm["hT_dve"], 1)

            mod3 = mod.rearrange("p (j c) -> p j c", c=2)

            def add_bias(piece):
                dve.wait_ge(sm["mod_turn"], piece + 1)
                for i in range(2):
                    o = 8 * piece + 4 * i
                    op = V.tensor_tensor(mod3[:, o:o + 4, :],
                                         ps[:, (6 if piece == 2 else 2) + i, 0:8].rearrange("p (j c) -> p j c", c=2),
                                         col("ada_b", o, 4).unsqueeze(2).broadcast_to([P, 4, 2]), ALU.add)
                op.then_inc(sm["mod_add"], 1)
                dve.wait_ge(sm["mod_add"], piece + 1)

            add_bias(0)
            xn(0)
            add_bias(1)
            mA3 = mA.rearrange("p (j c) -> p j c", c=2)
            V.tensor_scalar(mA, mod[:, 16:32], 1.0, None, ALU.add).then_inc(sm["mod_A"], 1)
            dve.wait_ge(sm["mod_A"], 1)
            V.tensor_tensor(mA3, mA3, col("pre", 0, 8).unsqueeze(2).broadcast_to([P, 8, 2]),
                            ALU.mult).then_inc(sm["mod_A"], 1)
            dve.wait_ge(sm["mod_A"], 2)
            xn(1)
            hT_even(0)
            xn(2)
            hT_even(1)
            hT_even(2)

            def gate_row():
                add_bias(2)
                V.tensor_tensor(gp_col, mod3[:, 16:24, 0], col("post", 0, 8), ALU.mult).then_inc(sm["gp_done"], 1)
                dve.wait_ge(sm["gp_done"], 1)
                V.tensor_tensor(gp_diag, ident.unsqueeze(1).broadcast_to([P, KD, P]),
                                gp_col.unsqueeze(2).broadcast_to([P, KD, P]), ALU.mult).then_inc(sm["diag_done"], 1)

            def gates_d0():
                logits_read = [j for j, a in enumerate(AUX) if a[0] == "logits"][0] + 1
                dve.wait_ge(sm["aux_read"], logits_read)
                V.tensor_tensor(xa, lg[:, :, 8:16], col("dt", 0, 8).unsqueeze(1).broadcast_to([P, NT, 8]),
                                ALU.add).then_inc(sm["gt_d"], 1)
                dve.wait_ge(sm["gt_d"], 1)
                V.scalar_tensor_tensor(out=na, in0=xa, scalar=-1.0, in1=xa, op0=ALU.mult,
                                       op1=ALU.max).then_inc(sm["gt_d"], 1)
                dve.wait_ge(sm["gt_a"], 4)
                V.scalar_tensor_tensor(out=sp, in0=xa, scalar=0.0, in1=en, op0=ALU.max,
                                       op1=ALU.add).then_inc(sm["gt_d"], 1)
                dve.wait_ge(sm["gt_d"], 3)
                V.scalar_tensor_tensor(out=g_, in0=sp, scalar=-1.0, in1=ea[:, :].unsqueeze(1).broadcast_to([P, NT, 8]),
                                       op0=ALU.mult, op1=ALU.mult).then_inc(sm["gt_d"], 1)

            def gates_d1():
                gj = [j for j, a in enumerate(AUX) if a[0] == "gates"][0]
                gb = 6 + gj % 2
                dve.wait_ge(sm["aux_mm"], gj + 1)
                V.tensor_copy(gam, ps[:, gb, 0:8 * NT].rearrange("p (c n) -> p c n", n=8)).then_inc(sm["gt_d"], 1)
                V.tensor_copy(tot, ps[:, gb, 128:128 + 8 * NT].rearrange("p (c n) -> p c n", n=8)).then_inc(sm["gt_d"], 1)
                dve.wait_ge(sm["gt_d"], 6)
                V.tensor_scalar(beta, beta, 1.0, None, ALU.add).then_inc(sm["aux_read"], 1)
                V.tensor_tensor(dtk, tot, gam, ALU.subtract).then_inc(sm["gt_d"], 1)
                dve.wait_ge(sm["aux_read"], gj + 1)
                dve.wait_ge(sm["gt_d"], 7)
                V.reciprocal(beta, beta).then_inc(sm["gt_d"], 1)
                dve.wait_ge(sm["gt_d"], 8)
                dve.wait_ge(sm["gt_a"], 7)
                V.tensor_tensor(bek, beta, EKD, ALU.mult).then_inc(sm["gt_d"], 1)


            for i in range(NG + 1):
                if i == GATES_AT - 2:
                    gates_d0()
                if i == GATES_AT + 1:
                    gates_d1()
                if 1 <= i < NG:
                    n = LAT if GDN_TILES[i] == "q" else CV_W
                    dve.wait_ge(sm["evac_done"], i + 1)
                    need(dve, sm["silu_done"], i - 2)
                    src, dst = raw[i % 2], cv[i % 2]
                    for j in range(CONV_W):
                        wj = col("conv", (i - 1) * CONV_W + j)
                        if j == 0:
                            op = V.tensor_scalar(dst[:, 0:n], src[:, 0:n], wj, None, ALU.mult)
                        else:
                            dve.wait_ge(sm["conv_step"], 5 * (i - 1) + j)
                            op = V.scalar_tensor_tensor(out=dst[:, 0:n], in0=src[:, j:j + n], scalar=wj,
                                                        in1=dst[:, 0:n], op0=ALU.mult, op1=ALU.add)
                        op.then_inc(sm["conv_step"], 1)
                t = i - 1
                if 1 <= t < NG:
                    n = LAT if GDN_TILES[t] == "q" else CV_W
                    dve.wait_ge(sm["tanh_done"], t)
                    y = y_of(t)
                    if GDN_TILES[t] == "v" and t >= 2 and GDN_TILES[t - 2] == "v":
                        dve.wait_ge(sm["aux_mm"], max(j for j, a in enumerate(AUX) if a[1] == t - 2) + 1)
                    op = V.scalar_tensor_tensor(out=y[:, 0:LAT], in0=tanh_buf[:, 0:LAT], scalar=1.0,
                                                in1=cv[t % 2][:, 0:LAT], op0=ALU.add, op1=ALU.mult)
                    if GDN_TILES[t] != "q":
                        op = V.scalar_tensor_tensor(out=y[:, LAT:TOK], in0=tanh_buf[:, CTX_CV:CTX_CV + CTX], scalar=1.0,
                                                    in1=cv[t % 2][:, CTX_CV:CTX_CV + CTX], op0=ALU.add, op1=ALU.mult)
                    op.then_inc(sm["silu_done"], 1)
                if i == 2:
                    gate_row()

            for g, group in enumerate(INVERSES):
                for s, c in enumerate(group):
                    dve.wait_ge(sm["gb_mm"], c + 1)
                    for d in range(2):
                        for h in range(H):
                            V.scalar_tensor_tensor(
                                out=iv[s]["E"][:, 4 * d + h, :], in0=ps[:, 2 * s + d, h * P:(h + 1) * P],
                                scalar=gam[:, c, 4 * d + h:4 * d + h + 1], in1=cst("neg_f" if d == 0 else "neg_b"),
                                op0=ALU.subtract, op1=ALU.min).then_inc(sm["ex_done"], 1)
                for s, c in enumerate(group):
                    kk = ps[:, 2 * s, :].rearrange("p (h n) -> p h n", n=P)
                    qk = ps[:, 2 * s + 1, :].rearrange("p (h n) -> p h n", n=P)
                    Qc = Q_all[:, c, :].rearrange("p (h n) -> p h n", n=P)
                    dve.wait_ge(sm["pool_w"], 3 * (c + 1))
                    dve.wait_ge(sm["pre_mm"], c + 1)
                    V.tensor_tensor(iv[s]["At"], kk, iv[s]["At"], ALU.mult).then_inc(sm["at_done"], 1)
                    dve.wait_ge(sm["at_done"], c + 1)
                    V.tensor_tensor(Qc, iv[s]["At"], heads(cst("sib1")), ALU.mult).then_inc(sm["q_step"], 1)
                    dve.wait_ge(sm["q_step"], 2 * c + 1)
                    V.tensor_tensor(Qc, heads(ident), Qc, ALU.subtract).then_inc(sm["q_step"], 1)
                    if c < NLAT:
                        for d in range(2):
                            V.tensor_tensor(QK[:, d * NLAT + c, :].rearrange("p (h n) -> p h n", n=P), qk,
                                            iv[s]["E"][:, 4 * d:4 * d + 4, :], ALU.mult).then_inc(sm["qk_done"], 1)
                for lev in range(6):
                    for s, c in enumerate(group):
                        n = inv_index(g, lev, s)
                        dve.wait_ge(sm["x_mm"], n + 1)
                        V.tensor_tensor(iv[s]["X"], ps[:, 2 * s, :].rearrange("p (h n) -> p h n", n=P),
                                        heads(cst(f"sib{LEVELS[lev + 1]}")), ALU.mult).then_inc(sm["xs_done"], 1)
                    for s, c in enumerate(group):
                        n = inv_index(g, lev, s)
                        if lev < 5:
                            dve.wait_ge(sm["pq_mm"], 2 * n + 1)
                            V.tensor_tensor(iv[s]["P"], iv[s]["P"],
                                            ps[:, 2 * s, :].rearrange("p (h n) -> p h n", n=P),
                                            ALU.subtract).then_inc(sm["upd"], 1)
                        dve.wait_ge(sm["pq_mm"], 2 * n + 2)
                        V.tensor_tensor(Q_all[:, c, :], Q_all[:, c, :], ps[:, 2 * s + 1, :],
                                        ALU.subtract).then_inc(sm["upd"], 1 if lev < 5 else 2)

            def h3(ap):
                return ap.rearrange("p (h n) -> p h n", n=P)
            dve.wait_ge(sm["gt_d"], 9)
            for i in range(NT):
                for d in range(2):
                    m = 2 * i + d
                    c = order[d][i]
                    dve.wait_ge(sm["ks_mm"], m + 1)
                    V.tensor_tensor(h3(R[:, d, :]), h3(ps[:, 4 * d, :]), per_head(EG[:, c, 4 * d:4 * d + 4]),
                                    ALU.mult).then_inc(sm["r_done"], 1)
                    dve.wait_ge(sm["r_done"], 2 * m + 1)
                    V.tensor_tensor(R[:, d, :], v_tok[:, c, :], R[:, d, :], ALU.subtract).then_inc(sm["r_done"], 1)
                for d in range(2):
                    m = 2 * i + d
                    c = order[d][i]
                    dve.wait_ge(sm["tr4_mm"], m + 1)
                    V.tensor_tensor(h3(Vs[:, d, :]), h3(ps[:, 4 * d + 1, :]), per_head(bek[:, c, 4 * d:4 * d + 4]),
                                    ALU.mult).then_inc(sm["vv_done"], 1)
                    need(dve, sm["qkv_mm"], len([q for q in LATSTEP if q <= m - 2]))
                    V.tensor_tensor(h3(Vn[:, d, :]), h3(ps[:, 4 * d + 1, :]), per_head(beta[:, c, 4 * d:4 * d + 4]),
                                    ALU.mult).then_inc(sm["vv_done"], 1)
                for d in range(2):
                    m = 2 * i + d
                    c = order[d][i]
                    dve.wait_ge(sm["ds_mm"], m + 1)
                    dve.wait_ge(sm["sg_done"], m + 1)
                    V.tensor_tensor(S[:, d, :], Sg[:, d, :], ps[:, 4 * d + 2, :], ALU.add).then_inc(sm["s_upd"], 1)
                    if c < NLAT:
                        li = LATSTEP.index(m)
                        dve.wait_ge(sm["qkv_mm"], li + 1)
                        dve.wait_ge(sm["t2_done"], li + 1)
                        V.tensor_tensor(t2[:, d, :], t2[:, d, :], ps[:, 4 * d, :], ALU.add).then_inc(sm["o1_done"], 1)
            dve.wait_ge(sm["osq_done"], 1)
            V.tensor_reduce(o_stat[:, 0:NLAT * H], o_sq, AX.X, ALU.add).then_inc(sm["ostat_d"], 1)
            dve.wait_ge(sm["ostat_a"], 2)
            oa3 = o_acc.rearrange("p c (h n) -> p (c h) n", n=P)
            V.tensor_tensor(oa3, oa3, o_stat[:, NLAT * H:].unsqueeze(2).broadcast_to([P, NLAT * H, P]),
                            ALU.mult).then_inc(sm["o_ready"], 1)

            lam4 = col("lam", 0, 128).rearrange("p (a b n) -> p a b n", a=2, b=2)
            lp = lam_p[:, :].rearrange("p (a n) -> p a n", a=2)
            V.tensor_tensor(lp, lam4[:, :, 0, :], lam4[:, :, 1, :], ALU.mult).then_inc(sm["lam_d"], 1)
            dve.wait_ge(sm["lam_d"], 1)
            V.tensor_reduce(lamt[:, 0:2], lp, AX.X, ALU.add).then_inc(sm["lam_d"], 1)
            V.tensor_scalar(og_half, col("og"), 0.5, None, ALU.mult).then_inc(sm["lam_d"], 1)
            V.tensor_scalar(lamt[:, 4:5], col("sg"), 0.5 * (1.0 - LAM_INIT), None, ALU.mult).then_inc(sm["lam_d"], 1)
            dve.wait_ge(sm["lam_d"], 4)

            rows = slice(KR0, KR0 + MLA_ROPE)

            def latent_norms():
                dve.wait_ge(sm["n_exp"], 2)
                for k in range(2):
                    V.scalar_tensor_tensor(out=cq[:, k, :], in0=cq[:, k, :], scalar=col("qg", k), in1=cq_rn,
                                           op0=ALU.mult, op1=ALU.mult).then_inc(sm["n_done"], 1)
                V.scalar_tensor_tensor(out=ckv, in0=ckv, scalar=col("kvg"), in1=kv_rn,
                                       op0=ALU.mult, op1=ALU.mult).then_inc(sm["n_done"], 1)
                wait_read2(dve, max(a for a, e in enumerate(AUX2) if e[0] == "swap_kr"))
                V.tensor_tensor(krT[rows, 0:LAT], krT[rows, 0:LAT], rope[rows, 0, :], ALU.mult).then_inc(sm["kr_c"], 1)
                dve.wait_ge(sm["kr_c"], 1)
                V.tensor_tensor(krT[rows, 0:LAT], krT[rows, 0:LAT], kr_buf[rows, :], ALU.add).then_inc(sm["kr_done"], 1)
                dve.wait_ge(sm["n_done"], 3)

            def z_dest(j):
                kind = REST_TILES[j]
                i = j - first_of[kind]
                return {"za": lambda: zbuf[:, i % 2, :], "zb": lambda: mixT[:, 4 + i, :],
                        "dz": lambda: mixT[:, 6 + i, :]}[kind]()

            for j in range(len(REST_TILES) + 1):
                if j == NORM_AT + 1:
                    latent_norms()
                if j < len(REST_TILES) and j in ZT:
                    z = ZT.index(j)
                    b = 3 * (j % 2)
                    dve.wait_ge(sm["z_tanh"], z + 1)
                    wait_read2(dve, max([a for a, e in enumerate(AUX2) if e[0] == "za" and e[1] <= j - 2] or [-1]))
                    V.scalar_tensor_tensor(out=z_dest(j).rearrange("p (a b) -> p a b", a=2),
                                           in0=z_half[:, z % 2, :].rearrange("p (a b) -> p a b", a=2), scalar=1.0,
                                           in1=ps[:, b:b + 2, :], op0=ALU.add, op1=ALU.mult).then_inc(sm["z_done"], 1)
                for a, (kind, t, s, w, jj) in enumerate(AUX2):
                    if jj != j or by_act((kind,)):
                        continue
                    dve.wait_ge(sm["aux2_mm"], a + 1)
                    bank = 6 + a % 2
                    if kind == "swap_kr":
                        V.tensor_tensor(kr_buf[rows, s:s + w], ps[rows, bank, 0:w], rope[rows, 1, s:s + w],
                                        ALU.mult).then_inc(sm["aux2_read"], 1)
                        continue
                    if kind == "za":
                        h = t - first_of["za"]
                        dve.wait_ge(sm["z_done"], ZT.index(t) + 1)
                        V.scalar_tensor_tensor(out=mixT[:, h, s:s + w], in0=ps[:, bank, 0:w], scalar=og_half,
                                               in1=zbuf[:, h % 2, s:s + w], op0=ALU.mult,
                                               op1=ALU.mult).then_inc(sm["aux2_read"], 1)
                    elif kind == "dv":
                        i = t - first_of["dv"]
                        V.tensor_copy(dv_tok[:, s // P:(s + w) // P, i * P:(i + 1) * P],
                                      ps[:, bank, 0:w].rearrange("p (c n) -> p c n", n=P)
                                      ).then_inc(sm["aux2_read"], 1)
                    else:
                        dve.wait_ge(sm["rope_in"], 16)
                        r = ROPED.index(t)
                        if s == 0:
                            need(dve, sm["rope_done"], 2 * r)
                        V.tensor_tensor(rbuf[:, s:s + w], ps[:, bank, 0:w], rope[:, 1, s:s + w],
                                        ALU.mult).then_inc(sm["aux2_read"], 1)

            def low_keys(g):
                dve.wait_ge(sm[f"k_in{g}"], 64)
                need(dve, sm["kst_done"], g)
                V.tensor_copy(k_hi[64:P, :], k_stage[g][64:P, :]).then_inc(sm["kh_done"], 1)
                dve.wait_ge(sm["kh_done"], g + 1)
                V.tensor_tensor(k_stack[g][64:P, :], k_stage[g][64:P, :], k_hi[64:P, :].bitcast(F32),
                                ALU.subtract).then_inc(sm["kst_done"], 1)

            low_keys(0)
            low_keys(1)
            dve.wait_ge(sm["rope_done"], 2 * len(ROPED))
            for h in range(H):
                dve.wait_ge(sm["mq_swap"], h + 1)
                dve.wait_ge(sm["mq_done"], h) if h else dve.wait_ge(sm["kr_done"], 1)
                V.tensor_tensor(rbuf[rows, :].rearrange("p (a b) -> p a b", a=2), ps[rows, 6:8, :],
                                rope[rows, 1, :].rearrange("p (a b) -> p a b", a=2), ALU.mult).then_inc(sm["mq_t"], 1)
                V.tensor_tensor(QTm[rows, h, :], QTm[rows, h, :], rope[rows, 0, :], ALU.mult).then_inc(sm["mq_c"], 1)
                dve.wait_ge(sm["mq_t"], h + 1)
                dve.wait_ge(sm["mq_c"], h + 1)
                V.tensor_tensor(QTm[rows, h, :], QTm[rows, h, :], rbuf[rows, :], ALU.add).then_inc(sm["mq_done"], 1)

            dve.wait_ge(sm["lam_a"], 1)
            V.tensor_tensor(lamt[:, 5:6], lamt[:, 1:2], lamt[:, 0:1], ALU.subtract).then_inc(sm["lam_d"], 1)
            dve.wait_ge(sm["lam_d"], 5)
            V.tensor_scalar(lamt[:, 6:7], lamt[:, 5:6], -LAM_INIT, None, ALU.add).then_inc(sm["lam_d"], 1)
            dve.wait_ge(sm["lam_d"], 6)

            def row_max(st):
                dve.wait_ge(sm["sc_mm"], st + 1)
                b = 3 * (st % 2)
                V.tensor_reduce(nmax[:, st:st + 1], ps[:, b:b + 3, :].rearrange("p a b -> p (a b)")[:, 0:TOK],
                                AX.X, ALU.max, negate=True).then_inc(sm["mx_done"], 1)

            linv = [0]

            def counted(op):
                linv[0] += 1
                op.then_inc(sm["l_inv"], 1)
                return linv[0]

            def combine(n):
                qb, u = UNITS[n]
                st = sets_of(n)
                dve.wait_ge(sm["p_exp"], st[-1] + 1)
                v = counted(V.reciprocal(rinv[:, n:n + 1], lsum[:, st[0]:st[0] + 1]))
                if u < H:
                    return
                v = counted(V.reciprocal(rinv1[:, n:n + 1], lsum[:, st[1]:st[1] + 1]))
                dve.wait_ge(sm["l_inv"], v)
                v = counted(V.scalar_tensor_tensor(out=coef[:, n:n + 1], in0=lsum[:, st[0]:st[0] + 1],
                                                   scalar=lamt[:, 6:7], in1=rinv1[:, n:n + 1],
                                                   op0=ALU.mult, op1=ALU.mult))
                dve.wait_ge(sm["l_inv"], v)
                p0, p1 = prob[:, st[0] % 4, :], prob[:, st[1] % 4, :]
                V.scalar_tensor_tensor(out=p0, in0=p1, scalar=coef[:, n:n + 1], in1=p0, op0=ALU.mult,
                                       op1=ALU.add).then_inc(sm["w_done"], 1)

            def diff_out(qb):
                return o_tok[:, qb % 2, H * 64:].rearrange("p (h n) -> p h n", n=64)

            def square(qb):
                dve.wait_ge(sm["pv_ev"], 8 * (qb + 1))
                V.tensor_tensor(d_sq, diff_out(qb), diff_out(qb), ALU.mult).then_inc(sm["d_sqd"], 1)
                dve.wait_ge(sm["d_sqd"], qb + 1)
                V.tensor_reduce(dss[:, 4 * qb:4 * qb + 4], d_sq, AX.X, ALU.add).then_inc(sm["d_red"], 1)

            def normalise(qb):
                r = drs[:, 4 * qb:4 * qb + 4]
                dve.wait_ge(sm["d_exp"], qb + 1)
                V.tensor_tensor(diff_out(qb), diff_out(qb), r.unsqueeze(2).broadcast_to([P, H, 64]),
                                ALU.mult).then_inc(sm["d_norm"], 1)

            def mix(qb):
                dve.wait_ge(sm["ot_mm"], qb + 1)
                mx = mixT[:, :, qb * P:(qb + 1) * P]
                pso = ps[:, 6, :].rearrange("p (i n) -> p i n", n=P)
                V.scalar_tensor_tensor(out=mx[:, 4:6, :], in0=pso[:, 0:2, :], scalar=0.5,
                                       in1=mx[:, 4:6, :], op0=ALU.mult, op1=ALU.mult).then_inc(sm["mix_b"], 1)
                V.scalar_tensor_tensor(out=mx[:, 6:8, :], in0=pso[:, 2:4, :], scalar=lamt[:, 4:5],
                                       in1=mx[:, 6:8, :], op0=ALU.mult, op1=ALU.mult).then_inc(sm["mix_b"], 1)

            row_max(0)
            for i in range(PAIRS):
                if i >= 7 and i % H == 3:
                    mix(i // H - 1)
                row_max(3 * i + 1)
                if i >= 5 and i % H == 1:
                    square(i // H - 1)
                row_max(3 * i + 2)
                if i >= 6 and i % H == 2:
                    normalise(i // H - 1)
                combine(2 * i)
                combine(2 * i + 1)
                if i < H - 1:
                    low_keys(2 * i + 2)
                if i + 1 < PAIRS:
                    row_max(3 * i + 3)
                if i < H - 1:
                    low_keys(2 * i + 3)
            square(NLAT - 1)
            normalise(NLAT - 1)
            mix(NLAT - 1)

            for t in range(NLAT):
                dve.wait_ge(sm["y_exp"], t + 1)
                if t >= 2:
                    dve.wait_ge(y_out[t % 2], 16 * (t // 2))
                if t == 0:
                    dve.wait_ge(sm["wt_mm"], 3 * len(UNITS))
                b = 2 * (t % 2)
                V.scalar_tensor_tensor(out=y_buf[:, t % 2, :].rearrange("p (a b) -> p a b", a=2),
                                       in0=ps[:, b:b + 2, :], scalar=yst[:, NLAT + t:NLAT + t + 1],
                                       in1=GP[:, :].rearrange("p (a b) -> p a b", a=2),
                                       op0=ALU.mult, op1=ALU.mult).then_inc(sm["y_scaled"], 1)

        @block.gpsimd
        def _(pool):
            G = nc.gpsimd
            pool.wait_ge(sm["xT_mm"], 24)
            for r in raw:
                G.memset(r[:, 0:2], 0.0).then_inc(sm["pad_done"], 1)
                G.memset(r[:, LAT + 2:LAT + 6], 0.0).then_inc(sm["pad_done"], 1)
                G.memset(r[:, RAW_W - 2:RAW_W], 0.0).then_inc(sm["pad_done"], 1)

            for i in range(NG + 3):
                t = i - 1
                if 1 <= t < NG:
                    y = y_of(t)
                    if GDN_TILES[t] in "qk":
                        n = ntok(GDN_TILES[t])
                        pool.wait_ge(sm["silu_done"], t)
                        need(pool, sm["fin_done"], QKI.index(t) - 1)
                        G.tensor_tensor(sqb[t % 2][:, 0:n], y[:, 0:n], y[:, 0:n], ALU.mult).then_inc(sm["sq_done"], 1)
                t = i - 2
                if t in QKI:
                    n = ntok(GDN_TILES[t])
                    y = y_of(t)
                    pool.wait_ge(sm["rn_done"], QKI.index(t) + 1)
                    G.tensor_tensor(y[:, 0:n], y[:, 0:n], sqb[t % 2][:, 0:n], ALU.mult).then_inc(sm["fin_done"], 1)

            for g, group in enumerate(INVERSES):
                for s, c in enumerate(group):
                    b = iv[s]
                    pool.wait_ge(sm["e_done"], c + 1)
                    G.tensor_tensor(b["tmp"], b["E"][:, 0:4, :], per_head(beta[:, c, 0:4]), ALU.mult
                                    ).then_inc(sm["pool_w"], 1)
                    G.tensor_tensor(b["At"], b["E"][:, 4:8, :], per_head(beta[:, c, 4:8]), ALU.mult
                                    ).then_inc(sm["pool_w"], 1)
                    pool.wait_ge(sm["pool_w"], 3 * c + 2)
                    G.tensor_tensor(b["At"], b["At"], b["tmp"], ALU.add).then_inc(sm["pool_w"], 1)
                for lev in range(6):
                    for s, c in enumerate(group):
                        n = inv_index(g, lev, s)
                        b = iv[s]
                        mask = heads(cst(f"alt{LEVELS[lev + 1]}"))
                        Qc = Q_all[:, c, :].rearrange("p (h n) -> p h n", n=P)
                        if lev == 0:
                            pool.wait_ge(sm["p_done"], c + 1)
                        else:
                            pool.wait_ge(sm["upd"], 2 * (n - len(group)) + 1)
                        G.tensor_tensor(b["M"], b["P"], mask, ALU.mult).then_inc(sm["mn_done"], 1)
                        if lev > 0:
                            pool.wait_ge(sm["upd"], 2 * (n - len(group)) + 2)
                        G.tensor_tensor(b["N"], Qc, mask, ALU.mult).then_inc(sm["mn_done"], 1)

            pool.wait_ge(sm["upd"], 2 * 60)
            G.memset(view(20, 4 * 256), 0.0).then_inc(sm["s_init"], 1)
            G.memset(view(148, 16 * 256), 0.0).then_inc(sm["s_init"], 1)
            pool.wait_ge(sm["s_init"], 2)

            def h3(ap):
                return ap.rearrange("p (h n) -> p h n", n=P)
            for i in range(NT + 1):
                for d in range(2):
                    m = 2 * i + d
                    if i < NT:
                        c = order[d][i]
                        need(pool, sm["tr4_mm"], m - 1)
                        G.tensor_tensor(h3(Um[:, d, :]), h3(Q_all[:, c, :]), heads(cst("triu" if d == 0 else "tril")),
                                        ALU.mult).then_inc(sm["um_done"], 1)
                        need(pool, sm["s_upd"], m - 1)
                        G.tensor_tensor(h3(Sg[:, d, :]), h3(S[:, d, :]), per_head(GL[:, c, 4 * d:4 * d + 4]),
                                        ALU.mult).then_inc(sm["sg_done"], 1)
                    if m - 2 in LATSTEP:
                        li = LATSTEP.index(m - 2)
                        c = order[d][i - 1]
                        pool.wait_ge(sm["o1_done"], li + 1)
                        need(pool, sm["oa_done"], li)
                        G.tensor_tensor(o_acc[:, c, :], o_acc[:, c, :], t2[:, d, :], ALU.add
                                        ).then_inc(sm["oa_done"], 1)
            pool.wait_ge(sm["oa_done"], 16)
            pool.wait_ge(sm["tr4_mm"], 20)
            oa = view(148, NLAT * H, P)
            G.tensor_tensor(o_sq, oa, oa, ALU.mult).then_inc(sm["osq_done"], 1)

            for j, kind in enumerate(REST_TILES + [""]):
                if j == 3:
                    pool.wait_ge(sm["c_evac"], 3)
                    for k in range(2):
                        G.tensor_tensor(cq_sq[:, k, :], cq[:, k, :], cq[:, k, :], ALU.mult).then_inc(sm["n_sq"], 1)
                    G.tensor_tensor(kv_sq, ckv, ckv, ALU.mult).then_inc(sm["n_sq"], 1)
                if j - 1 in ROPED:
                    t = j - 1
                    kind = REST_TILES[t]
                    r = ROPED.index(t)
                    a = max(q for q, e in enumerate(AUX2) if e[1] == t)
                    dst = (dq if kind == "dq" else dk)[:, t - first_of[kind], 0:LAT]
                    pool.wait_ge(sm["aux2_mm"], a + 1)
                    pool.wait_ge(sm["rope_in"], 16)
                    G.tensor_tensor(dst, dst, rope[:, 0, :], ALU.mult).then_inc(sm["rope_done"], 1)
                    pool.wait_ge(sm["rope_done"], 2 * r + 1)
                    wait_read2(pool, a)
                    G.tensor_tensor(dst, dst, rbuf, ALU.add).then_inc(sm["rope_done"], 1)
            for qb in range(NLAT):
                stage, stack, hi = q_stage[qb % 2], q_stack[qb % 2], q_hi[min(qb, 1)]
                pool.wait_ge(sm[f"q_in{qb % 2}"], 64 * (qb // 2 + 1))
                if qb == 0:
                    pool.wait_ge(sm["z_done"], len(ZT))
                need(pool, sm["qst_done"], 4 * qb)
                G.tensor_copy(hi, stage).then_inc(sm["qh_done"], 1)
                pool.wait_ge(sm["qh_done"], qb + 1)
                for r in range(4):
                    q = slice(32 * r, 32 * r + 32)
                    if r % 2 == 0:
                        op = G.tensor_copy(stack[q], stage[q])
                    else:
                        op = G.tensor_tensor(stack[q], stage[q], hi[q].bitcast(F32), ALU.subtract)
                    op.then_inc(sm["qst_done"], 1)
                if qb == 0:
                    pool.wait_ge(sm["qst_done"], 4)
                    for g in range(2 * H):
                        pool.wait_ge(sm[f"k_in{g}"], 64)
                        G.tensor_copy(k_stack[g][0:64, :], k_stage[g][0:64, :]).then_inc(sm["kup_done"], 1)
                    pool.wait_ge(sm["kup_done"], 2 * H)

            for t in range(NLAT):
                pool.wait_ge(sm["y_scaled"], t + 1)
                pool.wait_ge(x2_in[t % 2], 16 * (t // 2 + 1))
                G.tensor_tensor(y_buf[:, t % 2, :], y_buf[:, t % 2, :], x_buf[:, t % 2, :], ALU.add
                                ).then_inc(sm["y_added"], 1)


def constants():
    i = np.arange(P)
    r, c = i[:, None], i[None, :]
    m = {"ident": r == c, "triu": r <= c, "tril": r >= c, "ones": np.ones((P, P)),
         "swap": (r // 32 == c // 32) & ((r + 16) % 32 == c % 32),
         "neg_f": np.where(r <= c, 0.0, NEG), "neg_b": np.where(r >= c, 0.0, NEG)}
    for b in LEVELS:
        m[f"sib{b}"] = (r // (2 * b) == c // (2 * b)) & (r // b != c // b)
        even = (r // b) % 2 == 0
        m[f"alt{b}"] = (r // b == c // b) & np.where(even, r >= c, r <= c)
    const = np.ascontiguousarray(np.stack([np.asarray(m[n], np.float32) for n in CONSTS], axis=1))
    t = np.arange(LAT)
    half = MLA_ROPE // 2
    inv = 1.0 / (ROPE_BASE ** (np.arange(0, half, 2, dtype=np.float32) / half))
    ang = np.concatenate([(t // GRID_W)[:, None].astype(np.float32) * inv,
                          (t % GRID_W)[:, None].astype(np.float32) * inv], axis=1).astype(np.float32)
    cos, sin = np.cos(ang).T, np.sin(ang).T
    rope = np.stack([np.tile(np.concatenate([cos, cos]), (4, 1)), np.tile(np.concatenate([-sin, sin]), (4, 1))],
                    axis=1)
    return const, np.ascontiguousarray(rope, dtype=np.float32)


def column_order():
    gdn = 4 * QK_COLS + 16
    mla = Q_RANK + KV_RANK + MLA_ROPE + H * MLA_V
    a, b = gdn, gdn + mla
    misc = np.full(P, -1)
    misc[0:16] = np.arange(4 * QK_COLS, gdn)
    misc[KR0:KR0 + MLA_ROPE] = a + Q_RANK + KV_RANK + np.arange(MLA_ROPE)
    qkv = np.concatenate([QK_COLS + np.arange(QK_COLS), np.arange(QK_COLS), 2 * QK_COLS + np.arange(QK_COLS)])
    za = 3 * QK_COLS + np.arange(QK_COLS)
    zb = a + Q_RANK + KV_RANK + MLA_ROPE + np.arange(H * MLA_V)
    dqkv, dz = b + np.arange(3 * QK_COLS // 2), b + 3 * QK_COLS // 2 + np.arange(H * DIFF_V)
    return np.concatenate([misc, qkv, a + np.arange(Q_RANK + KV_RANK), dqkv, za, zb, dz])


def kernel(x, c, ctx, c_ctx, ada_w, ada_b, pre_gain, post_gain, w_in, gdn_conv, gdn_a_log, gdn_dt_bias,
           gdn_out_gain, mla_q_gain, mla_w_uq, mla_kv_gain, mla_w_ukv, diff_lambda, diff_sub_gain, w_out):
    import concourse.bacc as _bacc
    from concourse.bass_utils import run_bass_kernel_spmd as _run

    f = lambda a: np.asarray(a)
    tiles = lambda v: f(v).reshape(-1, P).T
    spread = lambda v: np.broadcast_to(f(v).reshape(1, -1), (P, f(v).size))
    const, rope = constants()
    conv = f(gdn_conv)[0].T.reshape(3, H, P, CONV_W)[[1, 0, 2]].transpose(2, 0, 1, 3).reshape(P, -1)
    cols = np.concatenate([
        np.stack([tiles(c), tiles(c_ctx)], axis=2).reshape(P, -1), tiles(ada_b[0]), tiles(pre_gain[0]),
        tiles(post_gain[0]), conv, tiles(gdn_out_gain[0]), tiles(mla_q_gain[0]), tiles(mla_kv_gain[0]),
        np.tile(f(diff_sub_gain)[0], 2).reshape(P, 1), spread(gdn_a_log[0]), spread(gdn_dt_bias[0]),
        spread(diff_lambda[0])], axis=1)
    order = column_order()
    wi = np.zeros((D, len(order)), f(w_in).dtype)
    wi[:, order >= 0] = f(w_in)[0][:, order[order >= 0]]
    arrays = {
        "x": f(x)[0], "ctx": f(ctx)[0], "cols": cols, "const": const, "rope": rope,
        "ada_w": f(ada_w)[0].reshape(KD, P, 3, D).transpose(2, 1, 0, 3),
        "w_in": wi.reshape(KD, P, len(TILES), P).transpose(2, 1, 0, 3),
        "w_uq": f(mla_w_uq)[0].reshape(2, P, -1).transpose(1, 0, 2), "w_ukv": f(mla_w_ukv)[0],
        "w_out": f(w_out)[0].reshape(KD, P, D),
    }
    nc = _bacc.Bacc("TRN2", target_bir_lowering=False, num_devices=1)
    args, feeds = [], {}
    for name, a in arrays.items():
        a = np.ascontiguousarray(a)
        feeds[f"in_{name}"] = a
        args.append(nc.dram_tensor(f"in_{name}", a.shape, mybir.dt.from_np(a.dtype), kind="ExternalInput").ap())
    out = nc.dram_tensor("out_0", (LAT, D), F32, kind="ExternalOutput").ap()
    hybrid_block(nc, *args, out)
    r = _run(nc, [feeds], core_ids=[0])
    return r.results[0]["out_0"].reshape(1, LAT, D)
```
